# Optimizing a Trainium2 kernel written in Bass

```python
import jax, jax.numpy as jnp
from jax import lax
import numpy as np

D_MODEL = 1024
BATCH = 1
SEQ = 512
DEPTH = 1

FOX_HEADS = 8
FOX_HEAD_DIM = D_MODEL // 16
GLA_HEADS = 4
GLA_HEAD_K = D_MODEL // 16
GLA_HEAD_V = D_MODEL // 8
GLA_GATE_RANK = 16
GLA_GATE_TAU = 16.0
GLA_CHUNK = 64
Q_BLOCK = 128
FOX_W = FOX_HEADS * FOX_HEAD_DIM
GLA_KW = GLA_HEADS * GLA_HEAD_K
GLA_VW = GLA_HEADS * GLA_HEAD_V
D_MIX = FOX_W + GLA_VW
IN_SPLITS = (FOX_W, FOX_W, FOX_W, FOX_HEADS, GLA_KW, GLA_KW, GLA_VW, GLA_VW, GLA_GATE_RANK)
D_IN = FOX_W * 3 + FOX_HEADS + GLA_KW * 2 + GLA_VW * 2 + GLA_GATE_RANK
N_MEM = 256
MEM_HEADS = 4
MEM_HEAD_DIM = D_MODEL // MEM_HEADS
D_FF = 2816
MACARON_W = 0.5
RMS_EPS = 1e-6

kernel_name = "fox_gla_hymba_macaron_sandwich_layer"

def rmsnorm(x, g):
    xf = x.astype(jnp.float32)
    y = xf * lax.rsqrt(jnp.mean(xf * xf, axis=-1, keepdims=True) + RMS_EPS)
    return (y * g.astype(jnp.float32)).astype(x.dtype)

def swiglu(x, w_gu, w_down):
    gate, up = jnp.split(x @ w_gu, 2, axis=-1)
    return (jax.nn.silu(gate) * up) @ w_down

def fox_attention(q, k, v, log_f):
    B, S, H, Dh = q.shape
    nb = S // Q_BLOCK
    c = jnp.cumsum(log_f, axis=1).transpose(0, 2, 1)
    kt = k.transpose(0, 2, 1, 3)
    vt = v.transpose(0, 2, 1, 3)
    qb = q.reshape(B, nb, Q_BLOCK, H, Dh).transpose(1, 0, 3, 2, 4)
    cb = c.reshape(B, H, nb, Q_BLOCK).transpose(2, 0, 1, 3)
    k_pos = jnp.arange(S)
    scale = Dh ** -0.5

    def block(args):
        qi, ci, i = args
        s = jnp.einsum('bhqd,bhkd->bhqk', qi, kt).astype(jnp.float32) * scale
        s = s + ci[..., None] - c[:, :, None, :]
        q_pos = i * Q_BLOCK + jnp.arange(Q_BLOCK)
        s = jnp.where(k_pos[None, :] <= q_pos[:, None], s, -jnp.inf)
        p = jax.nn.softmax(s, axis=-1).astype(vt.dtype)
        return jnp.einsum('bhqk,bhkd->bhqd', p, vt)

    o = lax.map(block, (qb, cb, jnp.arange(nb)))
    return o.transpose(1, 0, 3, 2, 4).reshape(B, S, H * Dh)

def gla_chunked(q, k, v, log_a):
    B, S, H, Dk = q.shape
    Dv = v.shape[-1]
    C = GLA_CHUNK
    nc = S // C
    f32 = jnp.float32
    qc = q.astype(f32).reshape(B, nc, C, H, Dk) * (Dk ** -0.5)
    kc = k.astype(f32).reshape(B, nc, C, H, Dk)
    vc = v.astype(f32).reshape(B, nc, C, H, Dv)
    b = jnp.cumsum(log_a.reshape(B, nc, C, H, Dk), axis=2)
    b_last = b[:, :, -1]
    q_dec = qc * jnp.exp(b)
    k_dec = kc * jnp.exp(-b)
    k_to_end = kc * jnp.exp(b_last[:, :, None] - b)
    causal = jnp.tril(jnp.ones((C, C), dtype=bool))
    a = jnp.einsum('bnihd,bnjhd->bnhij', q_dec, k_dec)
    a = jnp.where(causal, a, 0.0)
    o_intra = jnp.einsum('bnhij,bnjhv->bnihv', a, vc)
    s_chunk = jnp.einsum('bnchd,bnchv->nbhdv', k_to_end, vc)
    decay = jnp.exp(b_last).transpose(1, 0, 2, 3)

    def step(state, inp):
        d, sc = inp
        return d[..., None] * state + sc, state

    _, s_prev = lax.scan(step, jnp.zeros((B, H, Dk, Dv), f32), (decay, s_chunk))
    o_inter = jnp.einsum('bnihd,nbhdv->bnihv', q_dec, s_prev)
    return (o_intra + o_inter).reshape(B, S, H, Dv)

def hybrid_mixer(u, w_in, w_a2, b_a, b_f, g_gla, w_out):
    B, S, _ = u.shape
    offsets = [int(o) for o in np.cumsum(IN_SPLITS)[:-1]]
    fq, fk, fv, fz, gq, gk, gv, gr, ga = jnp.split(u @ w_in, offsets, axis=-1)
    log_f = jax.nn.log_sigmoid((fz + b_f).astype(jnp.float32))
    shp = (B, S, FOX_HEADS, FOX_HEAD_DIM)
    o_fox = fox_attention(fq.reshape(shp), fk.reshape(shp), fv.reshape(shp), log_f)
    log_a = jax.nn.log_sigmoid((ga @ w_a2 + b_a).astype(jnp.float32)) / GLA_GATE_TAU
    o_gla = gla_chunked(gq.reshape(B, S, GLA_HEADS, GLA_HEAD_K),
                        gk.reshape(B, S, GLA_HEADS, GLA_HEAD_K),
                        gv.reshape(B, S, GLA_HEADS, GLA_HEAD_V),
                        log_a.reshape(B, S, GLA_HEADS, GLA_HEAD_K)).astype(u.dtype)
    o_gla = rmsnorm(o_gla, g_gla.reshape(GLA_HEADS, GLA_HEAD_V)).reshape(B, S, GLA_VW)
    o_gla = o_gla * jax.nn.silu(gr)
    return jnp.concatenate([o_fox, o_gla], axis=-1) @ w_out

def memory_cross_attention(u, mem_n, w_mq, w_mkv, w_mo):
    B, S, _ = u.shape
    q = (u @ w_mq).reshape(B, S, MEM_HEADS, MEM_HEAD_DIM)
    k, v = jnp.split(mem_n @ w_mkv, 2, axis=-1)
    k = k.reshape(B, N_MEM, MEM_HEADS, MEM_HEAD_DIM)
    v = v.reshape(B, N_MEM, MEM_HEADS, MEM_HEAD_DIM)
    s = jnp.einsum('bshd,bnhd->bhsn', q, k).astype(jnp.float32) * (MEM_HEAD_DIM ** -0.5)
    p = jax.nn.softmax(s, axis=-1).astype(v.dtype)
    o = jnp.einsum('bhsn,bnhd->bshd', p, v).reshape(B, S, D_MODEL)
    return o @ w_mo

def _normal(k, shape, scale):
    return scale * jax.random.normal(k, shape, jnp.float32)

def _gain(k, shape):
    return 1.0 + 0.02 * jax.random.normal(k, shape, jnp.float32)

def setup_inputs(seed: int = 0) -> dict:
    key = jax.random.key(seed)
    ks = jax.random.split(key, 24)
    L = DEPTH
    return {
        "x": jax.random.normal(ks[0], (BATCH, SEQ, D_MODEL), jnp.float32),
        "mem": jax.random.normal(ks[1], (BATCH, N_MEM, D_MODEL), jnp.float32),
        "ffn1_g_pre": _gain(ks[2], (L, D_MODEL)),
        "ffn1_w_gu": _normal(ks[3], (L, D_MODEL, 2 * D_FF), D_MODEL ** -0.5),
        "ffn1_w_down": _normal(ks[4], (L, D_FF, D_MODEL), D_FF ** -0.5),
        "ffn1_g_post": _gain(ks[5], (L, D_MODEL)),
        "mix_g_pre": _gain(ks[6], (L, D_MODEL)),
        "mix_w_in": _normal(ks[7], (L, D_MODEL, D_IN), D_MODEL ** -0.5),
        "mix_w_a2": _normal(ks[8], (L, GLA_GATE_RANK, GLA_KW), GLA_GATE_RANK ** -0.5),
        "mix_b_a": _normal(ks[9], (L, GLA_KW), 0.1),
        "mix_b_f": _normal(ks[10], (L, FOX_HEADS), 0.1),
        "mix_g_gla": _gain(ks[11], (L, GLA_VW)),
        "mix_w_out": _normal(ks[12], (L, D_MIX, D_MODEL), D_MIX ** -0.5),
        "mix_g_post": _gain(ks[13], (L, D_MODEL)),
        "mem_g_pre": _gain(ks[14], (L, D_MODEL)),
        "mem_g_kv": _gain(ks[15], (L, D_MODEL)),
        "mem_w_q": _normal(ks[16], (L, D_MODEL, D_MODEL), D_MODEL ** -0.5),
        "mem_w_kv": _normal(ks[17], (L, D_MODEL, 2 * D_MODEL), D_MODEL ** -0.5),
        "mem_w_o": _normal(ks[18], (L, D_MODEL, D_MODEL), D_MODEL ** -0.5),
        "mem_g_post": _gain(ks[19], (L, D_MODEL)),
        "ffn2_g_pre": _gain(ks[20], (L, D_MODEL)),
        "ffn2_w_gu": _normal(ks[21], (L, D_MODEL, 2 * D_FF), D_MODEL ** -0.5),
        "ffn2_w_down": _normal(ks[22], (L, D_FF, D_MODEL), D_FF ** -0.5),
        "ffn2_g_post": _gain(ks[23], (L, D_MODEL)),
    }

def reference(x, mem, ffn1_g_pre, ffn1_w_gu, ffn1_w_down, ffn1_g_post,
              mix_g_pre, mix_w_in, mix_w_a2, mix_b_a, mix_b_f, mix_g_gla, mix_w_out, mix_g_post,
              mem_g_pre, mem_g_kv, mem_w_q, mem_w_kv, mem_w_o, mem_g_post,
              ffn2_g_pre, ffn2_w_gu, ffn2_w_down, ffn2_g_post):
    h = x
    for l in range(DEPTH):
        f = swiglu(rmsnorm(h, ffn1_g_pre[l]), ffn1_w_gu[l], ffn1_w_down[l])
        h = h + MACARON_W * rmsnorm(f, ffn1_g_post[l])
        m = hybrid_mixer(rmsnorm(h, mix_g_pre[l]), mix_w_in[l], mix_w_a2[l], mix_b_a[l],
                         mix_b_f[l], mix_g_gla[l], mix_w_out[l])
        h = h + rmsnorm(m, mix_g_post[l])
        c = memory_cross_attention(rmsnorm(h, mem_g_pre[l]), rmsnorm(mem, mem_g_kv[l]),
                                   mem_w_q[l], mem_w_kv[l], mem_w_o[l])
        h = h + rmsnorm(c, mem_g_post[l])
        f = swiglu(rmsnorm(h, ffn2_g_pre[l]), ffn2_w_gu[l], ffn2_w_down[l])
        h = h + MACARON_W * rmsnorm(f, ffn2_g_post[l])
    return h


_drawn_inputs = setup_inputs


def setup_inputs(seed=0):
    import zlib

    import numpy as np

    out = dict(_drawn_inputs(seed))
    spreads = {}
    factors = {'ffn1_g_pre': 3.118,
     'ffn1_g_post': 4.366,
     'mix_b_a': 2.702,
     'mix_b_f': 4.321,
     'mix_g_gla': 5.984,
     'mix_g_post': 3.968,
     'mem_g_pre': 5.087,
     'mem_g_kv': 3.385,
     'mem_g_post': 17.116,
     'ffn2_g_pre': 31.357,
     'ffn2_g_post': 45.922}
    for name, (base, spread) in spreads.items():
        noise = np.random.default_rng([zlib.crc32(name.encode()), seed]).standard_normal(out[name].shape)
        drawn = base * np.exp(spread * noise) if base else spread * noise
        out[name] = __import__('jax').numpy.asarray(drawn.astype(out[name].dtype))
    for name, factor in factors.items():
        out[name] = (out[name] * factor).astype(out[name].dtype)
    return out
```

```python
from contextlib import ExitStack

import concourse.bass as bass
from concourse import mybir

F32 = mybir.dt.float32
F32R = mybir.dt.float32r
ALU = mybir.AluOpType
ACT = mybir.ActivationFunctionType
AX_X = mybir.AxisListType.X

P = 128
SEQ = 512
D = 1024
DC = D // P
TC = SEQ // P
FF = 2816
FC = FF // P
FG = FC // 2
NMEM = 256
MC = NMEM // P
FOX_H, FOX_D = 8, 64
GLA_H, GLA_K, GLA_V, CHUNK, RANK = 4, 64, 128, 64, 16
NCH = SEQ // CHUNK
MEM_H, MEM_D = 4, 256
FOX_W, GLA_KW, GLA_VW = FOX_H * FOX_D, GLA_H * GLA_K, GLA_H * GLA_V
COL_FQ, COL_FK, COL_FV = 0, FOX_W, 2 * FOX_W
COL_FZ = 3 * FOX_W
COL_GQ = COL_FZ + FOX_H
COL_GV = COL_GQ + 2 * GLA_KW
COL_GR = COL_GV + GLA_VW
COL_GA = COL_GR + GLA_VW
EPS = 1e-6
TAU = 16.0
NEG = -1e30
SUBLAYERS = 4
BW = 1024
HW = BW // 2
RAW, SPLIT = 4, 2
LAND = 32

KB = DC // 2
B_UP1 = 0
B_DOWN1 = B_UP1 + FG * KB
B_IN = B_DOWN1 + FC
IN_COLS = (COL_FQ, COL_FK, COL_FV, COL_GQ, COL_GV, COL_GR)
B_OUT = B_IN + len(IN_COLS) * KB
B_KV = B_OUT + DC
B_MQ = B_KV + 4 * KB
B_MO = B_MQ + 2 * KB
B_UP2 = B_MO + DC
B_DOWN2 = B_UP2 + FG * KB
B_END = B_DOWN2 + FC
OUT_FIRST = (B_DOWN1, B_OUT, B_MO, B_DOWN2)
OUT_END = (B_IN, B_KV, B_UP2, B_END)

GAINS = ("ffn1_g_pre", "ffn1_g_post", "mix_g_pre", "mix_g_post", "mem_g_pre", "mem_g_kv",
         "mem_g_post", "ffn2_g_pre", "ffn2_g_post")
G_PRE = (0, 16, 32, 56)
G_POST = (8, 24, 48, 64)
G_KV = 40
G_BA = 72
G_GLA = 74
G_ROWS = 78
POST_SCALE = (0.5, 1.0, 1.0, 0.5)
SMALL_LOADS = len(GAINS) + 6

OUT_OFF = (4, 4, 0, 4)
STAT_BANK = (6, 2, 3, 6)
TOK_BANK, SMALL_BANK = 1, 3
IN_BANK = tuple(4 * ((g + 1) % 2) for g in range(6))
KV_BANK = (4, 0, 4, 0)
MQ_BANK = (4, 0)

FOX_UNITS = [(hd, i) for hd in range(FOX_H) for i in range(TC)]
MEM_UNITS = [(hd, i) for hd in range(MEM_H) for i in range(TC)]
N_FOX = len(FOX_UNITS)
N_UNITS = N_FOX + len(MEM_UNITS)
Y_FOX = FOX_H
Y_GLA = Y_FOX + GLA_H
N_CONSTS = 17


def build(nc, a, out):
    ctx = ExitStack()
    with ctx:
        sems = {}

        def sem(name):
            sems[name] = ctx.enter_context(nc.semaphore(name))
            return sems[name]

        top = [(nc.sbuf_base + 31) // 32 * 32]
        ends = []

        def sb(name, shape, dt=F32, at=None):
            size = 4
            for n in shape[1:]:
                size *= n
            where = top[0] if at is None else at
            if at is None:
                top[0] += (size + 31) // 32 * 32
            ends.append(where + size)
            return nc.alloc_sbuf_tensor_at(name, shape, dt, offset=where)

        h = sb("h", [P, DC, SEQ])
        xh = sb("xh", [P, DC, SEQ], F32R)
        xl = sb("xl", [P, DC, SEQ], F32R)
        raw = sb("raw", [P, RAW, BW])
        w_hi = sb("w_hi", [P, SPLIT, BW], F32R)
        w_lo = sb("w_lo", [P, SPLIT, BW], F32R)
        tmp = sb("tmp", [P, 4, SEQ])
        sq = sb("sq", [P, 2, SEQ])
        cum_hl = sb("cum_hl", [P, SEQ], F32R, at=top[0])
        acc = sb("acc", [P, SEQ])
        root = sb("root", [P, SEQ])
        rinv = sb("rinv", [P, SEQ])
        ident = sb("ident", [P, P])
        ones = sb("ones", [P, P])
        causal = sb("causal", [P, P])
        gla_mask = sb("gla_mask", [P, P])
        gains = sb("gains", [P, G_ROWS])
        post = sb("post", [P, SUBLAYERS, DC])
        root_tok = sb("root_tok", [P, TC])
        rinv_tok = sb("rinv_tok", [P, TC])
        eps_t = sb("eps_t", [P, 1])
        b_f = sb("b_f", [FOX_H, 1])
        decay = sb("decay", [P, 2, NCH])
        mx = sb("mx", [P, 4])
        nmx = sb("nmx", [P, 4])
        rs = sb("rs", [P, 4])
        rr = sb("rr", [P, 4])
        mem_ms = sb("mem_ms", [P, MC])
        mem_root = sb("mem_root", [P, MC])
        mem_rinv = sb("mem_rinv", [P, MC])
        shared = top[0]
        kib = 1024

        mid_hi = sb("mid_hi", [P, FC, SEQ], F32R, at=shared)
        mid_lo = sb("mid_lo", [P, FC, SEQ], F32R, at=shared + 44 * kib)
        x_tok = sb("x_tok", [P, TC, D], at=shared)
        out_tok = sb("out_tok", [P, TC, D], at=shared)
        gain_rows = sb("gain_rows", [G_ROWS, P], at=shared + 16 * kib)

        q_hi = sb("q_hi", [P, 4, SEQ], F32R, at=shared)
        q_lo = sb("q_lo", [P, 4, SEQ], F32R, at=shared + 8 * kib)
        k_hi = sb("k_hi", [P, 4, SEQ], F32R, at=shared + 16 * kib)
        k_lo = sb("k_lo", [P, 4, SEQ], F32R, at=shared + 24 * kib)
        v_hi = sb("v_hi", [P, TC, FOX_W], F32R, at=shared + 32 * kib)
        v_lo = sb("v_lo", [P, TC, FOX_W], F32R, at=shared + 40 * kib)
        gq = sb("gq", [P, 2, SEQ], at=shared + 48 * kib)
        gk = sb("gk", [P, 2, SEQ], at=shared + 52 * kib)
        gke = sb("gke", [P, 2, SEQ], at=shared + 56 * kib)
        gb = sb("gb", [P, 2, SEQ], at=shared + 60 * kib)
        gv = sb("gv", [P, TC, GLA_VW], at=shared + 64 * kib)
        gr = sb("gr", [P, GLA_H, SEQ], at=shared + 72 * kib)
        prob = sb("prob", [P, 3, SEQ], at=shared + 80 * kib)
        pt_hi = sb("pt_hi", [P, TC, SEQ], F32R, at=shared + 86 * kib)
        pt_lo = sb("pt_lo", [P, TC, SEQ], F32R, at=shared + 94 * kib)
        sel = sb("sel", [P, FOX_H, P], F32R, at=shared + 102 * kib)
        ls_min = sb("ls_min", [P, 2, SEQ], at=shared + 72 * kib)
        cum = sb("cum", [FOX_H, SEQ], at=shared + 80 * kib)
        w_small = sb("w_small", [P, DC, 48], at=shared + 88 * kib)
        w_small_g = sb("w_small_g", [P, DC, 48], at=shared + 88 * kib + 1536)
        zg = sb("zg", [48, SEQ], at=shared + 91 * kib)
        w_a2 = sb("w_a2", [48, GLA_KW], at=shared + 93 * kib)
        ls_abs = sb("ls_abs", [P, 3, SEQ], at=shared + 94 * kib)
        sel32 = sb("sel32", [P, FOX_H, P], at=shared + 94 * kib)
        reset = sb("reset", [P, SEQ], at=shared + 100 * kib)
        ke_tok = sb("ke_tok", [P, TC, 2, P], at=shared)
        at_sb = sb("at_sb", [P, 2, SEQ], at=shared + 4 * kib)
        state = sb("state", [P, NCH - 1, SEQ], at=shared + 8 * kib)
        qm_hi = sb("qm_hi", [P, DC, SEQ], F32R, at=shared)
        qm_lo = sb("qm_lo", [P, DC, SEQ], F32R, at=shared + 16 * kib)
        mem_hi = sb("mem_hi", [P, DC, NMEM], F32R, at=shared + 32 * kib)
        mem_lo = sb("mem_lo", [P, DC, NMEM], F32R, at=shared + 40 * kib)
        km_hi = sb("km_hi", [P, DC, NMEM], F32R, at=shared + 48 * kib)
        km_lo = sb("km_lo", [P, DC, NMEM], F32R, at=shared + 56 * kib)
        vm_hi = sb("vm_hi", [P, MC, D], F32R, at=shared + 64 * kib)
        vm_lo = sb("vm_lo", [P, MC, D], F32R, at=shared + 72 * kib)
        mem_tok = sb("mem_tok", [P, MC, D], at=shared + 86 * kib)
        mem_n = sb("mem_n", [P, MC, D], at=shared + 94 * kib)
        assert max(ends) <= nc.sbuf_usable_end, (max(ends), nc.sbuf_usable_end)
        f0 = tmp[:, 3, :]

        bank = [ctx.enter_context(nc.psum_tensor(f"bank{i}", [P, SEQ], F32)) for i in range(8)]

        def out_bank(s, c):
            return bank[(c + OUT_OFF[s]) % 8]

        landed = [sem(f"landed{i}") for i in range(RAW)]
        hi_ready = sem("hi_ready")
        lo_ready = sem("lo_ready")
        w_used = sem("w_used")
        x_landed = sem("x_landed")
        small_landed = sem("small_landed")
        mem_landed = sem("mem_landed")
        stored = sem("stored")
        consts = sem("consts")
        gains_turned = sem("gains_turned")
        gains_ready = sem("gains_ready")
        turned = sem("turned")
        h_ready = sem("h_ready")
        xh_ready = sem("xh_ready")
        xl_ready = sem("xl_ready")
        hsq_ready = sem("hsq_ready")
        hacc_ready = sem("hacc_ready")
        hstat = sem("hstat")
        hroot = sem("hroot")
        hinv = sem("hinv")
        out_done = sem("out_done")
        fsq_ready = sem("fsq_ready")
        facc_ready = sem("facc_ready")
        f0_saved = sem("f0_saved")
        fstat = sem("fstat")
        froot = sem("froot")
        finv = sem("finv")
        f_scaled = sem("f_scaled")
        gate_scaled = sem("gate_scaled")
        up_scaled = sem("up_scaled")
        silu_done = sem("silu_done")
        mid_done = sem("mid_done")
        midh_done = sem("midh_done")
        midl_done = sem("midl_done")
        small_scaled = sem("small_scaled")
        small_done = sem("small_done")
        tokstat = sem("tokstat")
        tokroot = sem("tokroot")
        tokinv = sem("tokinv")
        z_ready = sem("z_ready")
        ga_done = sem("ga_done")
        z_min = sem("z_min")
        ls_act = sem("ls_act")
        cum_step = sem("cum_step")
        gcum_step = sem("gcum_step")
        cum_hi = sem("cum_hi")
        cum_lo = sem("cum_lo")
        sel_ready = sem("sel_ready")
        in_tmp = sem("in_tmp")
        in_hi = sem("in_hi")
        in_lo = sem("in_lo")
        exps = sem("exps")
        gdec = sem("gdec")
        scored = sem("scored")
        masked = sem("masked")
        rowmax = sem("rowmax")
        maxed = sem("maxed")
        expd = sem("expd")
        rsum = sem("rsum")
        normed = sem("normed")
        pturned = sem("pturned")
        pt_h = sem("pt_h")
        pt_l = sem("pt_l")
        pv_done = sem("pv_done")
        y_h = sem("y_h")
        y_l = sem("y_l")
        ke_turned = sem("ke_turned")
        ke_saved = sem("ke_saved")
        at_done = sem("at_done")
        at_masked = sem("at_masked")
        sc_done = sem("sc_done")
        st_ready = sem("st_ready")
        o_done = sem("o_done")
        gsq = sem("gsq")
        gstat = sem("gstat")
        groot = sem("groot")
        ginv = sem("ginv")
        gnorm = sem("gnorm")
        gout = sem("gout")
        mem_sq = sem("mem_sq")
        mem_root_s = sem("mem_root_s")
        mem_inv = sem("mem_inv")
        mem_normed = sem("mem_normed")
        mem_turned = sem("mem_turned")
        mem_h = sem("mem_h")
        mem_l = sem("mem_l")
        kv_h = sem("kv_h")
        kv_l = sem("kv_l")
        mq_t = sem("mq_t")
        mq_h = sem("mq_h")
        mq_l = sem("mq_l")
        oturned = sem("oturned")
        ocopied_a = sem("ocopied_a")
        ocopied_v = sem("ocopied_v")

        def at_turn(i, step, n):
            return n if i is None else i * step + n

        def wait_out(eng, s, c):
            if c < DC - 1:
                eng.wait_ge(out_done, (DC - 1) * s + c + 1)
            else:
                eng.wait_ge(w_used, OUT_END[s])

        def pv_count(mem, hd, e=0):
            return FOX_H + 2 * hd + e if mem else hd

        def o_bank(mem, hd, e=0):
            return bank[5 + (2 * hd + e if mem else hd) % 3]

        def key_width(mem, i):
            return NMEM if mem else P * (i + 1)

        block = ctx.enter_context(nc.Block())

        @block.sync
        def _(sp):
            def fetch(n, srcs, i=None, step=0):
                if n >= RAW:
                    sp.wait_ge(lo_ready, at_turn(i, step, n - RAW + 1))
                for piece, src in enumerate(srcs):
                    dst = raw[:, n % RAW, :]
                    if len(src.shape) == 3:
                        dst = dst.rearrange("p (k u n) -> p k u n", k=2, u=2)[:, :, piece, :]
                    else:
                        dst = dst[:, piece * HW:(piece + 1) * HW]
                    sp.dma_start(dst, src).then_inc(landed[n % RAW], 16)

            def up_cols(w, k, col):
                return [w[2 * k * P:(2 * k + 2) * P, bass.ds(col + u * FF, 2 * P)].rearrange(
                    "(k p) n -> p k n", p=P) for u in range(2)]

            def row_pair(w, k, col):
                return [w[(2 * k + j) * P:(2 * k + j + 1) * P, col:col + HW] for j in range(2)]

            def row(w, start):
                return [w[bass.ds(start, P), j * HW:(j + 1) * HW] for j in range(2)]

            def swiglu_loads(w_gu, w_down, up, down):
                for k in range(KB):
                    fetch(up + k, up_cols(w_gu, k, 0))
                with sp.Fori(0, FG // 2) as i:
                    for k in range(2 * KB):
                        fetch(up + KB + k, up_cols(w_gu, k % KB, i * (4 * P) + (1 + k // KB) * 2 * P),
                              i, 2 * KB)
                for k in range(2):
                    fetch(down + k, row(w_down, k * P))
                with sp.Fori(0, (FC - 2) // 4) as i:
                    for k in range(4):
                        fetch(down + 2 + k, row(w_down, i * (4 * P) + (2 + k) * P), i, 4)

            for t in range(TC):
                sp.dma_start(x_tok[:, t, :], a["x"][0, t * P:(t + 1) * P, :]).then_inc(x_landed, 16)
            swiglu_loads(a["ffn1_w_gu"][0], a["ffn1_w_down"][0], B_UP1, B_DOWN1)
            for n in range(B_IN, B_OUT):
                fetch(n, row_pair(a["mix_w_in"][0], (n - B_IN) % KB, IN_COLS[(n - B_IN) // KB]))
            for n in range(B_OUT, B_KV):
                fetch(n, row(a["mix_w_out"][0], (n - B_OUT) * P))
                if n == B_OUT + RAW - 1:
                    sp.wait_ge(pv_done, FOX_H)
                    for t in range(MC):
                        sp.dma_start(mem_tok[:, t, :], a["mem"][0, t * P:(t + 1) * P, :]).then_inc(mem_landed, 16)
            for n in range(B_KV, B_MQ):
                fetch(n, row_pair(a["mem_w_kv"][0], (n - B_KV) % KB, (n - B_KV) // KB * HW))
            for n in range(B_MQ, B_MO):
                fetch(n, row_pair(a["mem_w_q"][0], (n - B_MQ) % KB, (n - B_MQ) // KB * HW))
            for n in range(B_MO, B_UP2):
                fetch(n, row(a["mem_w_o"][0], (n - B_MO) * P))
            swiglu_loads(a["ffn2_w_gu"][0], a["ffn2_w_down"][0], B_UP2, B_DOWN2)
            for half, copied in enumerate((ocopied_a, ocopied_v)):
                for t in range(TC):
                    sp.wait_ge(copied, t + 1)
                    cols = slice(half * HW, (half + 1) * HW)
                    sp.dma_start(out[0, t * P:(t + 1) * P, cols], out_tok[:, t, cols]).then_inc(stored, 16)
            sp.wait_ge(stored, 16 * 2 * TC)

        @block.gpsimd
        def _(gp):
            count = [0]

            def const(ins):
                count[0] += 1
                ins.then_inc(consts, 1)
                gp.wait_ge(consts, count[0])

            def split(n, i=None):
                gp.wait_ge(hi_ready, at_turn(i, RAW, n + 1))
                gp.tensor_tensor(w_lo[:, n % SPLIT, :], raw[:, n % RAW, :],
                                 w_hi[:, n % SPLIT, :].bitcast(F32), ALU.subtract).then_inc(lo_ready, 1)

            const(gp.memset(ident[:, :], 0.0))
            const(gp.affine_select(out=ident[:, :], in_=ident[:, :], compare_op=ALU.not_equal, fill=1.0,
                                   base=0, pattern=[[-1, P]], channel_multiplier=1))
            const(gp.memset(ones[:, :], 1.0))
            const(gp.memset(eps_t[:, :], EPS))
            const(gp.memset(w_small[:, :, :], 0.0))
            split(0)
            split(1)
            const(gp.memset(causal[:, :], 0.0))
            const(gp.affine_select(out=causal[:, :], in_=causal[:, :], compare_op=ALU.is_ge, fill=NEG,
                                   base=0, pattern=[[-1, P]], channel_multiplier=1))
            const(gp.memset(gla_mask[:, :], 1.0))
            const(gp.affine_select(out=gla_mask[:, :], in_=gla_mask[:, :], compare_op=ALU.is_ge, fill=0.0,
                                   base=0, pattern=[[1, P]], channel_multiplier=-1))
            const(gp.memset(gla_mask[0:CHUNK, CHUNK:P], 0.0))
            const(gp.memset(reset[:, :], 1.0))
            const(gp.memset(reset[:, :].rearrange("p (n c) -> p n c", c=CHUNK)[:, :, 0:1], 0.0))
            const(gp.memset(sel32[:, :, :], 0.0))
            for base in (0, -32, -64, -96):
                const(gp.affine_select(out=sel32[:, :, :], in_=sel32[:, :, :], compare_op=ALU.not_equal,
                                       fill=-1.0, base=base, pattern=[[-1, FOX_H], [0, P]],
                                       channel_multiplier=1))
            assert count[0] == N_CONSTS, count[0]
            split(2)
            split(3)
            with gp.Fori(1, B_END // RAW) as i:
                for q in range(RAW):
                    split(q, i)
            for n in range(B_END // RAW * RAW, B_END):
                split(n)

        @block.scalar
        def _(act):
            rounded = [0]

            def round_block(n, i=None, step=0):
                act.wait_ge(landed[n % RAW], at_turn(i, LAND * step // RAW, LAND * (n // RAW + 1)))
                if n >= SPLIT:
                    act.wait_ge(w_used, at_turn(i, step, n - SPLIT + 1))
                act.activation(w_hi[:, n % SPLIT, :], raw[:, n % RAW, :], ACT.Copy).then_inc(hi_ready, 1)

            def round_to(end):
                while rounded[0] < min(end, B_END):
                    round_block(rounded[0])
                    rounded[0] += 1

            def pre(s, c):
                act.wait_ge(h_ready, DC * s + c + 1)
                g = G_PRE[s] + c
                act.activation(xh[:, c, :], h[:, c, :], ACT.Copy, scale=gains[:, g:g + 1]).then_inc(xh_ready, 1)
                if c >= 2:
                    act.wait_ge(hacc_ready, DC * s + c - 1)
                elif s:
                    act.wait_ge(facc_ready, DC * s)
                act.activation(sq[:, c % 2, :], h[:, c, :], ACT.Square).then_inc(hsq_ready, 1)

            def rms_root(src, n, dst=None):
                return act.activation(root[:, :] if dst is None else dst, src, ACT.Sqrt,
                                      bias=eps_t[:, 0:1], scale=1.0 / n)

            def pre_root(s):
                act.wait_ge(hstat, s + 1)
                rms_root(bank[STAT_BANK[s]][:, :], D).then_inc(hroot, 1)

            def post_norm(s):
                round_to(OUT_END[s] + 1)
                for m in range(DC):
                    wait_out(act, s, m)
                    act.wait_ge(facc_ready if m >= 2 else hacc_ready, DC * s + m - 1 if m >= 2 else DC * (s + 1))
                    act.activation(sq[:, m % 2, :], out_bank(s, m)[:, :], ACT.Square).then_inc(fsq_ready, 1)
                round_to(OUT_END[s] + 2)
                act.wait_ge(fstat, s + 1)
                rms_root(out_bank(s, 0)[:, :], D).then_inc(froot, 1)

            def swiglu(s, up, down):
                first = 2 * FG * (s // 3)

                def group(g, i=None):
                    for pair in range(2):
                        act.wait_ge(gate_scaled, at_turn(i, 4, first + 2 * g + pair + 1))
                        act.activation(tmp[:, pair, :], tmp[:, pair, :], ACT.Silu).then_inc(silu_done, 1)
                    for pair in range(2):
                        act.wait_ge(mid_done, at_turn(i, 4, first + 2 * g + pair + 1))
                        act.activation(mid_hi[:, bass.ds(at_turn(i, 4, 2 * g + pair), 1), :],
                                       tmp[:, 2 + pair:3 + pair, :], ACT.Copy).then_inc(midh_done, 1)

                for c in range(DC):
                    pre(s, c)
                    if c in (3, 5):
                        round_to(up + 2 + (c - 1) // 2)
                pre_root(s)
                round_to(up + 6)
                group(0)
                with act.Fori(0, FG // 2) as i:
                    for g in range(2):
                        for k in range(KB):
                            round_block(up + 6 + KB * g + k, i, 2 * KB)
                        group(1 + g, i)
                with act.Fori(0, (FC - 2) // 4) as i:
                    for k in range(4):
                        round_block(down + 2 + k, i, 4)
                rounded[0] = down + FC

            def log_sigmoid(j):
                t = ls_abs[0:FOX_H, j, :] if j == 0 else ls_abs[:, j, :]
                act.wait_ge(z_ready, 1 + j)
                if j == 0:
                    act.activation(t, zg[0:FOX_H, :], ACT.Abs, bias=b_f[:, 0:1]).then_inc(ls_act, 1)
                else:
                    act.activation(t, gb[:, j - 1, :], ACT.Abs).then_inc(ls_act, 1)
                act.wait_ge(ls_act, 3 * j + 1)
                act.activation(t, t, ACT.Exp, scale=-1.0).then_inc(ls_act, 1)
                act.wait_ge(ls_act, 3 * j + 2)
                act.activation(t, t, ACT.Ln, bias=1.0).then_inc(ls_act, 1)

            def in_evacuate(g):
                b = bank[IN_BANK[g]:IN_BANK[g] + 4]
                for m in range(4):
                    if g < 2:
                        act.wait_ge(in_tmp, 4 * g + m + 1)
                        act.activation((q_hi, k_hi)[g][:, m, :], tmp[:, m, :], ACT.Copy).then_inc(in_hi, 1)
                    elif g in (2, 4):
                        act.wait_ge(w_used, B_IN + KB * (g + 1))
                        act.wait_ge(tokinv, 1)
                        act.activation((v_hi if g == 2 else gv)[:, m, :], b[m][:, :], ACT.Copy,
                                       scale=rinv_tok[:, m:m + 1]).then_inc(in_hi, 1)
                    elif g == 5:
                        act.wait_ge(in_tmp, 8 + m + 1)
                        act.activation(gr[:, m, :], tmp[:, m, :], ACT.Silu).then_inc(in_hi, 1)

            def decays():
                act.wait_ge(gcum_step, 5)
                act.activation(decay[:, :, :], gb[:, :, :].rearrange("p k (n c) -> p k n c", c=CHUNK)[:, :, :, CHUNK - 1],
                               ACT.Exp, scale=1.0 / TAU).then_inc(exps, 1)
                act.activation(ls_abs[:, 0:2, :], gb[:, :, :], ACT.Exp, scale=1.0 / TAU).then_inc(exps, 1)
                act.activation(gke[:, :, :], gke[:, :, :], ACT.Exp, scale=1.0 / TAU).then_inc(exps, 1)
                act.wait_ge(gdec, 2)
                act.activation(ls_abs[:, 0:2, :], gb[:, :, :], ACT.Exp, scale=-1.0 / TAU).then_inc(exps, 1)

            def attention(units, u0, mem):
                for k in range(len(units) + 4):
                    if k < len(units):
                        u, w = u0 + k, key_width(mem, units[k][1])
                        act.wait_ge(maxed, u + 1)
                        if u >= 3:
                            act.wait_ge(pturned, u - 2)
                        act.activation(prob[:, u % 3, 0:w], bank[k % 3][:, 0:w], ACT.Exp,
                                       bias=nmx[:, u % 4:u % 4 + 1],
                                       accum_out=rs[:, u % 4:u % 4 + 1]).then_inc(expd, 1)
                    if 0 <= k - 2 < len(units):
                        hd, i = units[k - 2]
                        nk = key_width(mem, i) // P
                        act.wait_ge(pturned, u0 + k - 1)
                        if hd:
                            act.wait_ge(pv_done, pv_count(mem, hd))
                        act.activation(pt_hi[:, 0:nk, i * P:(i + 1) * P],
                                       bank[3 + k % 2][:, 0:nk * P].rearrange("p (j n) -> p j n", n=P),
                                       ACT.Copy).then_inc(pt_h, 1)
                    if k >= 4 and units[k - 4][1] == TC - 1:
                        hd = units[k - 4][0]
                        for e in range(2 if mem else 1):
                            act.wait_ge(pv_done, pv_count(mem, hd, e) + 1)
                            o = o_bank(mem, hd, e)
                            if mem:
                                act.activation(y_h_of(2 * hd + e), o[:, :], ACT.Copy).then_inc(y_h, 1)
                            else:
                                r = slice(FOX_D * (hd % 2), FOX_D * (hd % 2 + 1))
                                act.activation(xh[r, hd // 2, :], o[r, :], ACT.Copy).then_inc(y_h, 1)

            def y_h_of(c):
                return xh[:, c, :]

            def gla():
                for t in range(2):
                    act.wait_ge(ke_turned, t + 1)
                    act.activation(ke_tok[:, 2 * t:2 * t + 2, :, :], bank[4 + t][:, :].rearrange(
                        "p (t c d) -> p t c d", t=2, c=2), ACT.Copy).then_inc(ke_saved, 1)
                act.wait_ge(mem_landed, 16 * MC)
                for t in range(MC):
                    act.activation(mem_n[:, t, :], mem_tok[:, t, :], ACT.Square,
                                   accum_out=mem_ms[:, t:t + 1]).then_inc(mem_sq, 1)
                act.wait_ge(mem_sq, MC)
                rms_root(mem_ms[:, :], D, mem_root[:, :]).then_inc(mem_root_s, 1)
                act.wait_ge(mem_inv, 1)
                for t in range(MC):
                    act.activation(mem_n[:, t, :], mem_tok[:, t, :], ACT.Copy,
                                   scale=mem_rinv[:, t:t + 1]).then_inc(mem_normed, 1)

                def head_square(hd):
                    if hd >= 2:
                        act.wait_ge(gstat, hd - 1)
                    act.activation(sq[:, hd % 2, :], bank[hd][:, :], ACT.Square).then_inc(gsq, 1)

                act.wait_ge(o_done, TC)
                head_square(0)
                for hd in range(GLA_H):
                    if hd + 1 < GLA_H:
                        head_square(hd + 1)
                    act.wait_ge(gstat, hd + 1)
                    if hd:
                        act.wait_ge(ginv, hd)
                    rms_root(bank[4 + hd % 2][:, :], GLA_V).then_inc(groot, 1)
                    if hd:
                        head_out(hd - 1)
                head_out(GLA_H - 1)
                for c in range(DC):
                    act.wait_ge(mem_turned, c // 2 + 1)
                    act.activation(mem_hi[:, c, :], bank[6 + c // 2 % 2][:, c % 2 * NMEM:(c % 2 + 1) * NMEM],
                                   ACT.Copy, scale=gains[:, G_KV + c:G_KV + c + 1]).then_inc(mem_h, 1)

            def head_out(hd):
                act.wait_ge(gout, hd + 1)
                act.activation(xh[:, 4 + hd, :], tmp[:, hd, :], ACT.Copy).then_inc(y_h, 1)

            def mixer():
                for c in range(DC):
                    pre(1, c)
                    if c in (3, 5):
                        round_to(B_IN + 2 + (c - 1) // 2)
                pre_root(1)
                act.wait_ge(tokstat, 1)
                rms_root(bank[TOK_BANK][:, 0:TC], D, root_tok[:, :]).then_inc(tokroot, 1)
                round_to(B_IN + 5)
                log_sigmoid(0)
                round_to(B_IN + 6)
                in_evacuate(0)
                round_to(B_IN + 8)
                log_sigmoid(1)
                log_sigmoid(2)
                act.wait_ge(cum_step, 3)
                for r in (0, 64):
                    act.activation(cum_hl[r:r + FOX_H, :], cum[:, :], ACT.Copy).then_inc(cum_hi, 1)
                for g in range(1, 6):
                    round_to(B_IN + KB * (g + 1) + 2)
                    if g == 3:
                        decays()
                    in_evacuate(g)
                attention(FOX_UNITS, 0, False)
                gla()
                round_to(B_KV)

            def memory():
                for g in range(4):
                    round_to(B_KV + KB * (g + 1) + 2)
                    for m in range(4 if g < 2 else MC):
                        b = bank[KV_BANK[g] + m]
                        act.wait_ge(w_used, B_KV + KB * (g + 1))
                        if g < 2:
                            act.activation(km_hi[:, 4 * g + m, :], b[:, 0:NMEM], ACT.Copy).then_inc(kv_h, 1)
                        else:
                            act.activation(vm_hi[:, m, (g - 2) * HW:(g - 1) * HW], b[:, :], ACT.Copy).then_inc(kv_h, 1)
                    pre(2, 2 * g)
                    pre(2, 2 * g + 1)
                pre_root(2)
                for g in range(2):
                    round_to(B_MQ + KB * (g + 1) + 2)
                    for m in range(4):
                        act.wait_ge(mq_t, 4 * g + m + 1)
                        act.activation(qm_hi[:, 4 * g + m, :], tmp[:, m, :], ACT.Copy).then_inc(mq_h, 1)
                attention(MEM_UNITS, N_FOX, True)
                round_to(B_UP2)

            for r, name in enumerate(GAINS):
                act.dma_start(gain_rows[r * 8:r * 8 + 8, :],
                              a[name].rearrange("l (c p) -> (l c) p", p=P)).then_inc(small_landed, 16)
            act.dma_start(gain_rows[G_BA:G_BA + 2, :],
                          a["mix_b_a"].rearrange("l (c p) -> (l c) p", p=P)).then_inc(small_landed, 16)
            act.dma_start(gain_rows[G_GLA:G_GLA + 4, :],
                          a["mix_g_gla"].rearrange("l (c p) -> (l c) p", p=P)).then_inc(small_landed, 16)
            act.dma_start(b_f[:, :], a["mix_b_f"].rearrange("l (h o) -> (l h) o", o=1)).then_inc(small_landed, 16)
            act.dma_start(w_a2[32:48, :], a["mix_w_a2"][0]).then_inc(small_landed, 16)
            round_to(2)
            act.wait_ge(consts, 5)
            for c0, width, where in ((COL_FZ, FOX_H, 0), (COL_GA, RANK, 32)):
                act.dma_start(w_small[:, :, where:where + width],
                              a["mix_w_in"][0][:, c0:c0 + width].rearrange("(c p) n -> p c n", p=P))\
                   .then_inc(small_landed, 16)
            act.wait_ge(consts, N_CONSTS)
            act.activation(sel[:, :, :], sel32[:, :, :], ACT.Copy).then_inc(sel_ready, 1)
            act.wait_ge(gains_ready, 1)
            swiglu(0, B_UP1, B_DOWN1)
            post_norm(0)
            mixer()
            post_norm(1)
            memory()
            post_norm(2)
            swiglu(3, B_UP2, B_DOWN2)
            post_norm(3)
            for t in range(TC):
                act.wait_ge(oturned, t + 1)
                act.activation(out_tok[:, t, 0:HW], bank[4 + t][:, :], ACT.Copy).then_inc(ocopied_a, 1)

        @block.vector
        def _(dve):
            def pre(s, c):
                g = G_PRE[s] + c
                dve.wait_ge(xh_ready, DC * s + c + 1)
                dve.scalar_tensor_tensor(out=xl[:, c, :], in0=h[:, c, :], scalar=gains[:, g:g + 1],
                                         in1=xh[:, c, :].bitcast(F32), op0=ALU.mult,
                                         op1=ALU.subtract).then_inc(xl_ready, 1)
                dve.wait_ge(hsq_ready, DC * s + c + 1)
                if c == 0:
                    if s:
                        dve.wait_ge(fstat, s)
                    dve.tensor_copy(acc[:, :], sq[:, 0, :]).then_inc(hacc_ready, 1)
                else:
                    dve.wait_ge(hacc_ready, DC * s + c)
                    dve.tensor_tensor(acc[:, :], acc[:, :], sq[:, c % 2, :], ALU.add).then_inc(hacc_ready, 1)

            def pre_inv(s):
                dve.wait_ge(hroot, s + 1)
                dve.reciprocal(rinv[:, :], root[:, :]).then_inc(hinv, 1)
                dve.wait_ge(hinv, s + 1)

            def post_norm(s):
                for m in range(DC):
                    dve.wait_ge(fsq_ready, DC * s + m + 1)
                    if m == 0:
                        dve.tensor_copy(f0, out_bank(s, 0)[:, :]).then_inc(f0_saved, 1)
                        dve.wait_ge(hstat, s + 1)
                        if s == 1:
                            dve.wait_ge(tokstat, 1)
                        dve.tensor_copy(acc[:, :], sq[:, 0, :]).then_inc(facc_ready, 1)
                    else:
                        dve.wait_ge(facc_ready, DC * s + m)
                        dve.tensor_tensor(acc[:, :], acc[:, :], sq[:, m % 2, :], ALU.add).then_inc(facc_ready, 1)
                dve.wait_ge(froot, s + 1)
                dve.reciprocal(rinv[:, :], root[:, :]).then_inc(finv, 1)
                dve.wait_ge(finv, s + 1)

            def residual(s, m):
                src = f0 if m == 0 else out_bank(s, m)[:, :]
                dve.tensor_tensor(tmp[:, m % 2, :], src, rinv[:, :], ALU.mult).then_inc(f_scaled, 1)
                dve.wait_ge(f_scaled, DC * s + m + 1)
                dve.scalar_tensor_tensor(out=h[:, m, :], in0=tmp[:, m % 2, :], scalar=post[:, s, m:m + 1],
                                         in1=h[:, m, :], op0=ALU.mult, op1=ALU.add).then_inc(h_ready, 1)
                dve.wait_ge(h_ready, DC * (s + 1) + m + 1)

            def swiglu(s, up):
                first = 2 * FG * (s // 3)

                def group(g, i=None):
                    b = bank[4 * (g % 2):4 * (g % 2) + 4]
                    dve.wait_ge(w_used, at_turn(i, 2 * KB, up + KB * (g + 1)))
                    for pair in range(2):
                        n = first + 2 * g + pair
                        if n >= 2:
                            dve.wait_ge(midl_done, at_turn(i, 4, n - 1))
                        dve.tensor_tensor(tmp[:, pair, :], b[pair][:, :], rinv[:, :], ALU.mult).then_inc(gate_scaled, 1)
                        dve.tensor_tensor(tmp[:, 2 + pair, :], b[2 + pair][:, :], rinv[:, :],
                                          ALU.mult).then_inc(up_scaled, 1)
                    for pair in range(2):
                        n = first + 2 * g + pair
                        dve.wait_ge(silu_done, at_turn(i, 4, n + 1))
                        dve.wait_ge(up_scaled, at_turn(i, 4, n + 2))
                        dve.tensor_tensor(tmp[:, 2 + pair, :], tmp[:, pair, :], tmp[:, 2 + pair, :],
                                          ALU.mult).then_inc(mid_done, 1)
                    for pair in range(2):
                        n = first + 2 * g + pair
                        dve.wait_ge(midh_done, at_turn(i, 4, n + 1))
                        chunk = at_turn(i, 4, 2 * g + pair)
                        dve.tensor_tensor(mid_lo[:, bass.ds(chunk, 1), :], tmp[:, 2 + pair:3 + pair, :],
                                          mid_hi[:, bass.ds(chunk, 1), :].bitcast(F32),
                                          ALU.subtract).then_inc(midl_done, 1)

                pre_inv(s)
                group(0)
                with dve.Fori(0, FG // 2) as i:
                    for g in range(2):
                        group(1 + g, i)

            def attention(units, u0, mem):
                y0 = Y_GLA if mem else 0
                for k in range(len(units) + 4):
                    if k < len(units):
                        u, w = u0 + k, key_width(mem, units[k][1])
                        r = slice(u % 4, u % 4 + 1)
                        s = bank[k % 3]
                        dve.wait_ge(scored, u + 1)
                        if not mem:
                            dve.tensor_tensor(s[:, w - P:w], s[:, w - P:w], causal[:, :], ALU.add).then_inc(masked, 1)
                            dve.wait_ge(masked, u + 1)
                        dve.tensor_reduce(mx[:, r], s[:, 0:w], AX_X, ALU.max).then_inc(rowmax, 1)
                        dve.wait_ge(rowmax, u + 1)
                        dve.tensor_scalar(nmx[:, r], mx[:, r], -1.0, None, ALU.mult).then_inc(maxed, 1)
                    if 0 <= k - 1 < len(units):
                        u, w = u0 + k - 1, key_width(mem, units[k - 1][1])
                        r = slice(u % 4, u % 4 + 1)
                        dve.wait_ge(expd, u + 1)
                        dve.reciprocal(rr[:, r], rs[:, r]).then_inc(rsum, 1)
                        dve.wait_ge(rsum, u + 1)
                        dve.tensor_scalar(prob[:, u % 3, 0:w], prob[:, u % 3, 0:w], rr[:, r], None,
                                          ALU.mult).then_inc(normed, 1)
                    if 0 <= k - 2 < len(units):
                        i = units[k - 2][1]
                        nk = key_width(mem, i) // P
                        dve.wait_ge(pt_h, u0 + k - 1)
                        dve.tensor_tensor(pt_lo[:, 0:nk, i * P:(i + 1) * P],
                                          bank[3 + k % 2][:, 0:nk * P].rearrange("p (j n) -> p j n", n=P),
                                          pt_hi[:, 0:nk, i * P:(i + 1) * P].bitcast(F32),
                                          ALU.subtract).then_inc(pt_l, 1)
                    if k >= 4 and units[k - 4][1] == TC - 1:
                        hd = units[k - 4][0]
                        for e in range(2 if mem else 1):
                            c = 2 * hd + e if mem else hd // 2
                            r = slice(0, P) if mem else slice(FOX_D * (hd % 2), FOX_D * (hd % 2 + 1))
                            dve.wait_ge(y_h, y0 + (2 * hd + e if mem else hd) + 1)
                            dve.tensor_tensor(xl[r, c, :], o_bank(mem, hd, e)[r, :], xh[r, c, :].bitcast(F32),
                                              ALU.subtract).then_inc(y_l, 1)

            def gates():
                for j in range(2):
                    dve.wait_ge(ga_done, j + 1)
                    dve.tensor_scalar(gb[:, j, :], bank[6 + j][:, :], gains[:, G_BA + j:G_BA + j + 1], None,
                                      ALU.add).then_inc(z_ready, 1)
                    dve.wait_ge(z_ready, 2 + j)
                    dve.tensor_scalar(ls_min[:, j, :], gb[:, j, :], 0.0, None, ALU.min).then_inc(z_min, 1)
                for j in range(2):
                    dve.wait_ge(ls_act, 6 + 3 * j)
                    dve.wait_ge(z_min, 2 + j)
                    dve.tensor_tensor(ls_min[:, j, :], ls_min[:, j, :], ls_abs[:, 1 + j, :],
                                      ALU.subtract).then_inc(gcum_step, 1)
                    dve.wait_ge(gcum_step, 2 * j + 1)
                    dve.tensor_tensor_scan(gb[:, j, :], reset[:, :], ls_min[:, j, :], 0.0,
                                           ALU.mult, ALU.add).then_inc(gcum_step, 1)
                dve.wait_ge(gcum_step, 4)
                b = gb[:, :, :].rearrange("p k (n c) -> p (k n) c", c=CHUNK)
                dve.tensor_tensor(gke[:, :, :].rearrange("p k (n c) -> p (k n) c", c=CHUNK),
                                  b[:, :, CHUNK - 1:CHUNK].to_broadcast([P, 2 * NCH, CHUNK]), b,
                                  ALU.subtract).then_inc(gcum_step, 1)

            def forget():
                dve.wait_ge(ls_act, 3)
                dve.wait_ge(z_min, 1)
                dve.tensor_tensor(cum[:, :], cum[:, :], ls_abs[0:FOX_H, 0, :], ALU.subtract).then_inc(cum_step, 1)
                dve.wait_ge(cum_step, 2)
                dve.tensor_tensor_scan(cum[:, :], ones[0:FOX_H, 0:1].to_broadcast([FOX_H, SEQ]), cum[:, :], 0.0,
                                       ALU.mult, ALU.add).then_inc(cum_step, 1)

            def in_evacuate(g):
                b = bank[IN_BANK[g]:IN_BANK[g] + 4]
                dve.wait_ge(w_used, B_IN + KB * (g + 1))
                if g in (0, 1, 5):
                    for m in range(4):
                        if g == 1:
                            dve.wait_ge(in_lo, m + 1)
                        dve.scalar_tensor_tensor(out=tmp[:, m, :], in0=b[m][:, :],
                                                 scalar=FOX_D ** -0.5 if g == 0 else 1.0, in1=rinv[:, :],
                                                 op0=ALU.mult, op1=ALU.mult).then_inc(in_tmp, 1)
                for m in range(4):
                    if g < 2:
                        hi, lo = ((q_hi, q_lo), (k_hi, k_lo))[g]
                        dve.wait_ge(in_hi, 4 * g + m + 1)
                        dve.tensor_tensor(lo[:, m, :], tmp[:, m, :], hi[:, m, :].bitcast(F32),
                                          ALU.subtract).then_inc(in_lo, 1)
                    elif g == 2:
                        dve.wait_ge(in_hi, 8 + m + 1)
                        dve.scalar_tensor_tensor(out=v_lo[:, m, :], in0=b[m][:, :], scalar=rinv_tok[:, m:m + 1],
                                                 in1=v_hi[:, m, :].bitcast(F32), op0=ALU.mult,
                                                 op1=ALU.subtract).then_inc(in_lo, 1)
                    elif g == 3:
                        dve.scalar_tensor_tensor(out=(gq if m < 2 else gk)[:, m % 2, :], in0=b[m][:, :],
                                                 scalar=GLA_K ** -0.5 if m < 2 else 1.0, in1=rinv[:, :],
                                                 op0=ALU.mult, op1=ALU.mult).then_inc(in_lo, 1)

            def decays():
                dve.wait_ge(in_lo, 16)
                dve.wait_ge(exps, 2)
                for c in range(2):
                    dve.tensor_tensor(gq[:, c, :], gq[:, c, :], ls_abs[:, c, :], ALU.mult).then_inc(gdec, 1)
                dve.wait_ge(exps, 3)
                dve.tensor_tensor(gke[:, :, :], gk[:, :, :], gke[:, :, :], ALU.mult).then_inc(gdec, 1)
                dve.wait_ge(exps, 4)
                dve.wait_ge(gdec, 3)
                dve.tensor_tensor(gk[:, :, :], gk[:, :, :], ls_abs[:, 0:2, :], ALU.mult).then_inc(gdec, 1)

            def gla():
                def mask(m):
                    dve.wait_ge(at_done, m + 1)
                    if m >= 2:
                        dve.wait_ge(o_done, m - 1)
                    for e in range(2):
                        dve.tensor_tensor(at_sb[:, m % 2, :].rearrange("p (c e i) -> p c e i", e=2, i=P)[:, :, e, :],
                                          bank[4 + e][:, 0:2 * P].rearrange("p (c i) -> p c i", i=P),
                                          gla_mask[:, :].rearrange("p (o i) -> p o i", o=1).to_broadcast([P, 2, P]),
                                          ALU.mult).then_inc(at_masked, 1)

                def step(n):
                    dve.wait_ge(sc_done, n + 1)
                    b = bank[6 + n % 2]
                    if n == 0:
                        dve.tensor_copy(state[:, 0, :], b[:, :]).then_inc(st_ready, 1)
                        return
                    dve.wait_ge(st_ready, 2 * n - 1)
                    for c in range(2):
                        half = slice(256 * c, 256 * c + 256)
                        dve.scalar_tensor_tensor(out=state[:, n, half], in0=state[:, n - 1, half],
                                                 scalar=decay[:, c, n:n + 1], in1=b[:, half],
                                                 op0=ALU.mult, op1=ALU.add).then_inc(st_ready, 1)

                mask(0)
                step(0)
                for m in range(1, TC):
                    mask(m)
                    step(2 * m - 1)
                    step(2 * m)
                dve.wait_ge(mem_root_s, 1)
                dve.reciprocal(mem_rinv[:, :], mem_root[:, :]).then_inc(mem_inv, 1)
                for hd in range(GLA_H):
                    dve.wait_ge(groot, hd + 1)
                    if hd:
                        dve.wait_ge(gnorm, hd)
                    dve.reciprocal(rinv[:, :], root[:, :]).then_inc(ginv, 1)
                    dve.wait_ge(ginv, hd + 1)
                    dve.tensor_tensor(tmp[:, hd, :], bank[hd][:, :], rinv[:, :], ALU.mult).then_inc(gnorm, 1)
                    dve.wait_ge(gnorm, hd + 1)
                    dve.scalar_tensor_tensor(out=tmp[:, hd, :], in0=tmp[:, hd, :],
                                             scalar=gains[:, G_GLA + hd:G_GLA + hd + 1], in1=gr[:, hd, :],
                                             op0=ALU.mult, op1=ALU.mult).then_inc(gout, 1)
                    if hd:
                        head_lo(hd - 1)
                head_lo(GLA_H - 1)
                for c in range(DC):
                    dve.wait_ge(mem_h, c // 2 * 2 + 2)
                    dve.scalar_tensor_tensor(out=mem_lo[:, c, :],
                                             in0=bank[6 + c // 2 % 2][:, c % 2 * NMEM:(c % 2 + 1) * NMEM],
                                             scalar=gains[:, G_KV + c:G_KV + c + 1],
                                             in1=mem_hi[:, c, :].bitcast(F32), op0=ALU.mult,
                                             op1=ALU.subtract).then_inc(mem_l, 1)

            def head_lo(hd):
                dve.wait_ge(y_h, Y_FOX + hd + 1)
                dve.tensor_tensor(xl[:, 4 + hd, :], tmp[:, hd, :], xh[:, 4 + hd, :].bitcast(F32),
                                  ALU.subtract).then_inc(y_l, 1)

            def mixer():
                residual(0, 0)
                for c in range(1, DC):
                    residual(0, c)
                    pre(1, c - 1)
                pre(1, DC - 1)
                pre_inv(1)
                dve.wait_ge(small_done, 1)
                dve.tensor_tensor(zg[:, :], bank[SMALL_BANK][0:48, :], rinv[0:48, :], ALU.mult).then_inc(z_ready, 1)
                dve.wait_ge(tokroot, 1)
                dve.reciprocal(rinv_tok[:, :], root_tok[:, :]).then_inc(tokinv, 1)
                dve.memset(cum_hl[:, :].bitcast(F32), 0.0).then_inc(cum_step, 1)
                dve.wait_ge(z_ready, 1)
                dve.tensor_scalar(cum[:, :], zg[0:FOX_H, :], b_f[:, 0:1], 0.0, ALU.add, ALU.min).then_inc(z_min, 1)
                in_evacuate(0)
                forget()
                gates()
                dve.wait_ge(cum_hi, 2)
                for r in (32, 96):
                    dve.tensor_tensor(cum_hl[r:r + FOX_H, :], cum[:, :], cum_hl[0:FOX_H, :].bitcast(F32),
                                      ALU.subtract).then_inc(cum_lo, 1)
                for g in (1, 2, 3):
                    in_evacuate(g)
                decays()
                in_evacuate(5)
                attention(FOX_UNITS, 0, False)
                gla()

            def memory():
                for c in range(DC):
                    residual(1, c)
                for g in range(4):
                    for m in range(4 if g < 2 else MC):
                        b = bank[KV_BANK[g] + m]
                        if g < 2:
                            dve.wait_ge(kv_h, 4 * g + m + 1)
                            dve.tensor_tensor(km_lo[:, 4 * g + m, :], b[:, 0:NMEM],
                                              km_hi[:, 4 * g + m, :].bitcast(F32), ALU.subtract).then_inc(kv_l, 1)
                        else:
                            cols = slice((g - 2) * HW, (g - 1) * HW)
                            dve.wait_ge(kv_h, 8 + MC * (g - 2) + m + 1)
                            dve.tensor_tensor(vm_lo[:, m, cols], b[:, :], vm_hi[:, m, cols].bitcast(F32),
                                              ALU.subtract).then_inc(kv_l, 1)
                    pre(2, 2 * g)
                    pre(2, 2 * g + 1)
                pre_inv(2)
                for g in range(2):
                    dve.wait_ge(w_used, B_MQ + KB * (g + 1))
                    for m in range(4):
                        if g:
                            dve.wait_ge(mq_l, m + 1)
                        dve.scalar_tensor_tensor(out=tmp[:, m, :], in0=bank[MQ_BANK[g] + m][:, :],
                                                 scalar=MEM_D ** -0.5, in1=rinv[:, :],
                                                 op0=ALU.mult, op1=ALU.mult).then_inc(mq_t, 1)
                    for m in range(4):
                        j = 4 * g + m
                        dve.wait_ge(mq_h, j + 1)
                        dve.tensor_tensor(qm_lo[:, j, :], tmp[:, m, :], qm_hi[:, j, :].bitcast(F32),
                                          ALU.subtract).then_inc(mq_l, 1)
                attention(MEM_UNITS, N_FOX, True)

            dve.wait_ge(gains_turned, 1)
            dve.tensor_copy(gains[:, :], bank[7][:, 0:G_ROWS]).then_inc(gains_ready, 1)
            dve.wait_ge(gains_ready, 1)
            for s in range(SUBLAYERS):
                dve.tensor_scalar(post[:, s, :], gains[:, G_POST[s]:G_POST[s] + DC], POST_SCALE[s], None,
                                  ALU.mult).then_inc(gains_ready if s else up_scaled, 1)
            for c in range(DC):
                dve.wait_ge(turned, c + 1)
                dve.tensor_copy(h[:, c, :], bank[c][:, :]).then_inc(h_ready, 1)
                dve.wait_ge(h_ready, c + 1)
                if c:
                    pre(0, c - 1)
            pre(0, DC - 1)
            dve.wait_ge(small_landed, 16 * SMALL_LOADS)
            for c in range(DC):
                g = G_PRE[1] + c
                dve.tensor_scalar(w_small_g[:, c, :], w_small[:, c, :], gains[:, g:g + 1], None,
                                  ALU.mult).then_inc(small_scaled, 1)
            swiglu(0, B_UP1)
            post_norm(0)
            mixer()
            post_norm(1)
            memory()
            post_norm(2)
            residual(2, 0)
            for c in range(1, DC):
                residual(2, c)
                pre(3, c - 1)
            pre(3, DC - 1)
            swiglu(3, B_UP2)
            post_norm(3)
            for c in range(DC):
                residual(3, c)
            for t in range(TC):
                dve.wait_ge(oturned, TC + t + 1)
                dve.tensor_copy(out_tok[:, t, HW:D], bank[t][:, :]).then_inc(ocopied_v, 1)

        @block.tensor
        def _(pe):
            def three(dst, w, x, start, stop, loose=False):
                pe.matmul(dst, w[0], x[0], start=start, stop=False, skip_group_check=loose)
                pe.matmul(dst, w[0], x[1], start=False, stop=False, skip_group_check=loose)
                return pe.matmul(dst, w[1], x[0], start=False, stop=stop, skip_group_check=loose)

            def pre_stat(s):
                pe.wait_ge(hacc_ready, DC * (s + 1))
                pe.matmul(bank[STAT_BANK[s]][:, :], ones[:, :], acc[:, :], start=True, stop=True).then_inc(hstat, 1)

            def out_stat(s):
                pe.wait_ge(facc_ready, DC * (s + 1))
                pe.wait_ge(f0_saved, s + 1)
                pe.matmul(out_bank(s, 0)[:, :], ones[:, :], acc[:, :], start=True, stop=True).then_inc(fstat, 1)

            def weights(n, i=None, step=0):
                pe.wait_ge(lo_ready, at_turn(i, step, n + 1))
                return w_hi[:, n % SPLIT, :], w_lo[:, n % SPLIT, :]

            def group_block(n, k, b0, x, width=SEQ, s=None, i=None, step=0):
                w = weights(n, i, step)
                for c in (2 * k, 2 * k + 1):
                    if s is not None:
                        pe.wait_ge(xl_ready, DC * s + c + 1)
                    for m in range(4):
                        cols = slice((c % 2 * 4 + m) * P, (c % 2 * 4 + m + 1) * P)
                        last = three(bank[b0 + m][:, 0:width], (w[0][:, cols], w[1][:, cols]),
                                     (x[0][:, c, :], x[1][:, c, :]), c == 0, c == DC - 1)
                last.then_inc(w_used, 1)

            def token_block(n, k, b0, x, tokens):
                w = weights(n)
                for c in (2 * k, 2 * k + 1):
                    cols = slice(c % 2 * HW, (c % 2 + 1) * HW)
                    for t in range(tokens):
                        tok = slice(t * P, (t + 1) * P)
                        last = three(bank[b0 + t][:, :], (x[0][:, c, tok], x[1][:, c, tok]),
                                     (w[0][:, cols], w[1][:, cols]), c == 0, c == DC - 1)
                last.then_inc(w_used, 1)

            def out_block(s, n, x, first, end, i=None, step=0):
                w = weights(n, i, step)
                for m in range(DC):
                    cols = slice(m * P, (m + 1) * P)
                    last = three(out_bank(s, m)[:, :], (w[0][:, cols], w[1][:, cols]), x, first, end, True)
                    if end and m < DC - 1:
                        last.then_inc(out_done, 1)
                last.then_inc(w_used, 1)

            def swiglu(s, up, down):
                first = 2 * FG * (s // 3)
                if s:
                    pe.wait_ge(f_scaled, DC * s - 4)
                for k in range(KB):
                    if k == KB - 1:
                        pre_stat(s)
                    group_block(up + k, k, 0, (xh, xl), s=s)
                pe.wait_ge(hroot, s + 1)
                with pe.Fori(0, FG // 2) as i:
                    for g in range(2):
                        pe.wait_ge(up_scaled, at_turn(i, 4, first + 2 * g + 1))
                        for k in range(KB):
                            group_block(up + KB * (1 + g) + k, k, 4 * ((1 + g) % 2), (xh, xl),
                                        i=i, step=2 * KB)
                def hidden(c):
                    return [t[:, bass.ds(c, 1), :].rearrange("p o n -> p (o n)") for t in (mid_hi, mid_lo)]

                pe.wait_ge(up_scaled, first + 2 * FG + 1)
                pe.wait_ge(midl_done, first + 1)
                out_block(s, down, hidden(0), True, False)
                with pe.Fori(0, (FC - 2) // 4) as i:
                    for k in range(4):
                        pe.wait_ge(midl_done, at_turn(i, 4, first + 2 + k))
                        out_block(s, down + 1 + k, hidden(at_turn(i, 4, 1 + k)), False, False, i, 4)
                pe.wait_ge(midl_done, first + FC)
                out_block(s, down + FC - 1, hidden(FC - 1), False, True)
                out_stat(s)

            def attention(units, u0, mem):
                y0 = Y_GLA if mem else 0
                for k in range(len(units) + 3):
                    if k < len(units):
                        hd, i = units[k]
                        u, w = u0 + k, key_width(mem, i)
                        if k >= 3:
                            pe.wait_ge(expd, u - 2)
                        dst, tok = bank[k % 3][:, 0:w], slice(i * P, (i + 1) * P)
                        if mem:
                            for e in range(2):
                                c = 2 * hd + e
                                last = three(dst, (qm_hi[:, c, tok], qm_lo[:, c, tok]),
                                             (km_hi[:, c, :], km_lo[:, c, :]), e == 0, e == 1)
                        else:
                            r, c = slice(FOX_D * (hd % 2), FOX_D * (hd % 2 + 1)), hd // 2
                            three(dst, (q_hi[r, c, tok], q_lo[r, c, tok]), (k_hi[r, c, 0:w], k_lo[r, c, 0:w]),
                                  True, False)
                            last = pe.matmul(dst, sel[r, hd, :], cum_hl[r, 0:w], start=False, stop=True)
                        last.then_inc(scored, 1)
                    if 0 <= k - 2 < len(units):
                        u, nk = u0 + k - 2, key_width(mem, units[k - 2][1]) // P
                        pe.wait_ge(normed, u + 1)
                        if k >= 4:
                            pe.wait_ge(pt_l, u - 1)
                        for j in range(nk):
                            last = pe.transpose(bank[3 + k % 2][:, j * P:(j + 1) * P],
                                                prob[:, u % 3, j * P:(j + 1) * P], ident[:, :])
                        last.then_inc(pturned, 1)
                    if k >= 3 and units[k - 3][1] == TC - 1:
                        hd = units[k - 3][0]
                        pe.wait_ge(pt_l, u0 + k - 2)
                        for e in range(2 if mem else 1):
                            idx = 2 * hd + e if mem else hd
                            if idx >= 3:
                                pe.wait_ge(y_l, y0 + idx - 2)
                            for j in range(MC if mem else TC):
                                v, c = ((vm_hi, vm_lo), 2 * hd + e) if mem else ((v_hi, v_lo), hd // 2)
                                q0 = 0 if mem else j * P
                                last = three(o_bank(mem, hd, e)[:, q0:SEQ],
                                             (v[0][:, j, c * P:(c + 1) * P], v[1][:, j, c * P:(c + 1) * P]),
                                             (pt_hi[:, j, q0:SEQ], pt_lo[:, j, q0:SEQ]),
                                             j == 0, j == (MC if mem else TC) - 1, True)
                            last.then_inc(pv_done, 1)

            def gla():
                def head(hd):
                    e = hd % 2
                    return hd // 2, slice(GLA_K * e, GLA_K * (e + 1)), slice(GLA_V * hd, GLA_V * (hd + 1))

                def scores(m):
                    if m:
                        pe.wait_ge(at_masked, 2 * m)
                    else:
                        pe.wait_ge(ke_saved, 2)
                    tok = slice(m * P, (m + 1) * P)
                    for hd in range(GLA_H):
                        c, r, cols = head(hd)
                        last = pe.matmul(bank[4 + hd % 2][:, c * P:(c + 1) * P], gk[r, c, tok], gq[r, c, tok],
                                         start=True, stop=True)
                    last.then_inc(at_done, 1)

                def chunk_state(n):
                    if n >= 2:
                        pe.wait_ge(st_ready, 2 * n - 3)
                    m, r = n // 2, slice(CHUNK * (n % 2), CHUNK * (n % 2 + 1))
                    for c in range(2):
                        cols = slice(2 * GLA_V * c, 2 * GLA_V * (c + 1))
                        last = pe.matmul(bank[6 + n % 2][:, cols], ke_tok[r, m, c, :], gv[r, m, cols],
                                         start=True, stop=True)
                    last.then_inc(sc_done, 1)

                def outputs(m):
                    pe.wait_ge(at_masked, 2 * m + 2)
                    pe.wait_ge(st_ready, 4 * m + 1)
                    for hd in range(GLA_H):
                        c, r, cols = head(hd)
                        last = pe.matmul(bank[hd][:, m * P:(m + 1) * P], gv[:, m, cols],
                                         at_sb[:, m % 2, cols], start=True, stop=False, skip_group_check=True)
                        for n in (2 * m, 2 * m + 1):
                            if n:
                                tok = slice(n * CHUNK, (n + 1) * CHUNK)
                                last = pe.matmul(bank[hd][:, tok], state[r, n - 1, cols], gq[r, c, tok],
                                                 start=False, stop=n % 2 == 1, skip_group_check=True)
                    last.then_inc(o_done, 1)

                pe.wait_ge(gdec, 4)
                pe.wait_ge(y_l, Y_FOX)
                for t in range(2):
                    for j in range(4):
                        m, c = 2 * t + j // 2, j % 2
                        last = pe.transpose(bank[4 + t][:, j * P:(j + 1) * P], gke[:, c, m * P:(m + 1) * P],
                                            ident[:, :])
                    last.then_inc(ke_turned, 1)
                scores(0)
                chunk_state(0)
                for m in range(TC):
                    if m + 1 < TC:
                        scores(m + 1)
                        chunk_state(2 * m + 1)
                        chunk_state(2 * m + 2)
                    outputs(m)

                def mem_turn(half):
                    if half == 0:
                        pe.wait_ge(st_ready, 2 * (NCH - 1) - 1)
                        pe.wait_ge(mem_normed, MC)
                    else:
                        pe.wait_ge(mem_l, 4)
                    for j in range(8):
                        c, t = 4 * half + j // 2, j % 2
                        col = c % 2 * NMEM + t * P
                        last = pe.transpose(bank[6 + c // 2 % 2][:, col:col + P], mem_n[:, t, c * P:(c + 1) * P],
                                            ident[:, :])
                        if j % 4 == 3:
                            last.then_inc(mem_turned, 1)

                for hd in range(GLA_H):
                    pe.wait_ge(gsq, hd + 1)
                    if hd >= 2:
                        pe.wait_ge(groot, hd - 1)
                    pe.matmul(bank[4 + hd % 2][:, :], ones[:, :], sq[:, hd % 2, :], start=True,
                              stop=True).then_inc(gstat, 1)
                mem_turn(0)
                mem_turn(1)

            def mixer():
                pe.wait_ge(f_scaled, 4)
                for k in range(KB):
                    if k == KB - 1:
                        pre_stat(1)
                        for t in range(TC):
                            last = pe.matmul(bank[TOK_BANK][:, t:t + 1], acc[:, t * P:(t + 1) * P], ones[:, 0:1],
                                             start=True, stop=True)
                        last.then_inc(tokstat, 1)
                        pe.wait_ge(small_scaled, DC)
                        for c in range(DC):
                            last = pe.matmul(bank[SMALL_BANK][0:48, :], w_small_g[:, c, :], h[:, c, :],
                                             start=c == 0, stop=c == DC - 1)
                        last.then_inc(small_done, 1)
                    group_block(B_IN + k, k, IN_BANK[0], (xh, xl), s=1)
                pe.wait_ge(hroot, 2)
                pe.wait_ge(tokroot, 1)
                pe.wait_ge(z_ready, 1)
                free = {2: (z_ready, 3), 3: (in_tmp, 8), 4: (in_lo, 12), 5: (in_lo, 16)}
                for g in range(1, 6):
                    if g in free:
                        pe.wait_ge(*free[g])
                    for k in range(KB):
                        n = B_IN + KB * g + k
                        if g in (2, 4):
                            token_block(n, k, IN_BANK[g], (xh, xl), TC)
                        else:
                            group_block(n, k, IN_BANK[g], (xh, xl))
                        if g == 1 and k == 1:
                            pe.wait_ge(in_tmp, 4)
                            for j in range(2):
                                pe.matmul(bank[6 + j][:, :], w_a2[32:48, j * P:(j + 1) * P], zg[32:48, :],
                                          start=True, stop=True).then_inc(ga_done, 1)
                pe.wait_ge(in_lo, 12)
                pe.wait_ge(cum_lo, 2)
                pe.wait_ge(sel_ready, 1)
                pe.wait_ge(in_tmp, 12)
                pe.wait_ge(in_hi, 16)
                attention(FOX_UNITS, 0, False)
                gla()
                pe.wait_ge(groot, GLA_H)
                pe.wait_ge(mem_l, DC)
                pe.wait_ge(gnorm, GLA_H)
                for c in range(DC):
                    pe.wait_ge(y_l, Y_FOX if c < 4 else Y_FOX + c - 3)
                    out_block(1, B_OUT + c, (xh[:, c, :], xl[:, c, :]), c == 0, c == DC - 1)
                out_stat(1)

            def memory():
                free = ((f_scaled, DC + 4), (f_scaled, 2 * DC), (kv_l, 4), (kv_l, 8))
                for g in range(4):
                    pe.wait_ge(*free[g])
                    for k in range(KB):
                        n = B_KV + KB * g + k
                        if g < 2:
                            group_block(n, k, KV_BANK[g], (mem_hi, mem_lo), NMEM)
                        else:
                            token_block(n, k, KV_BANK[g], (mem_hi, mem_lo), MC)
                pre_stat(2)
                for g in range(2):
                    pe.wait_ge(kv_l, 10 + 2 * g)
                    if g:
                        pe.wait_ge(hroot, 3)
                    for k in range(KB):
                        group_block(B_MQ + KB * g + k, k, MQ_BANK[g], (xh, xl))
                pe.wait_ge(mq_l, DC)
                attention(MEM_UNITS, N_FOX, True)
                pe.wait_ge(y_l, Y_GLA + DC)
                for c in range(DC):
                    out_block(2, B_MO + c, (xh[:, c, :], xl[:, c, :]), c == 0, c == DC - 1)
                out_stat(2)

            pe.wait_ge(consts, 5)
            pe.wait_ge(small_landed, 16 * SMALL_LOADS)
            pe.transpose(bank[7][:, 0:G_ROWS], gain_rows[:, :], ident[0:G_ROWS, 0:G_ROWS]).then_inc(gains_turned, 1)
            pe.wait_ge(x_landed, 16 * TC)
            for c in range(DC):
                if c == DC - 1:
                    pe.wait_ge(gains_ready, 1)
                for t in range(TC):
                    last = pe.transpose(bank[c][:, t * P:(t + 1) * P], x_tok[:, t, c * P:(c + 1) * P], ident[:, :])
                last.then_inc(turned, 1)
            pe.wait_ge(h_ready, 4)
            swiglu(0, B_UP1, B_DOWN1)
            mixer()
            memory()
            swiglu(3, B_UP2, B_DOWN2)
            for half in range(2):
                pe.wait_ge(h_ready, DC * SUBLAYERS + 4 * (half + 1))
                for t in range(TC):
                    for j in range(4):
                        last = pe.transpose(bank[4 * (1 - half) + t][:, j * P:(j + 1) * P],
                                            h[:, 4 * half + j, t * P:(t + 1) * P], ident[:, :])
                    last.then_inc(oturned, 1)


_INS = ("x", "mem", "ffn1_g_pre", "ffn1_w_gu", "ffn1_w_down", "ffn1_g_post", "mix_g_pre", "mix_w_in",
        "mix_w_a2", "mix_b_a", "mix_b_f", "mix_g_gla", "mix_w_out", "mix_g_post", "mem_g_pre",
        "mem_g_kv", "mem_w_q", "mem_w_kv", "mem_w_o", "mem_g_post", "ffn2_g_pre", "ffn2_w_gu",
        "ffn2_w_down", "ffn2_g_post")


def kernel(**inputs):
    import numpy as _np
    import concourse.bacc as _bacc
    from concourse import mybir as _mybir
    from concourse.bass_utils import run_bass_kernel_spmd as _run

    nc = _bacc.Bacc("TRN2", target_bir_lowering=False, num_devices=1)
    arrays, args = {}, {}
    for name in _INS:
        array = _np.ascontiguousarray(inputs[name])
        arrays[f"in_{name}"] = array
        args[name] = nc.dram_tensor(f"in_{name}", array.shape, _mybir.dt.from_np(array.dtype),
                                    kind="ExternalInput").ap()
    out = nc.dram_tensor("out", (1, SEQ, D), _mybir.dt.float32, kind="ExternalOutput").ap()
    build(nc, args, out)
    r = _run(nc, [arrays], core_ids=[0])
    return r.results[0]["out"]
```

```python
from contextlib import ExitStack

import concourse.bass as bass
from concourse import mybir

F32 = mybir.dt.float32
F32R = mybir.dt.float32r
ALU = mybir.AluOpType
ACT = mybir.ActivationFunctionType
AX_X = mybir.AxisListType.X

P = 128
SEQ = 512
D = 1024
DC = D // P
TC = SEQ // P
FF = 2816
FC = FF // P
FG = FC // 2
NMEM = 256
MC = NMEM // P
FOX_H, FOX_D = 8, 64
GLA_H, GLA_K, GLA_V, CHUNK, RANK = 4, 64, 128, 64, 16
NCH = SEQ // CHUNK
MEM_H, MEM_D = 4, 256
FOX_W, GLA_KW, GLA_VW = FOX_H * FOX_D, GLA_H * GLA_K, GLA_H * GLA_V
COL_FQ, COL_FK, COL_FV = 0, FOX_W, 2 * FOX_W
COL_FZ = 3 * FOX_W
COL_GQ = COL_FZ + FOX_H
COL_GV = COL_GQ + 2 * GLA_KW
COL_GR = COL_GV + GLA_VW
COL_GA = COL_GR + GLA_VW
EPS = 1e-6
TAU = 16.0
NEG = -1e30
SUBLAYERS = 4
BW = 1024
HW = BW // 2
RAW, SPLIT = 4, 2
LAND = 32

KB = DC // 2
B_UP1 = 0
B_DOWN1 = B_UP1 + FG * KB
B_IN = B_DOWN1 + FC
IN_COLS = (COL_FQ, COL_FK, COL_FV, COL_GQ, COL_GV, COL_GR)
B_OUT = B_IN + len(IN_COLS) * KB
B_KV = B_OUT + DC
B_MQ = B_KV + 4 * KB
B_MO = B_MQ + 2 * KB
B_UP2 = B_MO + DC
B_DOWN2 = B_UP2 + FG * KB
B_END = B_DOWN2 + FC
OUT_FIRST = (B_DOWN1, B_OUT, B_MO, B_DOWN2)
OUT_END = (B_IN, B_KV, B_UP2, B_END)

GAINS = ("ffn1_g_pre", "ffn1_g_post", "mix_g_pre", "mix_g_post", "mem_g_pre", "mem_g_kv",
         "mem_g_post", "ffn2_g_pre", "ffn2_g_post")
G_PRE = (0, 16, 32, 56)
G_POST = (8, 24, 48, 64)
G_KV = 40
G_BA = 72
G_GLA = 74
G_ROWS = 78
POST_SCALE = (0.5, 1.0, 1.0, 0.5)
GAIN_LOADS, SMALL_LOADS = len(GAINS) + 2, 4

OUT_OFF = (4, 4, 0, 4)
STAT_BANK = (6, 2, 2, 6)
SMALL_BANK = 3
IN_BANK = (4, 0, 4, 4, 4, 4)
KV_BANK = (4, 0, 4, 0)
MQ_BANK = (4, 0)

FOX_UNITS = [(hd, i) for hd in range(FOX_H) for i in range(TC)]
MEM_UNITS = [(hd, i) for hd in range(MEM_H) for i in range(TC)]
N_FOX = len(FOX_UNITS)
FILL_GROUPS = (3, 4, 5)
FILL_GROUP = 4 * KB
FILL = (0, 1, 2, 2, 1, 1, 2, 2, 1, 1, 2, 1,
        0, 1, 2, 2, 1, 1, 2, 2, 2, 1, 2,
        0, 1, 1, 2, 2, 2, 1, 2, 2, 2, 1)
FILL_END = tuple(min(k for k in range(len(FILL)) if sum(FILL[:k + 1]) == FILL_GROUP * (j + 1))
                 for j in range(len(FILL_GROUPS)))
N_UNITS = N_FOX + len(MEM_UNITS)
Y_FOX = FOX_H
Y_GLA = Y_FOX + GLA_H
N_CONSTS = 17


def build(nc, a, out):
    ctx = ExitStack()
    with ctx:
        sems = {}

        def sem(name):
            sems[name] = ctx.enter_context(nc.semaphore(name))
            return sems[name]

        top = [(nc.sbuf_base + 31) // 32 * 32]
        ends = []

        def sb(name, shape, dt=F32, at=None):
            size = 4
            for n in shape[1:]:
                size *= n
            where = top[0] if at is None else at
            if at is None:
                top[0] += (size + 31) // 32 * 32
            ends.append(where + size)
            return nc.alloc_sbuf_tensor_at(name, shape, dt, offset=where)

        h = sb("h", [P, DC, SEQ])
        xh = sb("xh", [P, DC, SEQ], F32R)
        xl = sb("xl", [P, DC, SEQ], F32R)
        raw = sb("raw", [P, RAW, BW])
        w_hi = sb("w_hi", [P, SPLIT, BW], F32R)
        w_lo = sb("w_lo", [P, SPLIT, BW], F32R)
        tmp = sb("tmp", [P, 4, SEQ])
        sq = sb("sq", [P, 2, SEQ])
        cum_hl = sb("cum_hl", [P, SEQ], F32R, at=top[0])
        acc = sb("acc", [P, SEQ])
        rinv = sb("rinv", [P, SEQ])
        ident = sb("ident", [P, P])
        ones = sb("ones", [P, P])
        ident_r = sb("ident_r", [P, P], F32R)
        causal = sb("causal", [P, P], F32R)
        gla_mask = sb("gla_mask", [P, P])
        gains = sb("gains", [P, G_ROWS])
        post = sb("post", [P, SUBLAYERS, DC])
        root_tok = sb("root_tok", [P, TC])
        rinv_tok = sb("rinv_tok", [P, TC])
        g_root = sb("g_root", [P, GLA_H * TC])
        g_rinv = sb("g_rinv", [P, GLA_H * TC])
        eps_t = sb("eps_t", [P, 1])
        b_f = sb("b_f", [FOX_H, 1])
        decay = sb("decay", [P, 2, NCH])
        nmx = sb("nmx", [P, 4])
        rs = sb("rs", [P, 4])
        rr = sb("rr", [P, 4])
        mem_ms = sb("mem_ms", [P, MC])
        mem_root = sb("mem_root", [P, MC])
        mem_rinv = sb("mem_rinv", [P, MC])
        shared = top[0]
        kib = 1024

        mid_hi = sb("mid_hi", [P, FC, SEQ], F32R, at=shared)
        mid_lo = sb("mid_lo", [P, FC, SEQ], F32R, at=shared + 44 * kib)
        x_tok = sb("x_tok", [P, TC, D], at=shared)
        out_tok = sb("out_tok", [P, TC, D], at=shared)
        gain_rows = sb("gain_rows", [G_ROWS, P], at=shared + 16 * kib)

        q_hi = sb("q_hi", [P, 4, SEQ], F32R, at=shared)
        q_lo = sb("q_lo", [P, 4, SEQ], F32R, at=shared + 8 * kib)
        k_hi = sb("k_hi", [P, 4, SEQ], F32R, at=shared + 16 * kib)
        k_lo = sb("k_lo", [P, 4, SEQ], F32R, at=shared + 24 * kib)
        v_hi = sb("v_hi", [P, TC, FOX_W], F32R, at=shared + 32 * kib)
        v_lo = sb("v_lo", [P, TC, FOX_W], F32R, at=shared + 40 * kib)
        gq = sb("gq", [P, 2, SEQ], at=shared + 48 * kib)
        gk = sb("gk", [P, 2, SEQ], at=shared + 52 * kib)
        gke = sb("gke", [P, 2, SEQ], at=shared + 56 * kib)
        gb = sb("gb", [P, 2, SEQ], at=shared + 60 * kib)
        gv = sb("gv", [P, TC, GLA_VW], at=shared + 64 * kib)
        gr = sb("gr", [P, GLA_H, SEQ], at=shared + 72 * kib)
        prob = sb("prob", [P, 2, SEQ], at=shared + 80 * kib)
        norm_diag = sb("norm_diag", [P, 2, P], at=shared + 84 * kib)
        pt_hi = sb("pt_hi", [P, TC, SEQ], F32R, at=shared + 86 * kib)
        pt_lo = sb("pt_lo", [P, TC, SEQ], F32R, at=shared + 94 * kib)
        sel = sb("sel", [P, FOX_H, P], F32R, at=shared + 102 * kib)
        ls_min = sb("ls_min", [P, 2, SEQ], at=shared + 72 * kib)
        cum = sb("cum", [FOX_H, SEQ], at=shared + 80 * kib)
        w_small = sb("w_small", [P, DC, 48], at=shared + 88 * kib)
        w_small_g = sb("w_small_g", [P, DC, 48], at=shared + 88 * kib + 1536)
        zg = sb("zg", [48, SEQ], at=shared + 91 * kib)
        w_a2 = sb("w_a2", [48, GLA_KW], at=shared + 93 * kib)
        ls_abs = sb("ls_abs", [P, 3, SEQ], at=shared + 94 * kib)
        sel32 = sb("sel32", [P, FOX_H, P], at=shared + 94 * kib)
        causal32 = sb("causal32", [P, P], at=shared + 98 * kib)
        reset = sb("reset", [P, SEQ], at=shared + 100 * kib)
        fox_hi, fox_lo = q_hi, q_lo
        ke_tok = sb("ke_tok", [P, TC, 2, P], at=shared + 16 * kib)
        at_sb = sb("at_sb", [P, 2, SEQ], at=shared + 20 * kib)
        state = sb("state", [P, NCH - 1, SEQ], at=shared + 24 * kib)
        qm_hi = sb("qm_hi", [P, DC, SEQ], F32R, at=shared)
        qm_lo = sb("qm_lo", [P, DC, SEQ], F32R, at=shared + 16 * kib)
        mem_hi = sb("mem_hi", [P, DC, NMEM], F32R, at=shared + 32 * kib)
        mem_lo = sb("mem_lo", [P, DC, NMEM], F32R, at=shared + 40 * kib)
        km_hi = sb("km_hi", [P, DC, NMEM], F32R, at=shared + 48 * kib)
        km_lo = sb("km_lo", [P, DC, NMEM], F32R, at=shared + 56 * kib)
        vm_hi = sb("vm_hi", [P, MC, D], F32R, at=shared + 64 * kib)
        vm_lo = sb("vm_lo", [P, MC, D], F32R, at=shared + 72 * kib)
        mem_tok = sb("mem_tok", [P, MC, D], at=shared + 86 * kib)
        mem_n = sb("mem_n", [P, MC, D], at=shared + 94 * kib)
        assert max(ends) <= nc.sbuf_usable_end, (max(ends), nc.sbuf_usable_end)
        f0 = tmp[:, 3, :]

        bank = [ctx.enter_context(nc.psum_tensor(f"bank{i}", [P, SEQ], F32)) for i in range(8)]

        def out_bank(s, c):
            return bank[(c + OUT_OFF[s]) % 8]

        landed = [sem(f"landed{i}") for i in range(RAW)]
        hi_ready = sem("hi_ready")
        lo_ready = sem("lo_ready")
        w_used = sem("w_used")
        x_landed = sem("x_landed")
        gains_landed = sem("gains_landed")
        small_landed = sem("small_landed")
        mem_landed = sem("mem_landed")
        stored = sem("stored")
        consts = sem("consts")
        gains_turned = sem("gains_turned")
        gains_ready = sem("gains_ready")
        turned = sem("turned")
        h_ready = sem("h_ready")
        xh_ready = sem("xh_ready")
        xl_ready = sem("xl_ready")
        hsq_ready = sem("hsq_ready")
        hacc_ready = sem("hacc_ready")
        hstat = sem("hstat")
        hroot = sem("hroot")
        hinv = sem("hinv")
        hspread = sem("hspread")
        hrinv = sem("hrinv")
        out_done = sem("out_done")
        fsq_ready = sem("fsq_ready")
        facc_ready = sem("facc_ready")
        f0_saved = sem("f0_saved")
        fstat = sem("fstat")
        froot = sem("froot")
        finv = sem("finv")
        fspread = sem("fspread")
        frinv = sem("frinv")
        f_scaled = sem("f_scaled")
        gate_scaled = sem("gate_scaled")
        up_scaled = sem("up_scaled")
        silu_done = sem("silu_done")
        mid_done = sem("mid_done")
        midh_done = sem("midh_done")
        midl_done = sem("midl_done")
        small_scaled = sem("small_scaled")
        small_done = sem("small_done")
        z_ready = sem("z_ready")
        ga_done = sem("ga_done")
        z_min = sem("z_min")
        ls_act = sem("ls_act")
        cum_step = sem("cum_step")
        gcum_step = sem("gcum_step")
        cum_hi = sem("cum_hi")
        cum_lo = sem("cum_lo")
        sel_ready = sem("sel_ready")
        in_tmp = sem("in_tmp")
        in_hi = sem("in_hi")
        in_lo = sem("in_lo")
        exps = sem("exps")
        gdec = sem("gdec")
        scored = sem("scored")
        maxed = sem("maxed")
        expd = sem("expd")
        rsum = sem("rsum")
        normed = sem("normed")
        pturned = sem("pturned")
        pt_h = sem("pt_h")
        pt_l = sem("pt_l")
        pv_done = sem("pv_done")
        y_h = sem("y_h")
        y_l = sem("y_l")
        ke_turned = sem("ke_turned")
        ke_saved = sem("ke_saved")
        at_done = sem("at_done")
        at_masked = sem("at_masked")
        sc_done = sem("sc_done")
        st_ready = sem("st_ready")
        o_done = sem("o_done")
        gsq = sem("gsq")
        gstat = sem("gstat")
        groot = sem("groot")
        ginv = sem("ginv")
        gspread = sem("gspread")
        gfactor = sem("gfactor")
        gout = sem("gout")
        mem_sq = sem("mem_sq")
        mem_root_s = sem("mem_root_s")
        mem_inv = sem("mem_inv")
        mem_normed = sem("mem_normed")
        mem_turned = sem("mem_turned")
        mem_h = sem("mem_h")
        mem_l = sem("mem_l")
        kv_h = sem("kv_h")
        kv_l = sem("kv_l")
        mq_t = sem("mq_t")
        mq_h = sem("mq_h")
        mq_l = sem("mq_l")
        oturned = sem("oturned")
        ocopied_a = sem("ocopied_a")
        ocopied_v = sem("ocopied_v")

        def at_turn(i, step, n):
            return n if i is None else i * step + n

        def wait_out(eng, s, c):
            if c < DC - 1:
                eng.wait_ge(out_done, (DC - 1) * s + c + 1)
            else:
                eng.wait_ge(w_used, OUT_END[s])

        def pv_count(mem, hd, e=0):
            return FOX_H + 2 * hd + e if mem else hd

        def s_bank(mem, k):
            return bank[k % (3 if mem else 2)]

        def p_bank(mem, k):
            return bank[3 + k % 2 if mem else 2]

        def o_bank(mem, hd, e=0):
            return bank[5 + (2 * hd + e) % 3 if mem else 3]

        def key_width(mem, i):
            return NMEM if mem else P * (i + 1)

        block = ctx.enter_context(nc.Block())

        @block.sync
        def _(sp):
            def fetch(n, srcs, i=None, step=0):
                if n >= RAW:
                    sp.wait_ge(lo_ready, at_turn(i, step, n - RAW + 1))
                for piece, src in enumerate(srcs):
                    dst = raw[:, n % RAW, :]
                    if len(src.shape) == 3:
                        dst = dst.rearrange("p (k u n) -> p k u n", k=2, u=2)[:, :, piece, :]
                    else:
                        dst = dst[:, piece * HW:(piece + 1) * HW]
                    sp.dma_start(dst, src).then_inc(landed[n % RAW], 16)

            def up_cols(w, k, col):
                return [w[2 * k * P:(2 * k + 2) * P, bass.ds(col + u * FF, 2 * P)].rearrange(
                    "(k p) n -> p k n", p=P) for u in range(2)]

            def row_pair(w, k, col):
                return [w[(2 * k + j) * P:(2 * k + j + 1) * P, col:col + HW] for j in range(2)]

            def row(w, start):
                return [w[bass.ds(start, P), j * HW:(j + 1) * HW] for j in range(2)]

            def small_loads():
                sp.dma_start(b_f[:, :], a["mix_b_f"].rearrange("l (h o) -> (l h) o", o=1)).then_inc(small_landed, 16)
                sp.dma_start(w_a2[32:48, :], a["mix_w_a2"][0]).then_inc(small_landed, 16)
                sp.wait_ge(consts, 5)
                for c0, width, where in ((COL_FZ, FOX_H, 0), (COL_GA, RANK, 32)):
                    sp.dma_start(w_small[:, :, where:where + width],
                                 a["mix_w_in"][0][:, c0:c0 + width].rearrange("(c p) n -> p c n", p=P))\
                      .then_inc(small_landed, 16)

            def swiglu_loads(w_gu, w_down, up, down, also=None):
                for k in range(KB):
                    fetch(up + k, up_cols(w_gu, k, 0))
                if also:
                    also()
                with sp.Fori(0, FG // 2) as i:
                    for k in range(2 * KB):
                        fetch(up + KB + k, up_cols(w_gu, k % KB, i * (4 * P) + (1 + k // KB) * 2 * P),
                              i, 2 * KB)
                for k in range(2):
                    fetch(down + k, row(w_down, k * P))
                with sp.Fori(0, (FC - 2) // 4) as i:
                    for k in range(4):
                        fetch(down + 2 + k, row(w_down, i * (4 * P) + (2 + k) * P), i, 4)

            for t in range(TC):
                sp.dma_start(x_tok[:, t, :], a["x"][0, t * P:(t + 1) * P, :]).then_inc(x_landed, 16)
            swiglu_loads(a["ffn1_w_gu"][0], a["ffn1_w_down"][0], B_UP1, B_DOWN1, small_loads)
            for n in range(B_IN, B_OUT):
                fetch(n, row_pair(a["mix_w_in"][0], (n - B_IN) % KB, IN_COLS[(n - B_IN) // KB]))
            for n in range(B_OUT, B_KV):
                fetch(n, row(a["mix_w_out"][0], (n - B_OUT) * P))
                if n == B_OUT + RAW - 1:
                    sp.wait_ge(pv_done, FOX_H)
                    for t in range(MC):
                        sp.dma_start(mem_tok[:, t, :], a["mem"][0, t * P:(t + 1) * P, :]).then_inc(mem_landed, 16)
            for n in range(B_KV, B_MQ):
                fetch(n, row_pair(a["mem_w_kv"][0], (n - B_KV) % KB, (n - B_KV) // KB * HW))
            for n in range(B_MQ, B_MO):
                fetch(n, row_pair(a["mem_w_q"][0], (n - B_MQ) % KB, (n - B_MQ) // KB * HW))
            for n in range(B_MO, B_UP2):
                fetch(n, row(a["mem_w_o"][0], (n - B_MO) * P))
            swiglu_loads(a["ffn2_w_gu"][0], a["ffn2_w_down"][0], B_UP2, B_DOWN2)
            for half, copied in enumerate((ocopied_a, ocopied_v)):
                for t in range(TC):
                    sp.wait_ge(copied, t + 1)
                    cols = slice(half * HW, (half + 1) * HW)
                    sp.dma_start(out[0, t * P:(t + 1) * P, cols], out_tok[:, t, cols]).then_inc(stored, 16)
            sp.wait_ge(stored, 16 * 2 * TC)

        @block.gpsimd
        def _(gp):
            count = [0]

            def const(ins):
                count[0] += 1
                ins.then_inc(consts, 1)
                gp.wait_ge(consts, count[0])

            def split(n, i=None):
                gp.wait_ge(hi_ready, at_turn(i, RAW, n + 1))
                gp.tensor_tensor(w_lo[:, n % SPLIT, :], raw[:, n % RAW, :],
                                 w_hi[:, n % SPLIT, :].bitcast(F32), ALU.subtract).then_inc(lo_ready, 1)

            const(gp.memset(ident[:, :], 0.0))
            const(gp.affine_select(out=ident[:, :], in_=ident[:, :], compare_op=ALU.not_equal, fill=1.0,
                                   base=0, pattern=[[-1, P]], channel_multiplier=1))
            const(gp.memset(ones[:, :], 1.0))
            const(gp.memset(eps_t[:, :], EPS))
            const(gp.memset(w_small[:, :, :], 0.0))
            split(0)
            split(1)
            const(gp.memset(causal32[:, :], 0.0))
            const(gp.affine_select(out=causal32[:, :], in_=causal32[:, :], compare_op=ALU.is_ge, fill=NEG,
                                   base=0, pattern=[[-1, P]], channel_multiplier=1))
            const(gp.memset(gla_mask[:, :], 1.0))
            const(gp.affine_select(out=gla_mask[:, :], in_=gla_mask[:, :], compare_op=ALU.is_ge, fill=0.0,
                                   base=0, pattern=[[1, P]], channel_multiplier=-1))
            const(gp.memset(gla_mask[0:CHUNK, CHUNK:P], 0.0))
            const(gp.memset(reset[:, :], 1.0))
            const(gp.memset(reset[:, :].rearrange("p (n c) -> p n c", c=CHUNK)[:, :, 0:1], 0.0))
            const(gp.memset(sel32[:, :, :], 0.0))
            for base in (0, -32, -64, -96):
                const(gp.affine_select(out=sel32[:, :, :], in_=sel32[:, :, :], compare_op=ALU.not_equal,
                                       fill=-1.0, base=base, pattern=[[-1, FOX_H], [0, P]],
                                       channel_multiplier=1))
            assert count[0] == N_CONSTS, count[0]
            split(2)
            split(3)
            with gp.Fori(1, B_END // RAW) as i:
                for q in range(RAW):
                    split(q, i)
            for n in range(B_END // RAW * RAW, B_END):
                split(n)

        @block.scalar
        def _(act):
            rounded = [0]

            def round_block(n, i=None, step=0):
                act.wait_ge(landed[n % RAW], at_turn(i, LAND * step // RAW, LAND * (n // RAW + 1)))
                if n >= SPLIT:
                    act.wait_ge(w_used, at_turn(i, step, n - SPLIT + 1))
                act.activation(w_hi[:, n % SPLIT, :], raw[:, n % RAW, :], ACT.Copy).then_inc(hi_ready, 1)

            def round_to(end):
                while rounded[0] < min(end, B_END):
                    round_block(rounded[0])
                    rounded[0] += 1

            def pre(s, c):
                act.wait_ge(h_ready, DC * s + c + 1)
                g = G_PRE[s] + c
                act.activation(xh[:, c, :], h[:, c, :], ACT.Copy, scale=gains[:, g:g + 1]).then_inc(xh_ready, 1)
                if c >= 2:
                    act.wait_ge(hacc_ready, (DC - 1) * s + c - 1)
                elif s:
                    act.wait_ge(facc_ready, (DC - 1) * s)
                act.activation(sq[:, c % 2, :], h[:, c, :], ACT.Square).then_inc(hsq_ready, 1)

            def rms_root(dst, src, n):
                return act.activation(dst, src, ACT.Sqrt, bias=eps_t[:, 0:1], scale=1.0 / n)

            def pre_root(s):
                act.wait_ge(hstat, s + 1)
                rms_root(root_tok[:, :], bank[STAT_BANK[s]][:, 0:TC], D).then_inc(hroot, 1)
                round_to((B_UP1, B_IN, B_MQ, B_UP2)[s] + KB + 1)
                act.wait_ge(hspread, s + 1)
                act.activation(rinv[:, :], bank[STAT_BANK[s]][:, :], ACT.Copy).then_inc(hrinv, 1)

            def post_norm(s):
                round_to(OUT_END[s] + 1)
                act.preload_act_table(ACT.Sqrt)
                for m in range(DC):
                    wait_out(act, s, m)
                    if m >= 2:
                        act.wait_ge(facc_ready, (DC - 1) * s + m - 1)
                    else:
                        act.wait_ge(hacc_ready, (DC - 1) * (s + 1))
                    act.activation(sq[:, m % 2, :], out_bank(s, m)[:, :], ACT.Square).then_inc(fsq_ready, 1)
                round_to(OUT_END[s] + 2)
                act.wait_ge(fstat, s + 1)
                rms_root(root_tok[:, :], out_bank(s, 0)[:, 0:TC], D).then_inc(froot, 1)
                act.wait_ge(fspread, s + 1)
                act.activation(rinv[:, :], out_bank(s, 0)[:, :], ACT.Copy).then_inc(frinv, 1)

            def swiglu(s, up, down):
                first = 2 * FG * (s // 3)

                def group(g, i=None):
                    for pair in range(2):
                        act.wait_ge(gate_scaled, at_turn(i, 4, first + 2 * g + pair + 1))
                        act.activation(tmp[:, pair, :], tmp[:, pair, :], ACT.Silu).then_inc(silu_done, 1)
                    for pair in range(2):
                        act.wait_ge(mid_done, at_turn(i, 4, first + 2 * g + pair + 1))
                        act.activation(mid_hi[:, bass.ds(at_turn(i, 4, 2 * g + pair), 1), :],
                                       tmp[:, 2 + pair:3 + pair, :], ACT.Copy).then_inc(midh_done, 1)

                for c in range(DC):
                    pre(s, c)
                    if c in (3, 5):
                        round_to(up + 2 + (c - 1) // 2)
                pre_root(s)
                round_to(up + 6)
                group(0)
                if s == 0:
                    act.wait_ge(consts, N_CONSTS)
                    act.activation(sel[:, :, :], sel32[:, :, :], ACT.Copy).then_inc(sel_ready, 1)
                    act.activation(causal[:, :], causal32[:, :], ACT.Copy).then_inc(sel_ready, 1)
                    act.activation(ident_r[:, :], ident[:, :], ACT.Copy).then_inc(sel_ready, 1)
                with act.Fori(0, FG // 2) as i:
                    for g in range(2):
                        for k in range(KB):
                            round_block(up + 6 + KB * g + k, i, 2 * KB)
                        group(1 + g, i)
                with act.Fori(0, (FC - 2) // 4) as i:
                    for k in range(4):
                        round_block(down + 2 + k, i, 4)
                rounded[0] = down + FC

            def log_sigmoid(gates):
                first, n = 3 * gates[0], len(gates)
                t = {j: ls_abs[0:FOX_H, j, :] if j == 0 else ls_abs[:, j, :] for j in gates}
                for j in gates:
                    act.wait_ge(z_ready, 1 + j)
                    if j == 0:
                        act.activation(t[j], zg[0:FOX_H, :], ACT.Abs, bias=b_f[:, 0:1]).then_inc(ls_act, 1)
                    else:
                        act.activation(t[j], gb[:, j - 1, :], ACT.Abs).then_inc(ls_act, 1)
                for k, j in enumerate(gates):
                    act.wait_ge(ls_act, first + k + 1)
                    act.activation(t[j], t[j], ACT.Exp, scale=-1.0).then_inc(ls_act, 1)
                for k, j in enumerate(gates):
                    act.wait_ge(ls_act, first + n + k + 1)
                    act.activation(t[j], t[j], ACT.Ln, bias=1.0).then_inc(ls_act, 1)

            def in_evacuate(g):
                b = bank[IN_BANK[g]:IN_BANK[g] + 4]
                for m in range(4):
                    if g < 2:
                        act.wait_ge(in_tmp, 4 * g + m + 1)
                        act.activation((q_hi, k_hi)[g][:, m, :], tmp[:, m, :], ACT.Copy).then_inc(in_hi, 1)
                    elif g in (2, 4):
                        act.wait_ge(w_used, B_IN + KB * (g + 1))
                        act.wait_ge(hinv, 2)
                        act.activation((v_hi if g == 2 else gv)[:, m, :], b[m][:, :], ACT.Copy,
                                       scale=rinv_tok[:, m:m + 1]).then_inc(in_hi, 1)
                    elif g == 5:
                        act.wait_ge(in_tmp, 12 + m + 1)
                        act.activation(gr[:, m, :], tmp[:, m, :], ACT.Silu).then_inc(in_hi, 1)

            def decays():
                act.wait_ge(gcum_step, 5)
                act.activation(decay[:, :, :], gb[:, :, :].rearrange("p k (n c) -> p k n c", c=CHUNK)[:, :, :, CHUNK - 1],
                               ACT.Exp, scale=1.0 / TAU).then_inc(exps, 1)
                act.activation(gq[:, :, :], gb[:, :, :], ACT.Exp, scale=1.0 / TAU).then_inc(exps, 1)
                act.activation(gke[:, :, :], gke[:, :, :], ACT.Exp, scale=1.0 / TAU).then_inc(exps, 1)
                act.activation(gk[:, :, :], gb[:, :, :], ACT.Exp, scale=-1.0 / TAU).then_inc(exps, 1)

            def attention(units, u0, mem):
                late = 2 if mem else 1
                for k in range(len(units) + late + 2):
                    if k < len(units):
                        u, w = u0 + k, key_width(mem, units[k][1])
                        act.wait_ge(maxed, u + 1)
                        if u >= 2:
                            act.wait_ge(pturned, u - 1)
                        act.activation(prob[:, u % 2, 0:w], s_bank(mem, k)[:, 0:w], ACT.Exp,
                                       bias=nmx[:, u % 4:u % 4 + 1],
                                       accum_out=rs[:, u % 4:u % 4 + 1]).then_inc(expd, 1)
                    if not mem:
                        round_to(B_IN + KB * FILL_GROUPS[0] + 2 + sum(FILL[:k]) // 4)
                    if 0 <= k - late < len(units):
                        hd, i = units[k - late]
                        nk = key_width(mem, i) // P
                        act.wait_ge(pturned, u0 + k - late + 1)
                        if hd:
                            act.wait_ge(pv_done, pv_count(mem, hd))
                        act.activation(pt_hi[:, 0:nk, i * P:(i + 1) * P],
                                       p_bank(mem, k)[:, 0:nk * P].rearrange("p (j n) -> p j n", n=P),
                                       ACT.Copy).then_inc(pt_h, 1)
                    done = k - late - 2 if mem else k - late - 1
                    if 0 <= done < len(units) and units[done][1] == TC - 1:
                        hd = units[done][0]
                        for e in range(2 if mem else 1):
                            act.wait_ge(pv_done, pv_count(mem, hd, e) + 1)
                            o = o_bank(mem, hd, e)
                            if mem:
                                act.activation(xh[:, 2 * hd + e, :], o[:, :], ACT.Copy).then_inc(y_h, 1)
                            else:
                                r = slice(FOX_D * (hd % 2), FOX_D * (hd % 2 + 1))
                                act.activation(fox_hi[r, hd // 2, :], o[r, :], ACT.Copy).then_inc(y_h, 1)
                    if not mem and k == FILL_END[1]:
                        in_evacuate(4)

            def gla():
                for t in range(2):
                    act.wait_ge(ke_turned, t + 1)
                    act.activation(ke_tok[:, 2 * t:2 * t + 2, :, :], bank[t][:, :].rearrange(
                        "p (t c d) -> p t c d", t=2, c=2), ACT.Copy).then_inc(ke_saved, 1)
                in_evacuate(5)
                act.preload_act_table(ACT.Sqrt)
                act.wait_ge(mem_landed, 16 * MC)
                for t in range(MC):
                    act.activation(mem_n[:, t, :], mem_tok[:, t, :], ACT.Square,
                                   accum_out=mem_ms[:, t:t + 1]).then_inc(mem_sq, 1)
                act.wait_ge(mem_sq, MC)
                rms_root(mem_root[:, :], mem_ms[:, :], D).then_inc(mem_root_s, 1)
                act.wait_ge(mem_inv, 1)
                for t in range(MC):
                    act.activation(mem_n[:, t, :], mem_tok[:, t, :], ACT.Copy,
                                   scale=mem_rinv[:, t:t + 1]).then_inc(mem_normed, 1)

                act.wait_ge(o_done, TC)
                for hd in range(GLA_H):
                    act.activation(tmp[:, hd, :], bank[hd][:, :], ACT.Square).then_inc(gsq, 1)
                act.wait_ge(gstat, 1)
                rms_root(g_root[:, :], bank[4][:, 0:GLA_H * TC], GLA_V).then_inc(groot, 1)
                for c in range(DC):
                    act.wait_ge(mem_turned, c // 2 + 1)
                    act.activation(mem_hi[:, c, :], bank[6 + c // 2 % 2][:, c % 2 * NMEM:(c % 2 + 1) * NMEM],
                                   ACT.Copy, scale=gains[:, G_KV + c:G_KV + c + 1]).then_inc(mem_h, 1)
                round_to(B_OUT + 2)
                for hd in range(GLA_H):
                    act.wait_ge(gout, hd + 1)
                    act.activation(xh[:, 4 + hd, :], tmp[:, hd, :], ACT.Copy).then_inc(y_h, 1)

            def mixer():
                for c in range(DC):
                    pre(1, c)
                    if c in (3, 5):
                        round_to(B_IN + 2 + (c - 1) // 2)
                pre_root(1)
                round_to(B_IN + 5)
                log_sigmoid((0,))
                round_to(B_IN + 6)
                in_evacuate(0)
                round_to(B_IN + 8)
                log_sigmoid((1, 2))
                act.wait_ge(cum_step, 3)
                for r in (0, 64):
                    act.activation(cum_hl[r:r + FOX_H, :], cum[:, :], ACT.Copy).then_inc(cum_hi, 1)
                round_to(B_IN + KB * 2 + 2)
                in_evacuate(1)
                round_to(B_IN + KB * 3)
                decays()
                round_to(B_IN + KB * 3 + 2)
                in_evacuate(2)
                attention(FOX_UNITS, 0, False)
                gla()
                round_to(B_KV)

            def memory():
                for g in range(4):
                    round_to(B_KV + KB * (g + 1) + 2)
                    for m in range(4 if g < 2 else MC):
                        b = bank[KV_BANK[g] + m]
                        act.wait_ge(w_used, B_KV + KB * (g + 1))
                        if g < 2:
                            act.activation(km_hi[:, 4 * g + m, :], b[:, 0:NMEM], ACT.Copy).then_inc(kv_h, 1)
                        else:
                            act.activation(vm_hi[:, m, (g - 2) * HW:(g - 1) * HW], b[:, :], ACT.Copy).then_inc(kv_h, 1)
                    pre(2, 2 * g)
                    pre(2, 2 * g + 1)
                round_to(B_MQ + KB)
                pre_root(2)
                for g in range(2):
                    round_to(B_MQ + KB * (g + 1) + 2)
                    for m in range(4):
                        act.wait_ge(mq_t, 4 * g + m + 1)
                        act.activation(qm_hi[:, 4 * g + m, :], tmp[:, m, :], ACT.Copy).then_inc(mq_h, 1)
                attention(MEM_UNITS, N_FOX, True)
                round_to(B_UP2)

            for r, name in enumerate(GAINS):
                act.dma_start(gain_rows[r * 8:r * 8 + 8, :],
                              a[name].rearrange("l (c p) -> (l c) p", p=P)).then_inc(gains_landed, 16)
            act.dma_start(gain_rows[G_BA:G_BA + 2, :],
                          a["mix_b_a"].rearrange("l (c p) -> (l c) p", p=P)).then_inc(gains_landed, 16)
            act.dma_start(gain_rows[G_GLA:G_GLA + 4, :],
                          a["mix_g_gla"].rearrange("l (c p) -> (l c) p", p=P)).then_inc(gains_landed, 16)
            act.preload_act_table(ACT.Sqrt)
            round_to(2)
            act.wait_ge(gains_ready, 1)
            swiglu(0, B_UP1, B_DOWN1)
            post_norm(0)
            mixer()
            post_norm(1)
            memory()
            post_norm(2)
            swiglu(3, B_UP2, B_DOWN2)
            post_norm(3)
            for t in range(TC):
                act.wait_ge(oturned, t + 1)
                act.activation(out_tok[:, t, 0:HW], bank[4 + t][:, :], ACT.Copy).then_inc(ocopied_a, 1)

        @block.vector
        def _(dve):
            def pre(s, c):
                g = G_PRE[s] + c
                dve.wait_ge(xh_ready, DC * s + c + 1)
                dve.scalar_tensor_tensor(out=xl[:, c, :], in0=h[:, c, :], scalar=gains[:, g:g + 1],
                                         in1=xh[:, c, :].bitcast(F32), op0=ALU.mult,
                                         op1=ALU.subtract).then_inc(xl_ready, 1)
                dve.wait_ge(hsq_ready, DC * s + c + 1)
                if c == 0:
                    if s:
                        dve.wait_ge(fstat, s)
                    dve.tensor_copy(acc[:, :], sq[:, 0, :]).then_inc(hacc_ready, 1)
                elif c < DC - 1:
                    dve.wait_ge(hacc_ready, (DC - 1) * s + c)
                    dve.tensor_tensor(acc[:, :], acc[:, :], sq[:, c % 2, :], ALU.add).then_inc(hacc_ready, 1)

            def pre_inv(s):
                dve.wait_ge(hroot, s + 1)
                dve.reciprocal(rinv_tok[:, :], root_tok[:, :]).then_inc(hinv, 1)
                dve.wait_ge(hrinv, s + 1)

            def post_norm(s):
                for m in range(DC):
                    dve.wait_ge(fsq_ready, DC * s + m + 1)
                    if m == 0:
                        dve.tensor_copy(f0, out_bank(s, 0)[:, :]).then_inc(f0_saved, 1)
                        dve.wait_ge(hstat, s + 1)
                        dve.tensor_copy(acc[:, :], sq[:, 0, :]).then_inc(facc_ready, 1)
                    elif m < DC - 1:
                        dve.wait_ge(facc_ready, (DC - 1) * s + m)
                        dve.tensor_tensor(acc[:, :], acc[:, :], sq[:, m % 2, :], ALU.add).then_inc(facc_ready, 1)
                dve.wait_ge(froot, s + 1)
                dve.reciprocal(rinv_tok[:, :], root_tok[:, :]).then_inc(finv, 1)
                dve.wait_ge(frinv, s + 1)

            def residual(s, m):
                src = f0 if m == 0 else out_bank(s, m)[:, :]
                dve.tensor_tensor(tmp[:, m % 2, :], src, rinv[:, :], ALU.mult).then_inc(f_scaled, 1)
                dve.wait_ge(f_scaled, DC * s + m + 1)
                dve.scalar_tensor_tensor(out=h[:, m, :], in0=tmp[:, m % 2, :], scalar=post[:, s, m:m + 1],
                                         in1=h[:, m, :], op0=ALU.mult, op1=ALU.add).then_inc(h_ready, 1)
                dve.wait_ge(h_ready, DC * (s + 1) + m + 1)

            def swiglu(s, up):
                first = 2 * FG * (s // 3)

                def group(g, i=None):
                    b = bank[4 * (g % 2):4 * (g % 2) + 4]
                    dve.wait_ge(w_used, at_turn(i, 2 * KB, up + KB * (g + 1)))
                    for pair in range(2):
                        n = first + 2 * g + pair
                        if n >= 2:
                            dve.wait_ge(midl_done, at_turn(i, 4, n - 1))
                        dve.tensor_tensor(tmp[:, pair, :], b[pair][:, :], rinv[:, :], ALU.mult).then_inc(gate_scaled, 1)
                        dve.tensor_tensor(tmp[:, 2 + pair, :], b[2 + pair][:, :], rinv[:, :],
                                          ALU.mult).then_inc(up_scaled, 1)
                    for pair in range(2):
                        n = first + 2 * g + pair
                        dve.wait_ge(silu_done, at_turn(i, 4, n + 1))
                        dve.wait_ge(up_scaled, at_turn(i, 4, n + 2))
                        dve.tensor_tensor(tmp[:, 2 + pair, :], tmp[:, pair, :], tmp[:, 2 + pair, :],
                                          ALU.mult).then_inc(mid_done, 1)
                    for pair in range(2):
                        n = first + 2 * g + pair
                        dve.wait_ge(midh_done, at_turn(i, 4, n + 1))
                        chunk = at_turn(i, 4, 2 * g + pair)
                        dve.tensor_tensor(mid_lo[:, bass.ds(chunk, 1), :], tmp[:, 2 + pair:3 + pair, :],
                                          mid_hi[:, bass.ds(chunk, 1), :].bitcast(F32),
                                          ALU.subtract).then_inc(midl_done, 1)

                pre_inv(s)
                group(0)
                if s == 0:
                    dve.wait_ge(small_landed, 16 * SMALL_LOADS)
                    for c in range(DC):
                        g = G_PRE[1] + c
                        dve.tensor_scalar(w_small_g[:, c, :], w_small[:, c, :], gains[:, g:g + 1], None,
                                          ALU.mult).then_inc(small_scaled, 1)
                with dve.Fori(0, FG // 2) as i:
                    for g in range(2):
                        group(1 + g, i)

            def attention(units, u0, mem):
                y0 = Y_GLA if mem else 0
                late = 2 if mem else 1
                for k in range(len(units) + late + 2):
                    if k < len(units):
                        u, w = u0 + k, key_width(mem, units[k][1])
                        r = slice(u % 4, u % 4 + 1)
                        dve.wait_ge(scored, u + 1)
                        dve.tensor_reduce(nmx[:, r], s_bank(mem, k)[:, 0:w], AX_X, ALU.max,
                                          negate=True).then_inc(maxed, 1)
                    if not mem:
                        if k == 0:
                            in_evacuate(2)
                    if 0 <= k - 1 < len(units):
                        u = u0 + k - 1
                        r = slice(u % 4, u % 4 + 1)
                        dve.wait_ge(expd, u + 1)
                        dve.reciprocal(rr[:, r], rs[:, r]).then_inc(rsum, 1)
                        dve.wait_ge(rsum, u + 1)
                        if u >= 2:
                            dve.wait_ge(pturned, u - 1)
                        dve.tensor_scalar(norm_diag[:, u % 2, :], ident[:, :], rr[:, r], None,
                                          ALU.mult).then_inc(normed, 1)
                    if 0 <= k - late < len(units):
                        i = units[k - late][1]
                        nk = key_width(mem, i) // P
                        dve.wait_ge(pt_h, u0 + k - late + 1)
                        dve.tensor_tensor(pt_lo[:, 0:nk, i * P:(i + 1) * P],
                                          p_bank(mem, k)[:, 0:nk * P].rearrange("p (j n) -> p j n", n=P),
                                          pt_hi[:, 0:nk, i * P:(i + 1) * P].bitcast(F32),
                                          ALU.subtract).then_inc(pt_l, 1)
                    done = k - late - 2 if mem else k - late - 1
                    if 0 <= done < len(units) and units[done][1] == TC - 1:
                        hd = units[done][0]
                        for e in range(2 if mem else 1):
                            y_hi, y_lo, c = (xh, xl, 2 * hd + e) if mem else (fox_hi, fox_lo, hd // 2)
                            r = slice(0, P) if mem else slice(FOX_D * (hd % 2), FOX_D * (hd % 2 + 1))
                            dve.wait_ge(y_h, y0 + (2 * hd + e if mem else hd) + 1)
                            dve.tensor_tensor(y_lo[r, c, :], o_bank(mem, hd, e)[r, :], y_hi[r, c, :].bitcast(F32),
                                              ALU.subtract).then_inc(y_l, 1)
                    if not mem:
                        if k == FILL_END[0]:
                            in_evacuate(3)
                        elif 0 < k - FILL_END[0] <= 3:
                            decayed(k - FILL_END[0] - 1)

            def gates():
                for j in range(2):
                    dve.wait_ge(ga_done, j + 1)
                    dve.tensor_scalar(gb[:, j, :], bank[6 + j][:, :], gains[:, G_BA + j:G_BA + j + 1], None,
                                      ALU.add).then_inc(z_ready, 1)
                    dve.wait_ge(z_ready, 2 + j)
                    dve.tensor_scalar(ls_min[:, j, :], gb[:, j, :], 0.0, None, ALU.min).then_inc(z_min, 1)
                for j in range(2):
                    dve.wait_ge(ls_act, 8 + j)
                    dve.wait_ge(z_min, 2 + j)
                    dve.tensor_tensor(ls_min[:, j, :], ls_min[:, j, :], ls_abs[:, 1 + j, :],
                                      ALU.subtract).then_inc(gcum_step, 1)
                    dve.wait_ge(gcum_step, 2 * j + 1)
                    dve.tensor_tensor_scan(gb[:, j, :], reset[:, :], ls_min[:, j, :], 0.0,
                                           ALU.mult, ALU.add).then_inc(gcum_step, 1)
                dve.wait_ge(gcum_step, 4)
                b = gb[:, :, :].rearrange("p k (n c) -> p (k n) c", c=CHUNK)
                dve.tensor_tensor(gke[:, :, :].rearrange("p k (n c) -> p (k n) c", c=CHUNK),
                                  b[:, :, CHUNK - 1:CHUNK].to_broadcast([P, 2 * NCH, CHUNK]), b,
                                  ALU.subtract).then_inc(gcum_step, 1)

            def forget():
                dve.wait_ge(ls_act, 3)
                dve.wait_ge(z_min, 1)
                dve.tensor_tensor(cum[:, :], cum[:, :], ls_abs[0:FOX_H, 0, :], ALU.subtract).then_inc(cum_step, 1)
                dve.wait_ge(cum_step, 2)
                dve.tensor_tensor_scan(cum[:, :], ones[0:FOX_H, 0:1].to_broadcast([FOX_H, SEQ]), cum[:, :], 0.0,
                                       ALU.mult, ALU.add).then_inc(cum_step, 1)

            def in_evacuate(g):
                b = bank[IN_BANK[g]:IN_BANK[g] + 4]
                dve.wait_ge(w_used, B_IN + KB * (g + 1))
                if g in (0, 1, 3, 5):
                    scale = {0: FOX_D ** -0.5, 3: GLA_K ** -0.5}
                    for m in range(4):
                        if g == 1:
                            dve.wait_ge(in_lo, m + 1)
                        elif g == 3:
                            dve.wait_ge(in_lo, 4 + m + 1)
                        elif g == 5:
                            dve.wait_ge(gdec, 3)
                        dve.scalar_tensor_tensor(out=tmp[:, m, :], in0=b[m][:, :],
                                                 scalar=scale[g] if g in scale and m < 2 or g == 0 else 1.0,
                                                 in1=rinv[:, :], op0=ALU.mult, op1=ALU.mult).then_inc(in_tmp, 1)
                for m in range(4):
                    if g < 2:
                        hi, lo = ((q_hi, q_lo), (k_hi, k_lo))[g]
                        dve.wait_ge(in_hi, 4 * g + m + 1)
                        dve.tensor_tensor(lo[:, m, :], tmp[:, m, :], hi[:, m, :].bitcast(F32),
                                          ALU.subtract).then_inc(in_lo, 1)
                    elif g == 2:
                        dve.wait_ge(in_hi, 8 + m + 1)
                        dve.scalar_tensor_tensor(out=v_lo[:, m, :], in0=b[m][:, :], scalar=rinv_tok[:, m:m + 1],
                                                 in1=v_hi[:, m, :].bitcast(F32), op0=ALU.mult,
                                                 op1=ALU.subtract).then_inc(in_lo, 1)

            def decayed(j):
                dst, src = ((gq, 0), (gke, 2), (gk, 2))[j]
                dve.wait_ge(exps, 4)
                dve.wait_ge(in_tmp, 8 + src + 2)
                dve.tensor_tensor(dst[:, :, :], tmp[:, src:src + 2, :], dst[:, :, :], ALU.mult).then_inc(gdec, 1)

            def gla():
                def mask(m):
                    dve.wait_ge(at_done, m + 1)
                    if m >= 2:
                        dve.wait_ge(o_done, m - 1)
                    for e in range(2):
                        dve.tensor_tensor(at_sb[:, m % 2, :].rearrange("p (c e i) -> p c e i", e=2, i=P)[:, :, e, :],
                                          bank[4 + e][:, 0:2 * P].rearrange("p (c i) -> p c i", i=P),
                                          gla_mask[:, :].rearrange("p (o i) -> p o i", o=1).to_broadcast([P, 2, P]),
                                          ALU.mult).then_inc(at_masked, 1)

                def step(n):
                    dve.wait_ge(sc_done, n + 1)
                    b = bank[6 + n % 2]
                    if n == 0:
                        dve.tensor_copy(state[:, 0, :], b[:, :]).then_inc(st_ready, 1)
                        return
                    dve.wait_ge(st_ready, 2 * n - 1)
                    for c in range(2):
                        half = slice(256 * c, 256 * c + 256)
                        dve.scalar_tensor_tensor(out=state[:, n, half], in0=state[:, n - 1, half],
                                                 scalar=decay[:, c, n:n + 1], in1=b[:, half],
                                                 op0=ALU.mult, op1=ALU.add).then_inc(st_ready, 1)

                mask(0)
                step(0)
                for m in range(1, TC):
                    mask(m)
                    step(2 * m - 1)
                    step(2 * m)
                dve.wait_ge(mem_root_s, 1)
                dve.reciprocal(mem_rinv[:, :], mem_root[:, :]).then_inc(mem_inv, 1)

                def mem_lo_chunk(c):
                    dve.wait_ge(mem_h, c // 2 * 2 + 2)
                    dve.scalar_tensor_tensor(out=mem_lo[:, c, :],
                                             in0=bank[6 + c // 2 % 2][:, c % 2 * NMEM:(c % 2 + 1) * NMEM],
                                             scalar=gains[:, G_KV + c:G_KV + c + 1],
                                             in1=mem_hi[:, c, :].bitcast(F32), op0=ALU.mult,
                                             op1=ALU.subtract).then_inc(mem_l, 1)

                def factor(hd):
                    dve.wait_ge(gspread, hd + 1)
                    dve.scalar_tensor_tensor(out=tmp[:, hd, :], in0=bank[5 - hd % 2][:, :],
                                             scalar=gains[:, G_GLA + hd:G_GLA + hd + 1], in1=gr[:, hd, :],
                                             op0=ALU.mult, op1=ALU.mult).then_inc(gfactor, 1)

                dve.wait_ge(groot, 1)
                dve.reciprocal(g_rinv[:, :], g_root[:, :]).then_inc(ginv, 1)
                factor(0)
                factor(1)
                for c in range(4):
                    mem_lo_chunk(c)
                factor(2)
                factor(3)
                for c in range(4, DC):
                    mem_lo_chunk(c)
                for hd in range(GLA_H):
                    dve.wait_ge(gfactor, hd + 1)
                    dve.tensor_tensor(tmp[:, hd, :], bank[hd][:, :], tmp[:, hd, :], ALU.mult).then_inc(gout, 1)
                for hd in range(GLA_H):
                    dve.wait_ge(y_h, Y_FOX + hd + 1)
                    dve.tensor_tensor(xl[:, 4 + hd, :], tmp[:, hd, :], xh[:, 4 + hd, :].bitcast(F32),
                                      ALU.subtract).then_inc(y_l, 1)

            def mixer():
                residual(0, 0)
                for c in range(1, DC):
                    residual(0, c)
                    pre(1, c - 1)
                pre(1, DC - 1)
                pre_inv(1)
                dve.wait_ge(small_done, 1)
                dve.tensor_tensor(zg[:, :], bank[SMALL_BANK][0:48, :], rinv[0:48, :], ALU.mult).then_inc(z_ready, 1)
                dve.memset(cum_hl[:, :].bitcast(F32), 0.0).then_inc(cum_step, 1)
                dve.wait_ge(z_ready, 1)
                dve.tensor_scalar(cum[:, :], zg[0:FOX_H, :], b_f[:, 0:1], 0.0, ALU.add, ALU.min).then_inc(z_min, 1)
                in_evacuate(0)
                forget()
                gates()
                dve.wait_ge(cum_hi, 2)
                for r in (32, 96):
                    dve.tensor_tensor(cum_hl[r:r + FOX_H, :], cum[:, :], cum_hl[0:FOX_H, :].bitcast(F32),
                                      ALU.subtract).then_inc(cum_lo, 1)
                in_evacuate(1)
                attention(FOX_UNITS, 0, False)
                in_evacuate(5)
                gla()

            def memory():
                for c in range(DC):
                    residual(1, c)
                for g in range(4):
                    for m in range(4 if g < 2 else MC):
                        b = bank[KV_BANK[g] + m]
                        if g < 2:
                            dve.wait_ge(kv_h, 4 * g + m + 1)
                            dve.tensor_tensor(km_lo[:, 4 * g + m, :], b[:, 0:NMEM],
                                              km_hi[:, 4 * g + m, :].bitcast(F32), ALU.subtract).then_inc(kv_l, 1)
                        else:
                            cols = slice((g - 2) * HW, (g - 1) * HW)
                            dve.wait_ge(kv_h, 8 + MC * (g - 2) + m + 1)
                            dve.tensor_tensor(vm_lo[:, m, cols], b[:, :], vm_hi[:, m, cols].bitcast(F32),
                                              ALU.subtract).then_inc(kv_l, 1)
                    pre(2, 2 * g)
                    pre(2, 2 * g + 1)
                pre_inv(2)
                for g in range(2):
                    dve.wait_ge(w_used, B_MQ + KB * (g + 1))
                    for m in range(4):
                        if g:
                            dve.wait_ge(mq_l, m + 1)
                        dve.scalar_tensor_tensor(out=tmp[:, m, :], in0=bank[MQ_BANK[g] + m][:, :],
                                                 scalar=MEM_D ** -0.5, in1=rinv[:, :],
                                                 op0=ALU.mult, op1=ALU.mult).then_inc(mq_t, 1)
                    for m in range(4):
                        j = 4 * g + m
                        dve.wait_ge(mq_h, j + 1)
                        dve.tensor_tensor(qm_lo[:, j, :], tmp[:, m, :], qm_hi[:, j, :].bitcast(F32),
                                          ALU.subtract).then_inc(mq_l, 1)
                attention(MEM_UNITS, N_FOX, True)

            dve.wait_ge(gains_turned, 1)
            dve.tensor_copy(gains[:, :], bank[7][:, 0:G_ROWS]).then_inc(gains_ready, 1)
            dve.wait_ge(gains_ready, 1)
            for s in range(SUBLAYERS):
                dve.tensor_scalar(post[:, s, :], gains[:, G_POST[s]:G_POST[s] + DC], POST_SCALE[s], None,
                                  ALU.mult).then_inc(gains_ready if s else up_scaled, 1)
            for c in range(DC):
                dve.wait_ge(turned, c + 1)
                dve.tensor_copy(h[:, c, :], bank[c][:, :]).then_inc(h_ready, 1)
                dve.wait_ge(h_ready, c + 1)
                if c:
                    pre(0, c - 1)
            pre(0, DC - 1)
            swiglu(0, B_UP1)
            post_norm(0)
            mixer()
            post_norm(1)
            memory()
            post_norm(2)
            residual(2, 0)
            for c in range(1, DC):
                residual(2, c)
                pre(3, c - 1)
            pre(3, DC - 1)
            swiglu(3, B_UP2)
            post_norm(3)
            for c in range(DC):
                residual(3, c)
            for t in range(TC):
                dve.wait_ge(oturned, TC + t + 1)
                dve.tensor_copy(out_tok[:, t, HW:D], bank[t][:, :]).then_inc(ocopied_v, 1)

        @block.tensor
        def _(pe):
            def three(dst, w, x, start, stop, loose=False):
                pe.matmul(dst, w[0], x[0], start=start, stop=False, skip_group_check=loose)
                pe.matmul(dst, w[0], x[1], start=False, stop=False, skip_group_check=loose)
                return pe.matmul(dst, w[1], x[0], start=False, stop=stop, skip_group_check=loose)

            def token_sums(dst):
                for t in range(TC):
                    tok = slice(t * P, (t + 1) * P)
                    pe.matmul(dst[:, t:t + 1], acc[:, tok], ones[:, 0:1], start=True, stop=False)
                    last = pe.matmul(dst[:, t:t + 1], sq[:, (DC - 1) % 2, tok], ones[:, 0:1], start=False, stop=True)
                return last

            def spread(dst, src):
                for t in range(TC):
                    last = pe.matmul(dst[:, t * P:(t + 1) * P], src[:, t:t + 1].to_broadcast([P, P]), ident[:, :],
                                     start=True, stop=True)
                return last

            def closing_block(s, n, b0, also=None):
                group_block(n, KB - 1, b0, (xh, xl), s=s, quarters=(0, 1, 2))
                pe.wait_ge(hacc_ready, (DC - 1) * (s + 1))
                pe.wait_ge(hsq_ready, DC * (s + 1))
                token_sums(bank[STAT_BANK[s]]).then_inc(hstat, 1)
                group_block(n, KB - 1, b0, (xh, xl), quarters=(3,))
                if also:
                    also()
                pe.wait_ge(hinv, s + 1)
                spread(bank[STAT_BANK[s]], rinv_tok).then_inc(hspread, 1)

            def out_stat(s):
                pe.wait_ge(facc_ready, (DC - 1) * (s + 1))
                pe.wait_ge(fsq_ready, DC * (s + 1))
                pe.wait_ge(f0_saved, s + 1)
                token_sums(out_bank(s, 0)).then_inc(fstat, 1)
                pe.wait_ge(finv, s + 1)
                spread(out_bank(s, 0), rinv_tok).then_inc(fspread, 1)

            def weights(n, i=None, step=0):
                pe.wait_ge(lo_ready, at_turn(i, step, n + 1))
                return w_hi[:, n % SPLIT, :], w_lo[:, n % SPLIT, :]

            def group_block(n, k, b0, x, width=SEQ, s=None, i=None, step=0, quarters=range(4)):
                w = weights(n, i, step)
                for q in quarters:
                    c = 2 * k + q // 2
                    if s is not None and q % 2 == 0:
                        pe.wait_ge(xl_ready, DC * s + c + 1)
                    for m in (q % 2 * 2, q % 2 * 2 + 1):
                        cols = slice((c % 2 * 4 + m) * P, (c % 2 * 4 + m + 1) * P)
                        last = three(bank[b0 + m][:, 0:width], (w[0][:, cols], w[1][:, cols]),
                                     (x[0][:, c, :], x[1][:, c, :]), c == 0, c == DC - 1)
                if 3 in quarters:
                    last.then_inc(w_used, 1)

            def token_block(n, k, b0, x, tokens, quarters=range(4)):
                w = weights(n)
                for q in quarters:
                    c = 2 * k + q // 2
                    cols = slice(c % 2 * HW, (c % 2 + 1) * HW)
                    for t in range(q % 2 * tokens // 2, (q % 2 + 1) * tokens // 2):
                        tok = slice(t * P, (t + 1) * P)
                        last = three(bank[b0 + t][:, :], (x[0][:, c, tok], x[1][:, c, tok]),
                                     (w[0][:, cols], w[1][:, cols]), c == 0, c == DC - 1)
                if 3 in quarters:
                    last.then_inc(w_used, 1)

            def out_block(s, n, x, first, end, i=None, step=0, free={}):
                w = weights(n, i, step)
                for m in range(DC):
                    if m in free:
                        pe.wait_ge(*free[m])
                    cols = slice(m * P, (m + 1) * P)
                    last = three(out_bank(s, m)[:, :], (w[0][:, cols], w[1][:, cols]), x, first, end, True)
                    if end and m < DC - 1:
                        last.then_inc(out_done, 1)
                last.then_inc(w_used, 1)

            def swiglu(s, up, down):
                first = 2 * FG * (s // 3)
                if s:
                    pe.wait_ge(f_scaled, DC * s - 4)
                for k in range(KB - 1):
                    group_block(up + k, k, 0, (xh, xl), s=s)
                closing_block(s, up + KB - 1, 0)
                with pe.Fori(0, FG // 2) as i:
                    for g in range(2):
                        pe.wait_ge(up_scaled, at_turn(i, 4, first + 2 * g + 1))
                        for k in range(KB):
                            parts = range(4)
                            if g == k == 0:
                                group_block(up + KB, 0, 4, (xh, xl), i=i, step=2 * KB, quarters=(0,))
                                pe.wait_ge(hrinv, s + 1)
                                parts = (1, 2, 3)
                            group_block(up + KB * (1 + g) + k, k, 4 * ((1 + g) % 2), (xh, xl),
                                        i=i, step=2 * KB, quarters=parts)
                def hidden(c):
                    return [t[:, bass.ds(c, 1), :].rearrange("p o n -> p (o n)") for t in (mid_hi, mid_lo)]

                pe.wait_ge(up_scaled, first + 2 * FG - 1)
                pe.wait_ge(midl_done, first + 1)
                out_block(s, down, hidden(0), True, False, free={4: (up_scaled, first + 2 * FG + 1)})
                with pe.Fori(0, (FC - 2) // 4) as i:
                    for k in range(4):
                        pe.wait_ge(midl_done, at_turn(i, 4, first + 2 + k))
                        out_block(s, down + 1 + k, hidden(at_turn(i, 4, 1 + k)), False, False, i, 4)
                pe.wait_ge(midl_done, first + FC)
                out_block(s, down + FC - 1, hidden(FC - 1), False, True)
                out_stat(s)

            def fill(turn):
                for q in range(sum(FILL[:turn]), sum(FILL[:turn + 1])):
                    g, q = FILL_GROUPS[q // FILL_GROUP], q % FILL_GROUP
                    if q == 0:
                        pe.wait_ge(*{3: (in_lo, 12), 4: (in_tmp, 12), 5: (in_hi, 16)}[g])
                    n = B_IN + KB * g + q // 4
                    if g == 4:
                        token_block(n, q // 4, IN_BANK[g], (xh, xl), TC, quarters=(q % 4,))
                    else:
                        group_block(n, q // 4, IN_BANK[g], (xh, xl), quarters=(q % 4,))

            def attention(units, u0, mem):
                y0 = Y_GLA if mem else 0
                late, depth = (2, 3) if mem else (1, 2)

                def scores(k):
                    hd, i = units[k]
                    w = key_width(mem, i)
                    if k >= depth:
                        pe.wait_ge(expd, u0 + k - depth + 1)
                    dst, tok = s_bank(mem, k)[:, 0:w], slice(i * P, (i + 1) * P)
                    if mem:
                        for e in range(2):
                            c = 2 * hd + e
                            last = three(dst, (qm_hi[:, c, tok], qm_lo[:, c, tok]),
                                         (km_hi[:, c, :], km_lo[:, c, :]), e == 0, e == 1)
                    else:
                        r, c = slice(FOX_D * (hd % 2), FOX_D * (hd % 2 + 1)), hd // 2
                        three(dst, (q_hi[r, c, tok], q_lo[r, c, tok]), (k_hi[r, c, 0:w], k_lo[r, c, 0:w]),
                              True, False)
                        pe.matmul(dst[:, w - P:w], ident_r[:, :], causal[:, :], start=False, stop=False,
                                  skip_group_check=True)
                        last = pe.matmul(dst, sel[r, hd, :], cum_hl[r, 0:w], start=False, stop=True)
                    last.then_inc(scored, 1)

                def turn(k):
                    u, nk = u0 + k, key_width(mem, units[k][1]) // P
                    pe.wait_ge(normed, u + 1)
                    if k >= late:
                        pe.wait_ge(pt_l, u - late + 1)
                    for j in range(nk):
                        last = pe.matmul(p_bank(mem, k)[:, j * P:(j + 1) * P], prob[:, u % 2, j * P:(j + 1) * P],
                                         norm_diag[:, u % 2, :], start=True, stop=True)
                    last.then_inc(pturned, 1)

                def output(k):
                    hd = units[k][0]
                    pe.wait_ge(pt_l, u0 + k + 1)
                    for e in range(2 if mem else 1):
                        idx = 2 * hd + e if mem else hd
                        if idx >= (3 if mem else 1):
                            pe.wait_ge(y_l, y0 + idx + 1 - (3 if mem else 1))
                        for j in range(MC if mem else TC):
                            v, c = ((vm_hi, vm_lo), 2 * hd + e) if mem else ((v_hi, v_lo), hd // 2)
                            q0 = 0 if mem else j * P
                            last = three(o_bank(mem, hd, e)[:, q0:SEQ],
                                         (v[0][:, j, c * P:(c + 1) * P], v[1][:, j, c * P:(c + 1) * P]),
                                         (pt_hi[:, j, q0:SEQ], pt_lo[:, j, q0:SEQ]),
                                         j == 0, j == (MC if mem else TC) - 1, True)
                        last.then_inc(pv_done, 1)

                for k in range(len(units) + late + 1):
                    if k < len(units):
                        scores(k)
                    if not mem:
                        fill(k)
                    if 0 <= k - late - 1 < len(units) and units[k - late - 1][1] == TC - 1:
                        output(k - late - 1)
                    if 0 <= k - late < len(units):
                        turn(k - late)

            def gla():
                def head(hd):
                    e = hd % 2
                    return hd // 2, slice(GLA_K * e, GLA_K * (e + 1)), slice(GLA_V * hd, GLA_V * (hd + 1))

                def scores(m):
                    if m:
                        pe.wait_ge(at_masked, 2 * m)
                    else:
                        pe.wait_ge(in_tmp, 16)
                    tok = slice(m * P, (m + 1) * P)
                    for hd in range(GLA_H):
                        c, r, cols = head(hd)
                        last = pe.matmul(bank[4 + hd % 2][:, c * P:(c + 1) * P], gk[r, c, tok], gq[r, c, tok],
                                         start=True, stop=True)
                    last.then_inc(at_done, 1)

                def chunk_state(n):
                    if n >= 2:
                        pe.wait_ge(st_ready, 2 * n - 3)
                    m, r = n // 2, slice(CHUNK * (n % 2), CHUNK * (n % 2 + 1))
                    for c in range(2):
                        cols = slice(2 * GLA_V * c, 2 * GLA_V * (c + 1))
                        last = pe.matmul(bank[6 + n % 2][:, cols], ke_tok[r, m, c, :], gv[r, m, cols],
                                         start=True, stop=True)
                    last.then_inc(sc_done, 1)

                def outputs(m):
                    pe.wait_ge(at_masked, 2 * m + 2)
                    pe.wait_ge(st_ready, 4 * m + 1)
                    for hd in range(GLA_H):
                        c, r, cols = head(hd)
                        last = pe.matmul(bank[hd][:, m * P:(m + 1) * P], gv[:, m, cols],
                                         at_sb[:, m % 2, cols], start=True, stop=False, skip_group_check=True)
                        for n in (2 * m, 2 * m + 1):
                            if n:
                                tok = slice(n * CHUNK, (n + 1) * CHUNK)
                                last = pe.matmul(bank[hd][:, tok], state[r, n - 1, cols], gq[r, c, tok],
                                                 start=False, stop=n % 2 == 1, skip_group_check=True)
                    last.then_inc(o_done, 1)

                pe.wait_ge(gdec, 3)
                pe.wait_ge(expd, N_FOX)
                for t in range(2):
                    for j in range(4):
                        m, c = 2 * t + j // 2, j % 2
                        last = pe.transpose(bank[t][:, j * P:(j + 1) * P], gke[:, c, m * P:(m + 1) * P],
                                            ident[:, :])
                    last.then_inc(ke_turned, 1)
                scores(0)
                pe.wait_ge(ke_saved, 2)
                pe.wait_ge(y_l, Y_FOX)
                chunk_state(0)
                for m in range(TC):
                    if m + 1 < TC:
                        scores(m + 1)
                        chunk_state(2 * m + 1)
                        chunk_state(2 * m + 2)
                    outputs(m)

                def mem_turn(half):
                    if half == 0:
                        pe.wait_ge(st_ready, 2 * (NCH - 1) - 1)
                        pe.wait_ge(mem_normed, MC)
                    else:
                        pe.wait_ge(mem_l, 4)
                    for j in range(8):
                        c, t = 4 * half + j // 2, j % 2
                        col = c % 2 * NMEM + t * P
                        last = pe.transpose(bank[6 + c // 2 % 2][:, col:col + P], mem_n[:, t, c * P:(c + 1) * P],
                                            ident[:, :])
                        if j % 4 == 3:
                            last.then_inc(mem_turned, 1)

                mem_turn(0)
                for hd in range(GLA_H):
                    pe.wait_ge(gsq, hd + 1)
                    for t in range(TC):
                        last = pe.matmul(bank[4][:, hd * TC + t:hd * TC + t + 1], tmp[:, hd, t * P:(t + 1) * P],
                                         ones[:, 0:1], start=True, stop=True)
                last.then_inc(gstat, 1)
                pe.wait_ge(ginv, 1)
                for hd in range(GLA_H):
                    if hd >= 2:
                        pe.wait_ge(gfactor, hd - 1)
                    spread(bank[5 - hd % 2], g_rinv[:, hd * TC:(hd + 1) * TC]).then_inc(gspread, 1)
                    if hd == 1:
                        mem_turn(1)

            def mixer():
                pe.wait_ge(f_scaled, 4)
                def small_columns():
                    pe.wait_ge(small_scaled, DC)
                    for c in range(DC):
                        last = pe.matmul(bank[SMALL_BANK][0:48, :], w_small_g[:, c, :], h[:, c, :],
                                         start=c == 0, stop=c == DC - 1)
                    last.then_inc(small_done, 1)

                for k in range(KB - 1):
                    group_block(B_IN + k, k, IN_BANK[0], (xh, xl), s=1)
                closing_block(1, B_IN + KB - 1, IN_BANK[0], small_columns)
                for g in (1, 2):
                    if g == 2:
                        pe.wait_ge(z_ready, 3)
                    for k in range(KB):
                        n = B_IN + KB * g + k
                        if g == 2:
                            token_block(n, k, IN_BANK[g], (xh, xl), TC)
                        elif k == 0:
                            group_block(n, k, IN_BANK[g], (xh, xl), quarters=(0, 2))
                            pe.wait_ge(hrinv, 2)
                            pe.wait_ge(z_ready, 1)
                            group_block(n, k, IN_BANK[g], (xh, xl), quarters=(1, 3))
                        else:
                            group_block(n, k, IN_BANK[g], (xh, xl))
                        if g == 1 and k == 1:
                            pe.wait_ge(in_tmp, 4)
                            for j in range(2):
                                pe.matmul(bank[6 + j][:, :], w_a2[32:48, j * P:(j + 1) * P], zg[32:48, :],
                                          start=True, stop=True).then_inc(ga_done, 1)
                pe.wait_ge(in_lo, 8)
                pe.wait_ge(cum_lo, 2)
                pe.wait_ge(sel_ready, 3)
                attention(FOX_UNITS, 0, False)
                gla()
                free = {0: (gfactor, GLA_H), 2: (mem_l, DC), 4: (gout, 1), 5: (gout, 2), 6: (gout, 3), 7: (gout, 4)}
                for c in range(DC):
                    pe.wait_ge(y_l, Y_FOX if c < 4 else Y_FOX + c - 3)
                    y = (fox_hi, fox_lo) if c < 4 else (xh, xl)
                    out_block(1, B_OUT + c, (y[0][:, c, :], y[1][:, c, :]), c == 0, c == DC - 1,
                              free={} if c else free)
                out_stat(1)

            def memory():
                free = ((f_scaled, DC + 4), (f_scaled, 2 * DC), (kv_l, 4), (kv_l, 8))
                for g in range(4):
                    pe.wait_ge(*free[g])
                    for k in range(KB):
                        n = B_KV + KB * g + k
                        if g < 2:
                            group_block(n, k, KV_BANK[g], (mem_hi, mem_lo), NMEM)
                        else:
                            token_block(n, k, KV_BANK[g], (mem_hi, mem_lo), MC)
                pe.wait_ge(kv_l, 10)
                for k in range(KB - 1):
                    group_block(B_MQ + k, k, MQ_BANK[0], (xh, xl), s=2)
                pe.wait_ge(kv_l, 12)
                closing_block(2, B_MQ + KB - 1, MQ_BANK[0])
                for k in range(KB):
                    group_block(B_MQ + KB + k, k, MQ_BANK[1], (xh, xl), quarters=(0, 2))
                    pe.wait_ge(hrinv, 3)
                    group_block(B_MQ + KB + k, k, MQ_BANK[1], (xh, xl), quarters=(1, 3))
                pe.wait_ge(mq_l, DC)
                attention(MEM_UNITS, N_FOX, True)
                pe.wait_ge(y_l, Y_GLA + DC)
                for c in range(DC):
                    out_block(2, B_MO + c, (xh[:, c, :], xl[:, c, :]), c == 0, c == DC - 1)
                out_stat(2)

            pe.wait_ge(consts, 5)
            pe.wait_ge(gains_landed, 16 * GAIN_LOADS)
            pe.transpose(bank[7][:, 0:G_ROWS], gain_rows[:, :], ident[0:G_ROWS, 0:G_ROWS]).then_inc(gains_turned, 1)
            pe.wait_ge(x_landed, 16 * TC)
            for c in range(DC):
                if c == DC - 1:
                    pe.wait_ge(gains_ready, 1)
                for t in range(TC):
                    last = pe.transpose(bank[c][:, t * P:(t + 1) * P], x_tok[:, t, c * P:(c + 1) * P], ident[:, :])
                last.then_inc(turned, 1)
            pe.wait_ge(h_ready, 4)
            swiglu(0, B_UP1, B_DOWN1)
            mixer()
            memory()
            swiglu(3, B_UP2, B_DOWN2)
            for half in range(2):
                pe.wait_ge(h_ready, DC * SUBLAYERS + 4 * (half + 1))
                for t in range(TC):
                    for j in range(4):
                        last = pe.transpose(bank[4 * (1 - half) + t][:, j * P:(j + 1) * P],
                                            h[:, 4 * half + j, t * P:(t + 1) * P], ident[:, :])
                    last.then_inc(oturned, 1)


_INS = ("x", "mem", "ffn1_g_pre", "ffn1_w_gu", "ffn1_w_down", "ffn1_g_post", "mix_g_pre", "mix_w_in",
        "mix_w_a2", "mix_b_a", "mix_b_f", "mix_g_gla", "mix_w_out", "mix_g_post", "mem_g_pre",
        "mem_g_kv", "mem_w_q", "mem_w_kv", "mem_w_o", "mem_g_post", "ffn2_g_pre", "ffn2_w_gu",
        "ffn2_w_down", "ffn2_g_post")


def kernel(**inputs):
    import numpy as _np
    import concourse.bacc as _bacc
    from concourse import mybir as _mybir
    from concourse.bass_utils import run_bass_kernel_spmd as _run

    nc = _bacc.Bacc("TRN2", target_bir_lowering=False, num_devices=1)
    arrays, args = {}, {}
    for name in _INS:
        array = _np.ascontiguousarray(inputs[name])
        arrays[f"in_{name}"] = array
        args[name] = nc.dram_tensor(f"in_{name}", array.shape, _mybir.dt.from_np(array.dtype),
                                    kind="ExternalInput").ap()
    out = nc.dram_tensor("out", (1, SEQ, D), _mybir.dt.float32, kind="ExternalOutput").ap()
    build(nc, args, out)
    r = _run(nc, [arrays], core_ids=[0])
    return r.results[0]["out"]
```

```python
from contextlib import ExitStack

import concourse.bass as bass
from concourse import mybir

F32 = mybir.dt.float32
F32R = mybir.dt.float32r
ALU = mybir.AluOpType
ACT = mybir.ActivationFunctionType
AX_X = mybir.AxisListType.X

P = 128
SEQ = 512
D = 1024
DC = D // P
TC = SEQ // P
FF = 2816
FC = FF // P
FG = FC // 2
NMEM = 256
MC = NMEM // P
FOX_H, FOX_D = 8, 64
GLA_H, GLA_K, GLA_V, CHUNK, RANK = 4, 64, 128, 64, 16
NCH = SEQ // CHUNK
MEM_H, MEM_D = 4, 256
FOX_W, GLA_KW, GLA_VW = FOX_H * FOX_D, GLA_H * GLA_K, GLA_H * GLA_V
COL_FQ, COL_FK, COL_FV = 0, FOX_W, 2 * FOX_W
COL_FZ = 3 * FOX_W
COL_GQ = COL_FZ + FOX_H
COL_GV = COL_GQ + 2 * GLA_KW
COL_GR = COL_GV + GLA_VW
COL_GA = COL_GR + GLA_VW
EPS = 1e-6
WARM_UP = 8
SUM_ROWS = P // GLA_H
TAU = 16.0
NEG = -1e30
SUBLAYERS = 4
FSQ = 5
BW = 1024
HW = BW // 2
RAW, SPLIT = 4, 2
LAND = 32

KB = DC // 2
B_UP1 = 0
B_DOWN1 = B_UP1 + FG * KB
B_IN = B_DOWN1 + FC
IN_COLS = (COL_FQ, COL_FK, COL_FV, COL_GQ, COL_GV, COL_GR)
B_OUT = B_IN + len(IN_COLS) * KB
B_KV = B_OUT + DC
MEM_BLOCKS = [("k", g, k) for g in range(2) for k in range(KB)]
MEM_BLOCKS += [block for k in range(2) for block in (("v", 0, k), ("v", 1, k), ("q", 0, k))]
MEM_BLOCKS += [("v", g, k) for k in (2, 3) for g in range(2)] + [("q", 0, 2), ("q", 0, 3)]
MEM_BLOCKS += [("q", 1, k) for k in range(KB)]
B_MO = B_KV + len(MEM_BLOCKS)
HALVED = range(B_KV, B_MO - KB)
B_UP2 = B_MO + DC
B_DOWN2 = B_UP2 + FG * KB
B_END = B_DOWN2 + FC
OUT_FIRST = (B_DOWN1, B_OUT, B_MO, B_DOWN2)
OUT_END = (B_IN, B_KV, B_UP2, B_END)

GAINS = ("ffn1_g_pre", "ffn1_g_post", "mix_g_pre", "mix_g_post", "mem_g_pre", "mem_g_kv",
         "mem_g_post", "ffn2_g_pre", "ffn2_g_post")
G_PRE = (0, 16, 32, 56)
G_POST = (8, 24, 48, 64)
G_KV = 40
G_BA = 72
G_GLA = 74
G_ROWS = 78
POST_SCALE = (0.5, 1.0, 1.0, 0.5)
GAIN_LOADS, SMALL_LOADS = len(GAINS) + 2, 4

OUT_OFF = (4, 4, 0, 4)
STAT_BANK = (6, 2, 4, 6)
SMALL_BANK = 3
IN_BANK = (4, 0, 4, 4, 4, 4)
KV_BANK = {("k", 0): 4, ("k", 1): 0, ("v", 0): 4, ("v", 1): 6}
MQ_BANK = (0, 4)

FOX_UNITS = [(hd, i) for hd in range(FOX_H) for i in range(TC)]
MEM_UNITS = [(hd, i) for hd in range(MEM_H) for i in range(TC)]
N_FOX = len(FOX_UNITS)
FOX, MEM_A, MEM_B = range(3)
HALF_MEM = len(MEM_UNITS) // 2
UNITS = (FOX_UNITS, MEM_UNITS[:HALF_MEM], MEM_UNITS[HALF_MEM:])
FIRST_UNIT = (0, N_FOX, N_FOX + HALF_MEM)
LATE = (1, 1, 2)


def mem_block(kind, g, k):
    return B_KV + MEM_BLOCKS.index((kind, g, k))


FILL_GROUPS = (3, 4, 5)
GROUP_Q = 4 * KB
FILL = (0, 1, 2, 2, 1, 1, 2, 2, 1, 1, 2, 1,
        1, 1, 2, 2, 1, 1, 2, 2, 1, 1, 2,
        1, 1, 1, 2, 1, 1, 1, 2, 2, 2, 2)


def fill_turn(j, quarters):
    return min(k for k in range(len(FILL)) if sum(FILL[:k + 1]) >= GROUP_Q * j + quarters)


LAST_ORDER = (0, 2, 1, 3)
MEM_FILL = ((2, 0), (1, 1), (1, 1), (1, 1), (1, 1), (1, 1), (1, 1), (0, 1), (0, 1))
MEM_FILLED = tuple(sum(sum(turn) for turn in MEM_FILL[:k]) for k in range(len(MEM_FILL) + 1))
MEM_PAIR_TURN = MEM_FILLED.index(min(n for n in MEM_FILLED if n >= GROUP_Q - 2)) - 1
PAIR_TURN = tuple(fill_turn(j, GROUP_Q - 2) for j in range(len(FILL_GROUPS)))
END_TURN = tuple(fill_turn(j, GROUP_Q) for j in range(len(FILL_GROUPS)))
N_UNITS = N_FOX + len(MEM_UNITS)
Y_FOX = FOX_H
Y_GLA = Y_FOX + GLA_H
N_CONSTS = 17
H_ADDS, F_ADDS = DC - 2, DC - 3



def build(nc, a, out):
    ctx = ExitStack()
    with ctx:
        sems = {}

        def sem(name):
            sems[name] = ctx.enter_context(nc.semaphore(name))
            return sems[name]

        top = [(nc.sbuf_base + 31) // 32 * 32]
        ends = []

        def sb(name, shape, dt=F32, at=None):
            size = 4
            for n in shape[1:]:
                size *= n
            where = top[0] if at is None else at
            if at is None:
                top[0] += (size + 31) // 32 * 32
            ends.append(where + size)
            return nc.alloc_sbuf_tensor_at(name, shape, dt, offset=where)

        h = sb("h", [P, DC, SEQ])
        xh = sb("xh", [P, DC, SEQ], F32R)
        xl = sb("xl", [P, DC, SEQ], F32R)
        raw = sb("raw", [P, RAW, BW])
        w_hi = sb("w_hi", [P, SPLIT, BW], F32R)
        w_lo = sb("w_lo", [P, SPLIT, BW], F32R)
        tmp = sb("tmp", [P, 4, SEQ])
        sq = sb("sq", [P, 2, SEQ])
        cum_hl = sb("cum_hl", [P, SEQ], F32R, at=top[0])
        acc = sb("acc", [P, SEQ])
        rinv = sb("rinv", [P, SEQ])
        ident = sb("ident", [P, P])
        ones = sb("ones", [P, P])
        ident_r = sb("ident_r", [P, P], F32R)
        causal = sb("causal", [P, P], F32R)
        gla_mask = sb("gla_mask", [P, P])
        gains = sb("gains", [P, G_ROWS])
        post = sb("post", [P, SUBLAYERS, DC])
        root_tok = sb("root_tok", [P, TC])
        rinv_tok = sb("rinv_tok", [P, TC])
        eps_t = sb("eps_t", [P, 1])
        b_f = sb("b_f", [FOX_H, 1])
        decay = sb("decay", [P, 2, NCH])
        nmx = sb("nmx", [P, 4])
        rs = sb("rs", [P, 4])
        rr = sb("rr", [P, 4])
        mem_ms = sb("mem_ms", [P, MC])
        mem_root = sb("mem_root", [P, MC])
        mem_rinv = sb("mem_rinv", [P, MC])
        shared = top[0]
        kib = 1024

        mid_hi = sb("mid_hi", [P, FC, SEQ], F32R, at=shared)
        mid_lo = sb("mid_lo", [P, FC, SEQ], F32R, at=shared + 44 * kib)
        x_tok = sb("x_tok", [P, TC, D], at=shared)
        f_fin = sb("f_fin", [P, DC, SEQ], at=shared)
        out_tok = sb("out_tok", [P, TC, D], at=shared + 16 * kib)
        f_saved = sb("f_saved", [P, 3, SEQ], at=shared + 88 * kib)
        gain_rows = sb("gain_rows", [G_ROWS, P], at=shared + 16 * kib)

        q_hi = sb("q_hi", [P, 4, SEQ], F32R, at=shared)
        q_lo = sb("q_lo", [P, 4, SEQ], F32R, at=shared + 8 * kib)
        k_hi = sb("k_hi", [P, 4, SEQ], F32R, at=shared + 16 * kib)
        k_lo = sb("k_lo", [P, 4, SEQ], F32R, at=shared + 24 * kib)
        v_hi = sb("v_hi", [P, TC, FOX_W], F32R, at=shared + 32 * kib)
        v_lo = sb("v_lo", [P, TC, FOX_W], F32R, at=shared + 40 * kib)
        gq = sb("gq", [P, 2, SEQ], at=shared + 48 * kib)
        gk = sb("gk", [P, 2, SEQ], at=shared + 52 * kib)
        gke = sb("gke", [P, 2, SEQ], at=shared + 56 * kib)
        gb = sb("gb", [P, 2, SEQ], at=shared + 60 * kib)
        gv = sb("gv", [P, TC, GLA_VW], at=shared + 64 * kib)
        gr = sb("gr", [P, GLA_H, SEQ], at=shared + 72 * kib)
        prob = sb("prob", [P, 2, SEQ], at=shared + 80 * kib)
        norm_diag = sb("norm_diag", [P, 2, P], at=shared + 84 * kib)
        pt_hi = sb("pt_hi", [P, TC, SEQ], F32R, at=shared + 86 * kib)
        pt_lo = sb("pt_lo", [P, TC, SEQ], F32R, at=shared + 94 * kib)
        sel = sb("sel", [P, FOX_H, P], F32R, at=shared + 102 * kib)
        ls_min = sb("ls_min", [P, 2, SEQ], at=shared + 72 * kib)
        cum = sb("cum", [FOX_H, SEQ], at=shared + 80 * kib)
        w_small = sb("w_small", [P, DC, 48], at=shared + 88 * kib)
        w_small_g = sb("w_small_g", [P, DC, 48], at=shared + 88 * kib + 1536)
        zg = sb("zg", [48, SEQ], at=shared + 91 * kib)
        w_a2 = sb("w_a2", [48, GLA_KW], at=shared + 93 * kib)
        ls_abs = sb("ls_abs", [P, 3, SEQ], at=shared + 94 * kib)
        sel32 = sb("sel32", [P, FOX_H, P], at=shared + 94 * kib)
        causal32 = sb("causal32", [P, P], at=shared + 98 * kib)
        reset = sb("reset", [P, SEQ], at=shared + 100 * kib)
        fox_hi, fox_lo = q_hi, q_lo
        ke_tok = sb("ke_tok", [P, TC, 2, P], at=shared + 16 * kib)
        at_sb = sb("at_sb", [P, 2, SEQ], at=shared + 20 * kib)
        o_sb = sb("o_sb", [P, GLA_H, SEQ], at=shared + 16 * kib)
        state = sb("state", [P, NCH - 1, SEQ], at=shared + 24 * kib)
        qm_hi = sb("qm_hi", [P, DC, SEQ], F32R, at=shared)
        qm_lo = sb("qm_lo", [P, DC, SEQ], F32R, at=shared + 16 * kib)
        mem_hi = sb("mem_hi", [P, DC, NMEM], F32R, at=shared + 32 * kib)
        mem_lo = sb("mem_lo", [P, DC, NMEM], F32R, at=shared + 40 * kib)
        km_hi = sb("km_hi", [P, DC, NMEM], F32R, at=shared + 48 * kib)
        km_lo = sb("km_lo", [P, DC, NMEM], F32R, at=shared + 56 * kib)
        vm_hi = sb("vm_hi", [P, MC, D], F32R, at=shared + 64 * kib)
        vm_lo = sb("vm_lo", [P, MC, D], F32R, at=shared + 72 * kib)
        mem_tok = sb("mem_tok", [P, MC, D], at=shared + 86 * kib)
        mem_n = sb("mem_n", [P, MC, D], at=shared + 94 * kib)
        assert max(ends) <= nc.sbuf_usable_end, (max(ends), nc.sbuf_usable_end)
        f0 = tmp[:, 3, :]

        bank = [ctx.enter_context(nc.psum_tensor(f"bank{i}", [P, SEQ], F32)) for i in range(8)]

        def out_bank(s, c):
            return bank[(c + OUT_OFF[s]) % 8]

        landed = [sem(f"landed{i}") for i in range(RAW)]
        hi_ready = sem("hi_ready")
        hi_half = sem("hi_half")
        lo_half = sem("lo_half")
        lo_ready = sem("lo_ready")
        w_used = sem("w_used")
        x_landed = [sem(f"x_landed{t}") for t in range(TC)]
        gains_landed = sem("gains_landed")
        small_landed = sem("small_landed")
        mem_landed = sem("mem_landed")
        stored = sem("stored")
        consts = sem("consts")
        gains_turned = sem("gains_turned")
        gains_ready = sem("gains_ready")
        turned = sem("turned")
        h_ready = sem("h_ready")
        xh_ready = sem("xh_ready")
        xl_ready = sem("xl_ready")
        hsq_ready = sem("hsq_ready")
        hacc_ready = sem("hacc_ready")
        hstat = sem("hstat")
        hroot = sem("hroot")
        hinv = sem("hinv")
        hspread = sem("hspread")
        hrinv = sem("hrinv")
        out_done = sem("out_done")
        fsq_ready = sem("fsq_ready")
        facc_ready = sem("facc_ready")
        f0_saved = sem("f0_saved")
        fstat = sem("fstat")
        froot = sem("froot")
        finv = sem("finv")
        fspread = sem("fspread")
        frinv = sem("frinv")
        f_scaled = sem("f_scaled")
        gate_scaled = sem("gate_scaled")
        up_scaled = sem("up_scaled")
        silu_done = sem("silu_done")
        mid_done = sem("mid_done")
        midh_done = sem("midh_done")
        midl_done = sem("midl_done")
        pair_done = sem("pair_done")
        small_scaled = sem("small_scaled")
        small_done = sem("small_done")
        z_ready = sem("z_ready")
        ga_done = sem("ga_done")
        z_min = sem("z_min")
        ls_act = sem("ls_act")
        cum_step = sem("cum_step")
        gcum_step = sem("gcum_step")
        cum_hi = sem("cum_hi")
        cum_lo = sem("cum_lo")
        sel_ready = sem("sel_ready")
        in_tmp = sem("in_tmp")
        in_hi = sem("in_hi")
        in_lo = sem("in_lo")
        exps = sem("exps")
        gdec = sem("gdec")
        scored = sem("scored")
        maxed = sem("maxed")
        expd = sem("expd")
        rsum = sem("rsum")
        normed = sem("normed")
        pturned = sem("pturned")
        pt_h = sem("pt_h")
        pt_l = sem("pt_l")
        pv_done = sem("pv_done")
        y_h = sem("y_h")
        y_l = sem("y_l")
        ke_turned = sem("ke_turned")
        ke_saved = sem("ke_saved")
        at_done = sem("at_done")
        at_masked = sem("at_masked")
        sc_done = sem("sc_done")
        st_ready = sem("st_ready")
        o_done = sem("o_done")
        gsq = sem("gsq")
        gcopy = sem("gcopy")
        gstat = sem("gstat")
        groot = sem("groot")
        ginv = sem("ginv")
        gspread = sem("gspread")
        gfactor = sem("gfactor")
        gout = sem("gout")
        mem_sq = sem("mem_sq")
        mem_root_s = sem("mem_root_s")
        mem_inv = sem("mem_inv")
        mem_normed = sem("mem_normed")
        mem_turned = sem("mem_turned")
        mem_h = sem("mem_h")
        mem_l = sem("mem_l")
        kv_h = sem("kv_h")
        kv_l = sem("kv_l")
        mq_t = sem("mq_t")
        mq_h = sem("mq_h")
        mq_l = sem("mq_l")
        saved_v = sem("saved_v")
        saved_a = sem("saved_a")
        normed_v = sem("normed_v")
        normed_p = sem("normed_p")
        summed_v = sem("summed_v")
        summed_p = sem("summed_p")
        oturned = sem("oturned")
        ocopied_a = sem("ocopied_a")
        ocopied_v = sem("ocopied_v")

        def at_turn(i, step, n):
            return n if i is None else i * step + n

        def fsq(m):
            m %= FSQ
            return sq[:, m, :] if m < 2 else tmp[:, m - 2, :]

        def wait_out(eng, s, c):
            if c < DC - 1:
                eng.wait_ge(out_done, (DC - 1) * s + c + 1)
            else:
                eng.wait_ge(w_used, OUT_END[s])

        def wait_group(eng, g, m):
            if g and m < 2:
                eng.wait_ge(pair_done, g)
            else:
                eng.wait_ge(w_used, B_IN + KB * (g + 1))

        def pv_count(mem, hd, e=0):
            return FOX_H + 2 * hd + e if mem else hd

        def s_bank(phase, k):
            return bank[k % (3 if phase == MEM_B else 2)]

        def p_bank(phase, k):
            return bank[3 + k % 2 if phase == MEM_B else 2]

        def o_bank(phase, hd, e=0):
            if phase == MEM_B:
                return bank[(6, 7, 5, 6)[2 * (hd - 2) + e]]
            return bank[5 if (phase, hd, e) == (MEM_A, 1, 1) else 3]

        def key_width(mem, i):
            return NMEM if mem else P * (i + 1)

        block = ctx.enter_context(nc.Block())

        @block.sync
        def _(sp):
            def fetch(n, srcs, i=None, step=0):
                if n >= RAW:
                    sp.wait_ge(lo_ready, at_turn(i, step, n - RAW + 1))
                for piece, src in enumerate(srcs):
                    dst = raw[:, n % RAW, :]
                    if len(src.shape) == 3:
                        dst = dst.rearrange("p (k u n) -> p k u n", k=2, u=2)[:, :, piece, :]
                    else:
                        dst = dst[:, piece * HW:(piece + 1) * HW]
                    sp.dma_start(dst, src).then_inc(landed[n % RAW], 16)

            def up_cols(w, k, col):
                return [w[2 * k * P:(2 * k + 2) * P, bass.ds(col + u * FF, 2 * P)].rearrange(
                    "(k p) n -> p k n", p=P) for u in range(2)]

            def row_pair(w, k, col):
                return [w[(2 * k + j) * P:(2 * k + j + 1) * P, col:col + HW] for j in range(2)]

            def row(w, start):
                return [w[bass.ds(start, P), j * HW:(j + 1) * HW] for j in range(2)]

            def small_loads():
                sp.dma_start(b_f[:, :], a["mix_b_f"].rearrange("l (h o) -> (l h) o", o=1)).then_inc(small_landed, 16)
                sp.dma_start(w_a2[32:48, :], a["mix_w_a2"][0]).then_inc(small_landed, 16)
                sp.wait_ge(consts, 5)
                for c0, width, where in ((COL_FZ, FOX_H, 0), (COL_GA, RANK, 32)):
                    sp.dma_start(w_small[:, :, where:where + width],
                                 a["mix_w_in"][0][:, c0:c0 + width].rearrange("(c p) n -> p c n", p=P))\
                      .then_inc(small_landed, 16)

            def swiglu_loads(w_gu, w_down, up, down, also=None):
                for k in range(KB):
                    fetch(up + k, up_cols(w_gu, k, 0))
                if also:
                    also()
                with sp.Fori(0, FG // 2) as i:
                    for k in range(2 * KB):
                        fetch(up + KB + k, up_cols(w_gu, k % KB, i * (4 * P) + (1 + k // KB) * 2 * P),
                              i, 2 * KB)
                for k in range(2):
                    fetch(down + k, row(w_down, k * P))
                with sp.Fori(0, (FC - 2) // 4) as i:
                    for k in range(4):
                        fetch(down + 2 + k, row(w_down, i * (4 * P) + (2 + k) * P), i, 4)

            for t in range(TC):
                sp.dma_start(x_tok[:, t, :], a["x"][0, t * P:(t + 1) * P, :]).then_inc(x_landed[t], 16)
            swiglu_loads(a["ffn1_w_gu"][0], a["ffn1_w_down"][0], B_UP1, B_DOWN1, small_loads)
            for n in range(B_IN, B_OUT):
                fetch(n, row_pair(a["mix_w_in"][0], (n - B_IN) % KB, IN_COLS[(n - B_IN) // KB]))
            for n in range(B_OUT, B_KV):
                j = n - B_OUT
                fetch(n, row_pair(a["mix_w_out"][0], j % 2, j // 2 * HW) if j < 4
                      else row(a["mix_w_out"][0], j * P))
                if n == B_OUT + RAW - 1:
                    sp.wait_ge(pv_done, FOX_H)
                    for t in range(MC):
                        sp.dma_start(mem_tok[:, t, :], a["mem"][0, t * P:(t + 1) * P, :]).then_inc(mem_landed, 16)
            for n, (kind, g, k) in enumerate(MEM_BLOCKS, B_KV):
                w, col = (a["mem_w_q"][0], 0) if kind == "q" else (a["mem_w_kv"][0], D if kind == "v" else 0)
                fetch(n, row_pair(w, k, col + g * HW))
            for n in range(B_MO, B_UP2):
                fetch(n, row(a["mem_w_o"][0], (n - B_MO) * P))
            swiglu_loads(a["ffn2_w_gu"][0], a["ffn2_w_down"][0], B_UP2, B_DOWN2)
            copied = [(ocopied_a, t + 1) for t in range(TC)]
            copied += [((ocopied_a, ocopied_v)[t % 2], (TC, 0)[t % 2] + t // 2 + 1) for t in range(TC)]
            for n, (semaphore, count) in enumerate(copied):
                half, t = n // TC, n % TC
                sp.wait_ge(semaphore, count)
                cols = slice(half * HW, (half + 1) * HW)
                sp.dma_start(out[0, t * P:(t + 1) * P, cols], out_tok[:, t, cols]).then_inc(stored, 16)
            sp.wait_ge(stored, 16 * 2 * TC)

        @block.gpsimd
        def _(gp):
            count = [0]

            def const(ins):
                count[0] += 1
                ins.then_inc(consts, 1)
                gp.wait_ge(consts, count[0])

            def split(n, i=None):
                if i is None and n in HALVED:
                    gp.wait_ge(hi_half, HALVED.index(n) + 1)
                    gp.tensor_tensor(w_lo[:, n % SPLIT, 0:HW], raw[:, n % RAW, 0:HW],
                                     w_hi[:, n % SPLIT, 0:HW].bitcast(F32), ALU.subtract).then_inc(lo_half, 1)
                    gp.wait_ge(hi_ready, n + 1)
                    gp.tensor_tensor(w_lo[:, n % SPLIT, HW:BW], raw[:, n % RAW, HW:BW],
                                     w_hi[:, n % SPLIT, HW:BW].bitcast(F32), ALU.subtract).then_inc(lo_ready, 1)
                    return
                gp.wait_ge(hi_ready, at_turn(i, RAW, n + 1))
                gp.tensor_tensor(w_lo[:, n % SPLIT, :], raw[:, n % RAW, :],
                                 w_hi[:, n % SPLIT, :].bitcast(F32), ALU.subtract).then_inc(lo_ready, 1)

            const(gp.memset(ident[:, :], 0.0))
            const(gp.affine_select(out=ident[:, :], in_=ident[:, :], compare_op=ALU.not_equal, fill=1.0,
                                   base=0, pattern=[[-1, P]], channel_multiplier=1))
            const(gp.memset(ones[:, :], 1.0))
            const(gp.memset(eps_t[:, :], EPS))
            const(gp.memset(w_small[:, :, :], 0.0))
            split(0)
            split(1)
            const(gp.memset(causal32[:, :], 0.0))
            const(gp.affine_select(out=causal32[:, :], in_=causal32[:, :], compare_op=ALU.is_ge, fill=NEG,
                                   base=0, pattern=[[-1, P]], channel_multiplier=1))
            const(gp.memset(gla_mask[:, :], 1.0))
            const(gp.affine_select(out=gla_mask[:, :], in_=gla_mask[:, :], compare_op=ALU.is_ge, fill=0.0,
                                   base=0, pattern=[[1, P]], channel_multiplier=-1))
            const(gp.memset(gla_mask[0:CHUNK, CHUNK:P], 0.0))
            const(gp.memset(reset[:, :], 1.0))
            const(gp.memset(reset[:, :].rearrange("p (n c) -> p n c", c=CHUNK)[:, :, 0:1], 0.0))
            const(gp.memset(sel32[:, :, :], 0.0))
            for base in (0, -32, -64, -96):
                const(gp.affine_select(out=sel32[:, :, :], in_=sel32[:, :, :], compare_op=ALU.not_equal,
                                       fill=-1.0, base=base, pattern=[[-1, FOX_H], [0, P]],
                                       channel_multiplier=1))
            assert count[0] == N_CONSTS, count[0]
            split(2)
            split(3)
            whole = HALVED.start // RAW, -(-HALVED.stop // RAW)
            with gp.Fori(1, whole[0]) as i:
                for q in range(RAW):
                    split(q, i)
            for n in range(whole[0] * RAW, whole[1] * RAW):
                split(n)
            with gp.Fori(whole[1], B_END // RAW) as i:
                for q in range(RAW):
                    split(q, i)
            for n in range(B_END // RAW * RAW, B_END):
                split(n)
            gp.wait_ge(frinv, SUBLAYERS)
            for c in (2, 3):
                gp.wait_ge(saved_a, c - 1)
                gp.tensor_tensor(f_fin[:, c, :], f_saved[:, c - 1, :], rinv[:, :], ALU.mult).then_inc(normed_p, 1)
            gp.wait_ge(normed_v, 3)
            gp.tensor_tensor(h[:, 7, :], h[:, 7, :], f_fin[:, 7, :], ALU.add).then_inc(summed_p, 1)

        @block.scalar
        def _(act):
            rounded = [0]

            def round_block(n, i=None, step=0):
                act.wait_ge(landed[n % RAW], at_turn(i, LAND * step // RAW, LAND * (n // RAW + 1)))
                if n >= SPLIT:
                    act.wait_ge(w_used, at_turn(i, step, n - SPLIT + 1))
                if i is None and n in HALVED:
                    act.activation(w_hi[:, n % SPLIT, 0:HW], raw[:, n % RAW, 0:HW], ACT.Copy).then_inc(hi_half, 1)
                    act.activation(w_hi[:, n % SPLIT, HW:BW], raw[:, n % RAW, HW:BW], ACT.Copy).then_inc(hi_ready, 1)
                    return
                act.activation(w_hi[:, n % SPLIT, :], raw[:, n % RAW, :], ACT.Copy).then_inc(hi_ready, 1)

            def round_to(end):
                while rounded[0] < min(end, B_END):
                    round_block(rounded[0])
                    rounded[0] += 1

            def pre_hi(s, c):
                act.wait_ge(h_ready, DC * s + c + 1)
                g = G_PRE[s] + c
                act.activation(xh[:, c, :], h[:, c, :], ACT.Copy, scale=gains[:, g:g + 1]).then_inc(xh_ready, 1)

            def pre_square(s, c):
                if c >= 2:
                    act.wait_ge(hacc_ready, H_ADDS * s + max(c - 2, 1))
                elif s:
                    act.wait_ge(facc_ready, F_ADDS * s)
                act.activation(sq[:, c % 2, :], h[:, c, :], ACT.Square).then_inc(hsq_ready, 1)

            def rms_root(dst, src, n):
                return act.activation(dst, src, ACT.Sqrt, bias=eps_t[:, 0:1], scale=1.0 / n)

            def pre_root(s):
                second = (B_UP1 + KB, B_IN + KB, mem_block("q", 1, 0), B_UP2 + KB)[s]
                round_to(second + 1)
                act.wait_ge(hstat, s + 1)
                rms_root(root_tok[:, :], bank[STAT_BANK[s]][:, 0:TC], D).then_inc(hroot, 1)
                if s in (0, 3):
                    act.preload_act_table(ACT.Silu)
                    round_to(second + 2)
                act.wait_ge(hspread, s + 1)
                act.activation(rinv[:, :], bank[STAT_BANK[s]][:, :], ACT.Copy).then_inc(hrinv, 1)

            def post_norm(s):
                round_to(OUT_END[s])
                act.preload_act_table(ACT.Sqrt)
                round_to(OUT_END[s] + 1)
                act.wait_ge(hacc_ready, H_ADDS * (s + 1))
                for m in range(DC):
                    wait_out(act, s, m)
                    if m >= FSQ:
                        act.wait_ge(facc_ready, F_ADDS * s + max(m - FSQ, 1))
                    act.activation(fsq(m), out_bank(s, m)[:, :], ACT.Square).then_inc(fsq_ready, 1)
                    if s == SUBLAYERS - 1 and m in (2, 3):
                        act.activation(f_saved[:, m - 1, :], out_bank(s, m)[:, :], ACT.Copy,
                                       scale=post[:, s, m:m + 1]).then_inc(saved_a, 1)
                round_to(OUT_END[s] + 2)
                act.wait_ge(fstat, s + 1)
                rms_root(root_tok[:, :], out_bank(s, 0)[:, 0:TC], D).then_inc(froot, 1)
                act.wait_ge(fspread, s + 1)
                if s < SUBLAYERS - 1:
                    act.wait_ge(f_scaled, DC * s + 1)
                act.activation(rinv[:, :], out_bank(s, 0)[:, :], ACT.Copy).then_inc(frinv, 1)

            def pre(s, start):
                for c in range(DC):
                    pre_hi(s, c)
                    if c in (3, 5):
                        round_to(start + 2 + (c - 1) // 2)
                    if c >= 2:
                        pre_square(s, c - 2)
                pre_square(s, DC - 2)
                pre_square(s, DC - 1)

            def swiglu(s, up, down):
                first = 2 * FG * (s // 3)

                def group(g, i=None):
                    for pair in range(2):
                        act.wait_ge(gate_scaled, at_turn(i, 4, first + 2 * g + pair + 1))
                        act.activation(tmp[:, pair, :], tmp[:, pair, :], ACT.Silu).then_inc(silu_done, 1)
                    for pair in range(2):
                        act.wait_ge(mid_done, at_turn(i, 4, first + 2 * g + pair + 1))
                        act.activation(mid_hi[:, bass.ds(at_turn(i, 4, 2 * g + pair), 1), :],
                                       tmp[:, 2 + pair:3 + pair, :], ACT.Copy).then_inc(midh_done, 1)

                pre(s, up)
                pre_root(s)
                round_to(up + 6)
                group(0)
                with act.Fori(0, FG // 2) as i:
                    for g in range(2):
                        for k in range(KB):
                            round_block(up + 6 + KB * g + k, i, 2 * KB)
                        group(1 + g, i)
                if s == 0:
                    act.wait_ge(consts, N_CONSTS)
                    act.activation(sel[:, :, :], sel32[:, :, :], ACT.Copy).then_inc(sel_ready, 1)
                    act.activation(causal[:, :], causal32[:, :], ACT.Copy).then_inc(sel_ready, 1)
                    act.activation(ident_r[:, :], ident[:, :], ACT.Copy).then_inc(sel_ready, 1)
                with act.Fori(0, (FC - 2) // 4) as i:
                    for k in range(4):
                        round_block(down + 2 + k, i, 4)
                rounded[0] = down + FC

            def log_sigmoid():
                t = [ls_abs[0:FOX_H, 0, :], ls_abs[:, 1, :], ls_abs[:, 2, :]]
                act.wait_ge(z_ready, 3)
                act.activation(t[0], zg[0:FOX_H, :], ACT.Abs, bias=b_f[:, 0:1]).then_inc(ls_act, 1)
                for j in (1, 2):
                    act.activation(t[j], gb[:, j - 1, :], ACT.Abs).then_inc(ls_act, 1)
                for j in range(3):
                    act.wait_ge(ls_act, j + 1)
                    act.activation(t[j], t[j], ACT.Exp, scale=-1.0).then_inc(ls_act, 1)
                round_to(B_IN + KB * 2 + 1)
                for j in range(3):
                    act.wait_ge(ls_act, 3 + j + 1)
                    act.activation(t[j], t[j], ACT.Ln, bias=1.0).then_inc(ls_act, 1)

            def in_evacuate(g, ms=range(4)):
                b = bank[IN_BANK[g]:IN_BANK[g] + 4]
                for m in ms:
                    if g < 2:
                        act.wait_ge(in_tmp, 4 * g + m + 1)
                        act.activation((q_hi, k_hi)[g][:, m, :], tmp[:, m, :], ACT.Copy).then_inc(in_hi, 1)
                    elif g in (2, 4):
                        wait_group(act, g, m)
                        act.wait_ge(hinv, 2)
                        act.activation((v_hi if g == 2 else gv)[:, m, :], b[m][:, :], ACT.Copy,
                                       scale=rinv_tok[:, m:m + 1]).then_inc(in_hi, 1)
                    elif g == 5:
                        act.wait_ge(in_tmp, 12 + m + 1)
                        act.activation(gr[:, m, :], tmp[:, m, :], ACT.Silu).then_inc(in_hi, 1)

            def decays(part):
                if part == 1:
                    act.activation(gke[:, :, :], gke[:, :, :], ACT.Exp, scale=1.0 / TAU).then_inc(exps, 1)
                    act.activation(gk[:, :, :], gb[:, :, :], ACT.Exp, scale=-1.0 / TAU).then_inc(exps, 1)
                    return
                act.wait_ge(gcum_step, 5)
                act.activation(decay[:, :, :], gb[:, :, :].rearrange("p k (n c) -> p k n c", c=CHUNK)[:, :, :, CHUNK - 1],
                               ACT.Exp, scale=1.0 / TAU).then_inc(exps, 1)
                act.activation(gq[:, :, :], gb[:, :, :], ACT.Exp, scale=1.0 / TAU).then_inc(exps, 1)

            def attention(phase):
                units, u0, late, mem = UNITS[phase], FIRST_UNIT[phase], LATE[phase], phase != FOX

                def output(done):
                    if not 0 <= done < len(units) or units[done][1] < TC - 1:
                        return
                    hd = units[done][0]
                    for e in range(2 if mem else 1):
                        act.wait_ge(pv_done, pv_count(mem, hd, e) + 1)
                        o = o_bank(phase, hd, e)
                        if mem:
                            act.activation(xh[:, 2 * hd + e, :], o[:, :], ACT.Copy).then_inc(y_h, 1)
                        else:
                            r = slice(FOX_D * (hd % 2), FOX_D * (hd % 2 + 1))
                            act.activation(fox_hi[r, hd // 2, :], o[r, :], ACT.Copy).then_inc(y_h, 1)

                for k in range(len(units) + late + 2):
                    if k < len(units):
                        u, w = u0 + k, key_width(mem, units[k][1])
                        act.wait_ge(maxed, u + 1)
                        if u >= 2:
                            act.wait_ge(pturned, u - 1)
                        act.activation(prob[:, u % 2, 0:w], s_bank(phase, k)[:, 0:w], ACT.Exp,
                                       bias=nmx[:, u % 4:u % 4 + 1],
                                       accum_out=rs[:, u % 4:u % 4 + 1]).then_inc(expd, 1)
                    if phase == FOX and k <= len(units) + late:
                        round_to(B_IN + KB * FILL_GROUPS[0] + 2 + sum(FILL[:k]) // 4)
                    elif phase == MEM_A:
                        round_to(mem_block("q", 1, 0) + 2 + MEM_FILLED[min(k, len(MEM_FILL))] // 4)
                    if phase == MEM_A:
                        output(k - late - 1)
                    if 0 <= k - late < len(units):
                        hd, i = units[k - late]
                        nk = key_width(mem, i) // P
                        act.wait_ge(pturned, u0 + k - late + 1)
                        if hd:
                            act.wait_ge(pv_done, pv_count(mem, hd))
                        act.activation(pt_hi[:, 0:nk, i * P:(i + 1) * P],
                                       p_bank(phase, k - late)[:, 0:nk * P].rearrange("p (j n) -> p j n", n=P),
                                       ACT.Copy).then_inc(pt_h, 1)
                    if phase != MEM_A:
                        output(k - late - (2 if mem else 1))
                    if phase == FOX:
                        if k == PAIR_TURN[1]:
                            in_evacuate(4, (0, 1))
                        if k == END_TURN[1]:
                            in_evacuate(4, (2, 3))
                    elif phase == MEM_A:
                        if k == MEM_PAIR_TURN:
                            mq_hi(1, (0, 1))
                        if k == len(MEM_FILL) - 1:
                            mq_hi(1, (2, 3))

            def mq_hi(g, ms=range(4)):
                for m in ms:
                    act.wait_ge(mq_t, 4 * g + m + 1)
                    act.activation(qm_hi[:, 4 * g + m, :], tmp[:, m, :], ACT.Copy).then_inc(mq_h, 1)

            def gla():
                for t in range(2):
                    act.wait_ge(ke_turned, t + 1)
                    act.activation(ke_tok[:, 2 * t:2 * t + 2, :, :], bank[t][:, :].rearrange(
                        "p (t c d) -> p t c d", t=2, c=2), ACT.Copy).then_inc(ke_saved, 1)
                round_to(B_OUT + 2)
                in_evacuate(5)
                act.preload_act_table(ACT.Sqrt)
                act.wait_ge(mem_landed, 16 * MC)
                for t in range(MC):
                    act.activation(mem_n[:, t, :], mem_tok[:, t, :], ACT.Square,
                                   accum_out=mem_ms[:, t:t + 1]).then_inc(mem_sq, 1)
                act.wait_ge(mem_sq, MC)
                rms_root(mem_root[:, :], mem_ms[:, :], D).then_inc(mem_root_s, 1)
                act.wait_ge(mem_inv, 1)
                for t in range(MC):
                    act.activation(mem_n[:, t, :], mem_tok[:, t, :], ACT.Copy,
                                   scale=mem_rinv[:, t:t + 1]).then_inc(mem_normed, 1)

                act.wait_ge(o_done, TC)
                for hd in range(GLA_H):
                    act.activation(tmp[:, hd, :], bank[4 + hd][:, :], ACT.Square).then_inc(gsq, 1)

                def mem_hi_chunks(cs):
                    for c in cs:
                        act.wait_ge(mem_turned, c // 2 + 1)
                        act.activation(mem_hi[:, c, :], bank[2 + c // 2 % 2][:, c % 2 * NMEM:(c % 2 + 1) * NMEM],
                                       ACT.Copy, scale=gains[:, G_KV + c:G_KV + c + 1]).then_inc(mem_h, 1)

                act.wait_ge(gstat, 1)
                rms_root(tmp[:, 3, :], bank[0][:, :], GLA_V).then_inc(groot, 1)
                mem_hi_chunks(range(4))
                round_to(B_OUT + 3)
                mem_hi_chunks(range(4, DC))
                round_to(B_OUT + 4)
                for hd in range(GLA_H):
                    act.wait_ge(gout, hd + 1)
                    act.activation(xh[:, 4 + hd, :], tmp[:, hd, :], ACT.Copy).then_inc(y_h, 1)

            def mixer():
                pre(1, B_IN)
                pre_root(1)
                round_to(B_IN + 6)
                in_evacuate(0)
                round_to(B_IN + 8)
                log_sigmoid()
                act.wait_ge(cum_step, 3)
                for r in (0, 64):
                    act.activation(cum_hl[r:r + FOX_H, :], cum[:, :], ACT.Copy).then_inc(cum_hi, 1)
                round_to(B_IN + KB * 2 + 2)
                in_evacuate(1)
                round_to(B_IN + KB * 3 - 1)
                decays(0)
                round_to(B_IN + KB * 3)
                decays(1)
                round_to(B_IN + KB * 3 + 1)
                in_evacuate(2, (0, 1))
                round_to(B_IN + KB * 3 + 2)
                in_evacuate(2, (2, 3))
                attention(FOX)
                gla()
                round_to(B_KV)

            def memory():
                def pre(c):
                    pre_hi(2, c)
                    pre_square(2, c)

                for g in range(2):
                    round_to(B_KV + KB * (g + 1) + 2)
                    for m in range(4):
                        act.wait_ge(w_used, B_KV + KB * (g + 1))
                        act.activation(km_hi[:, 4 * g + m, :], bank[KV_BANK["k", g] + m][:, 0:NMEM],
                                       ACT.Copy).then_inc(kv_h, 1)
                    pre(2 * g)
                    pre(2 * g + 1)
                for k in range(3):
                    round_to(mem_block("q", 0, k) + 1)
                    pre(4 + k)
                pre(7)
                for g in range(2):
                    for m in range(MC):
                        act.wait_ge(w_used, mem_block("v", 1, KB - 1) + 1)
                        act.activation(vm_hi[:, m, g * HW:(g + 1) * HW], bank[KV_BANK["v", g] + m][:, :],
                                       ACT.Copy).then_inc(kv_h, 1)
                round_to(mem_block("q", 0, KB - 1) + 1)
                pre_root(2)
                round_to(mem_block("q", 1, 0) + 2)
                mq_hi(0)
                attention(MEM_A)
                attention(MEM_B)
                round_to(B_UP2)

            for r, name in enumerate(GAINS):
                act.dma_start(gain_rows[r * 8:r * 8 + 8, :],
                              a[name].rearrange("l (c p) -> (l c) p", p=P)).then_inc(gains_landed, 16)
            act.dma_start(gain_rows[G_BA:G_BA + 2, :],
                          a["mix_b_a"].rearrange("l (c p) -> (l c) p", p=P)).then_inc(gains_landed, 16)
            act.dma_start(gain_rows[G_GLA:G_GLA + 4, :],
                          a["mix_g_gla"].rearrange("l (c p) -> (l c) p", p=P)).then_inc(gains_landed, 16)
            act.preload_act_table(ACT.Sqrt)
            round_to(2)
            act.wait_ge(gains_ready, 1)
            swiglu(0, B_UP1, B_DOWN1)
            post_norm(0)
            mixer()
            post_norm(1)
            memory()
            post_norm(2)
            swiglu(3, B_UP2, B_DOWN2)
            post_norm(3)
            for t in range(TC):
                act.wait_ge(oturned, t + 1)
                act.activation(out_tok[:, t, 0:HW], bank[4 + t][:, :], ACT.Copy).then_inc(ocopied_a, 1)
            for t in range(0, TC, 2):
                act.wait_ge(oturned, TC + t + 1)
                act.activation(out_tok[:, t, HW:D], bank[t][:, :], ACT.Copy).then_inc(ocopied_a, 1)

        @block.vector
        def _(dve):
            def pre_lo(s, c):
                g = G_PRE[s] + c
                dve.wait_ge(xh_ready, DC * s + c + 1)
                dve.scalar_tensor_tensor(out=xl[:, c, :], in0=h[:, c, :], scalar=gains[:, g:g + 1],
                                         in1=xh[:, c, :].bitcast(F32), op0=ALU.mult,
                                         op1=ALU.subtract).then_inc(xl_ready, 1)

            def add_square(acc_ready, adds, norms, c, square, before):
                if c == 1:
                    for semaphore, count in before:
                        dve.wait_ge(semaphore, count)
                    dve.tensor_tensor(acc[:, :], square(0), square(1), ALU.add).then_inc(acc_ready, 1)
                elif 1 < c <= adds:
                    dve.wait_ge(acc_ready, adds * norms + c - 1)
                    dve.tensor_tensor(acc[:, :], acc[:, :], square(c), ALU.add).then_inc(acc_ready, 1)

            def pre_add(s, c):
                dve.wait_ge(hsq_ready, DC * s + c + 1)
                add_square(hacc_ready, H_ADDS, s, c, lambda k: sq[:, k % 2, :], [(fstat, s)] if s else [])

            def pre(s, chunk):
                for c in range(DC):
                    chunk(c)
                    if c >= 3:
                        pre_add(s, c - 3)
                    if s:
                        pre_lo(s, c)
                    elif c:
                        pre_lo(s, c - 1)
                if s == 0:
                    pre_lo(s, DC - 1)
                for c in range(DC - 3, DC - 1):
                    pre_add(s, c)

            def pre_inv(s):
                dve.wait_ge(hroot, s + 1)
                dve.reciprocal(rinv_tok[:, :], root_tok[:, :]).then_inc(hinv, 1)
                dve.wait_ge(hrinv, s + 1)

            def post_norm(s):
                for m in range(DC):
                    dve.wait_ge(fsq_ready, DC * s + m + 1)
                    if m == 0:
                        dve.tensor_copy(f0, out_bank(s, 0)[:, :]).then_inc(f0_saved, 1)
                    if m == 1 and s == SUBLAYERS - 1:
                        dve.tensor_scalar(f_saved[:, 0, :], out_bank(s, 1)[:, :], post[:, s, 1:2], None,
                                          ALU.mult).then_inc(saved_v, 1)
                    add_square(facc_ready, F_ADDS, s, m, fsq, [(hstat, s + 1)])
                dve.wait_ge(froot, s + 1)
                dve.reciprocal(rinv_tok[:, :], root_tok[:, :]).then_inc(finv, 1)
                if s == SUBLAYERS - 1:
                    dve.wait_ge(frinv, s + 1)

            def scale_output(s, m):
                if m == 0:
                    dve.wait_ge(fspread, s + 1)
                    dve.tensor_tensor(tmp[:, 0, :], f0, out_bank(s, 0)[:, :], ALU.mult).then_inc(f_scaled, 1)
                    return
                if m == 1:
                    dve.wait_ge(frinv, s + 1)
                dve.tensor_tensor(tmp[:, m % 2, :], out_bank(s, m)[:, :], rinv[:, :], ALU.mult).then_inc(f_scaled, 1)

            def residual(s, m):
                if m == 0:
                    scale_output(s, 0)
                dve.wait_ge(f_scaled, DC * s + m + 1)
                dve.scalar_tensor_tensor(out=h[:, m, :], in0=tmp[:, m % 2, :], scalar=post[:, s, m:m + 1],
                                         in1=h[:, m, :], op0=ALU.mult, op1=ALU.add).then_inc(h_ready, 1)
                if m < DC - 1:
                    scale_output(s, m + 1)

            def swiglu(s, up):
                first = 2 * FG * (s // 3)

                def group(g, i=None):
                    b = bank[4 * (g % 2):4 * (g % 2) + 4]
                    dve.wait_ge(w_used, at_turn(i, 2 * KB, up + KB * (g + 1)))
                    for pair in range(2):
                        n = first + 2 * g + pair
                        if n >= 2:
                            dve.wait_ge(midl_done, at_turn(i, 4, n - 1))
                        dve.tensor_tensor(tmp[:, pair, :], b[pair][:, :], rinv[:, :], ALU.mult).then_inc(gate_scaled, 1)
                        dve.tensor_tensor(tmp[:, 2 + pair, :], b[2 + pair][:, :], rinv[:, :],
                                          ALU.mult).then_inc(up_scaled, 1)
                    for pair in range(2):
                        n = first + 2 * g + pair
                        dve.wait_ge(silu_done, at_turn(i, 4, n + 1))
                        dve.wait_ge(up_scaled, at_turn(i, 4, n + 2))
                        dve.tensor_tensor(tmp[:, 2 + pair, :], tmp[:, pair, :], tmp[:, 2 + pair, :],
                                          ALU.mult).then_inc(mid_done, 1)
                    for pair in range(2):
                        n = first + 2 * g + pair
                        dve.wait_ge(midh_done, at_turn(i, 4, n + 1))
                        chunk = at_turn(i, 4, 2 * g + pair)
                        dve.tensor_tensor(mid_lo[:, bass.ds(chunk, 1), :], tmp[:, 2 + pair:3 + pair, :],
                                          mid_hi[:, bass.ds(chunk, 1), :].bitcast(F32),
                                          ALU.subtract).then_inc(midl_done, 1)

                pre_inv(s)
                group(0)
                if s == 0:
                    dve.wait_ge(small_landed, 16 * SMALL_LOADS)
                    for c in range(DC):
                        g = G_PRE[1] + c
                        dve.tensor_scalar(w_small_g[:, c, :], w_small[:, c, :], gains[:, g:g + 1], None,
                                          ALU.mult).then_inc(small_scaled, 1)
                with dve.Fori(0, FG // 2) as i:
                    for g in range(2):
                        group(1 + g, i)

            def attention(phase):
                units, u0, late, mem = UNITS[phase], FIRST_UNIT[phase], LATE[phase], phase != FOX
                y0 = Y_GLA if mem else 0

                def output(done):
                    if not 0 <= done < len(units) or units[done][1] < TC - 1:
                        return
                    hd = units[done][0]
                    for e in range(2 if mem else 1):
                        y_hi, y_lo, c = (xh, xl, 2 * hd + e) if mem else (fox_hi, fox_lo, hd // 2)
                        r = slice(0, P) if mem else slice(FOX_D * (hd % 2), FOX_D * (hd % 2 + 1))
                        dve.wait_ge(y_h, y0 + (2 * hd + e if mem else hd) + 1)
                        dve.tensor_tensor(y_lo[r, c, :], o_bank(phase, hd, e)[r, :], y_hi[r, c, :].bitcast(F32),
                                          ALU.subtract).then_inc(y_l, 1)

                for k in range(len(units) + late + 2):
                    if k < len(units):
                        u, w = u0 + k, key_width(mem, units[k][1])
                        r = slice(u % 4, u % 4 + 1)
                        dve.wait_ge(scored, u + 1)
                        dve.tensor_reduce(nmx[:, r], s_bank(phase, k)[:, 0:w], AX_X, ALU.max,
                                          negate=True).then_inc(maxed, 1)
                    if phase == FOX and k == 0:
                        in_evacuate(2, (2, 3))
                    if 0 <= k - 1 < len(units):
                        u = u0 + k - 1
                        r = slice(u % 4, u % 4 + 1)
                        dve.wait_ge(expd, u + 1)
                        dve.reciprocal(rr[:, r], rs[:, r]).then_inc(rsum, 1)
                        dve.wait_ge(rsum, u + 1)
                        if u >= 2:
                            dve.wait_ge(pturned, u - 1)
                        dve.tensor_scalar(norm_diag[:, u % 2, :], ident[:, :], rr[:, r], None,
                                          ALU.mult).then_inc(normed, 1)
                    if phase == MEM_A:
                        output(k - late - 1)
                    if 0 <= k - late < len(units):
                        i = units[k - late][1]
                        nk = key_width(mem, i) // P
                        dve.wait_ge(pt_h, u0 + k - late + 1)
                        dve.tensor_tensor(pt_lo[:, 0:nk, i * P:(i + 1) * P],
                                          p_bank(phase, k - late)[:, 0:nk * P].rearrange("p (j n) -> p j n", n=P),
                                          pt_hi[:, 0:nk, i * P:(i + 1) * P].bitcast(F32),
                                          ALU.subtract).then_inc(pt_l, 1)
                    if phase != MEM_A:
                        output(k - late - (2 if mem else 1))
                    if phase == FOX:
                        for g in (3, 5):
                            if k == PAIR_TURN[g - 3]:
                                in_evacuate(g, (0, 1))
                            if k == END_TURN[g - 3]:
                                in_evacuate(g, (2, 3))
                        if 0 < k - END_TURN[0] <= 3:
                            decayed(k - END_TURN[0] - 1)
                    elif phase == MEM_A:
                        if k == MEM_PAIR_TURN:
                            mq_scaled(1, (0, 1))
                        if k == MEM_PAIR_TURN + 1:
                            mq_lo(1, (0, 1))
                        if k == len(MEM_FILL) - 1:
                            mq_scaled(1, (2, 3))
                        if k == len(MEM_FILL):
                            mq_lo(1, (2, 3))

            def mq_scaled(g, ms=range(4)):
                for m in ms:
                    if g:
                        dve.wait_ge(mq_l, m + 1)
                    if g and m < 2:
                        dve.wait_ge(pair_done, 6)
                    else:
                        dve.wait_ge(w_used, mem_block("q", g, KB - 1) + 1)
                    dve.scalar_tensor_tensor(out=tmp[:, m, :], in0=bank[MQ_BANK[g] + m][:, :],
                                             scalar=MEM_D ** -0.5, in1=rinv[:, :],
                                             op0=ALU.mult, op1=ALU.mult).then_inc(mq_t, 1)

            def mq_lo(g, ms=range(4)):
                for m in ms:
                    j = 4 * g + m
                    dve.wait_ge(mq_h, j + 1)
                    dve.tensor_tensor(qm_lo[:, j, :], tmp[:, m, :], qm_hi[:, j, :].bitcast(F32),
                                      ALU.subtract).then_inc(mq_l, 1)

            def gates():
                for j in range(2):
                    dve.wait_ge(ga_done, j + 1)
                    dve.tensor_scalar(gb[:, j, :], bank[6 + j][:, :], gains[:, G_BA + j:G_BA + j + 1], None,
                                      ALU.add).then_inc(z_ready, 1)
                    dve.wait_ge(z_ready, 2 + j)
                    dve.tensor_scalar(ls_min[:, j, :], gb[:, j, :], 0.0, None, ALU.min).then_inc(z_min, 1)
                forget()
                for j in range(2):
                    dve.wait_ge(ls_act, 8 + j)
                    dve.wait_ge(z_min, 2 + j)
                    dve.tensor_tensor(ls_min[:, j, :], ls_min[:, j, :], ls_abs[:, 1 + j, :],
                                      ALU.subtract).then_inc(gcum_step, 1)
                    dve.wait_ge(gcum_step, 2 * j + 1)
                    dve.tensor_tensor_scan(gb[:, j, :], reset[:, :], ls_min[:, j, :], 0.0,
                                           ALU.mult, ALU.add).then_inc(gcum_step, 1)
                dve.wait_ge(gcum_step, 4)
                b = gb[:, :, :].rearrange("p k (n c) -> p (k n) c", c=CHUNK)
                dve.tensor_tensor(gke[:, :, :].rearrange("p k (n c) -> p (k n) c", c=CHUNK),
                                  b[:, :, CHUNK - 1:CHUNK].to_broadcast([P, 2 * NCH, CHUNK]), b,
                                  ALU.subtract).then_inc(gcum_step, 1)

            def forget():
                dve.wait_ge(ls_act, 7)
                dve.wait_ge(z_min, 1)
                dve.tensor_tensor(cum[:, :], cum[:, :], ls_abs[0:FOX_H, 0, :], ALU.subtract).then_inc(cum_step, 1)
                dve.wait_ge(cum_step, 2)
                dve.tensor_tensor_scan(cum[:, :], ones[0:FOX_H, 0:1].to_broadcast([FOX_H, SEQ]), cum[:, :], 0.0,
                                       ALU.mult, ALU.add).then_inc(cum_step, 1)

            def in_evacuate(g, ms=range(4)):
                b = bank[IN_BANK[g]:IN_BANK[g] + 4]
                if g in (0, 1, 3, 5):
                    scale = {0: FOX_D ** -0.5, 3: GLA_K ** -0.5}
                    for m in ms:
                        wait_group(dve, g, m)
                        if g == 1:
                            dve.wait_ge(in_lo, m + 1)
                        elif g == 3:
                            dve.wait_ge(in_lo, 4 + m + 1)
                        elif g == 5:
                            dve.wait_ge(gdec, 3)
                        dve.scalar_tensor_tensor(out=tmp[:, m, :], in0=b[m][:, :],
                                                 scalar=scale[g] if g in scale and m < 2 or g == 0 else 1.0,
                                                 in1=rinv[:, :], op0=ALU.mult, op1=ALU.mult).then_inc(in_tmp, 1)
                for m in ms:
                    if g < 2:
                        hi, lo = ((q_hi, q_lo), (k_hi, k_lo))[g]
                        dve.wait_ge(in_hi, 4 * g + m + 1)
                        dve.tensor_tensor(lo[:, m, :], tmp[:, m, :], hi[:, m, :].bitcast(F32),
                                          ALU.subtract).then_inc(in_lo, 1)
                    elif g == 2:
                        dve.wait_ge(in_hi, 8 + m + 1)
                        dve.scalar_tensor_tensor(out=v_lo[:, m, :], in0=b[m][:, :], scalar=rinv_tok[:, m:m + 1],
                                                 in1=v_hi[:, m, :].bitcast(F32), op0=ALU.mult,
                                                 op1=ALU.subtract).then_inc(in_lo, 1)

            def decayed(j):
                dst, src = ((gq, 0), (gke, 2), (gk, 2))[j]
                dve.wait_ge(exps, 4)
                dve.wait_ge(in_tmp, 8 + src + 2)
                dve.tensor_tensor(dst[:, :, :], tmp[:, src:src + 2, :], dst[:, :, :], ALU.mult).then_inc(gdec, 1)

            def gla():
                def mask(m):
                    dve.wait_ge(at_done, m + 1)
                    if m >= 2:
                        dve.wait_ge(o_done, m - 1)
                    for e in range(2):
                        dve.tensor_tensor(at_sb[:, m % 2, :].rearrange("p (c e i) -> p c e i", e=2, i=P)[:, :, e, :],
                                          bank[e][:, 0:2 * P].rearrange("p (c i) -> p c i", i=P),
                                          gla_mask[:, :].rearrange("p (o i) -> p o i", o=1).to_broadcast([P, 2, P]),
                                          ALU.mult).then_inc(at_masked, 1)

                def step(n):
                    dve.wait_ge(sc_done, n + 1)
                    b = bank[2 + n % 2]
                    if n == 0:
                        dve.tensor_copy(state[:, 0, :], b[:, :]).then_inc(st_ready, 1)
                        return
                    dve.wait_ge(st_ready, 2 * n - 1)
                    for c in range(2):
                        half = slice(256 * c, 256 * c + 256)
                        dve.scalar_tensor_tensor(out=state[:, n, half], in0=state[:, n - 1, half],
                                                 scalar=decay[:, c, n:n + 1], in1=b[:, half],
                                                 op0=ALU.mult, op1=ALU.add).then_inc(st_ready, 1)

                mask(0)
                step(0)
                for m in range(1, TC):
                    mask(m)
                    step(2 * m - 1)
                    step(2 * m)
                dve.wait_ge(mem_root_s, 1)
                dve.reciprocal(mem_rinv[:, :], mem_root[:, :]).then_inc(mem_inv, 1)

                def mem_lo_chunk(c):
                    dve.wait_ge(mem_h, c // 2 * 2 + 2)
                    dve.scalar_tensor_tensor(out=mem_lo[:, c, :],
                                             in0=bank[2 + c // 2 % 2][:, c % 2 * NMEM:(c % 2 + 1) * NMEM],
                                             scalar=gains[:, G_KV + c:G_KV + c + 1],
                                             in1=mem_hi[:, c, :].bitcast(F32), op0=ALU.mult,
                                             op1=ALU.subtract).then_inc(mem_l, 1)

                def factor(hd):
                    dve.wait_ge(gspread, hd + 1)
                    dve.scalar_tensor_tensor(out=tmp[:, hd, :], in0=bank[1 - hd % 2][:, :],
                                             scalar=gains[:, G_GLA + hd:G_GLA + hd + 1], in1=gr[:, hd, :],
                                             op0=ALU.mult, op1=ALU.mult).then_inc(gfactor, 1)

                for hd in range(GLA_H):
                    dve.wait_ge(gsq, hd + 1)
                    dve.tensor_copy(o_sb[:, hd, :], bank[4 + hd][:, :]).then_inc(gcopy, 1)
                dve.wait_ge(groot, 1)
                dve.reciprocal(tmp[:, 3, :], tmp[:, 3, :]).then_inc(ginv, 1)
                for c in range(4):
                    mem_lo_chunk(c)
                factor(0)
                factor(1)
                factor(2)
                factor(3)
                for c in range(4, DC):
                    mem_lo_chunk(c)
                for hd in range(GLA_H):
                    dve.wait_ge(gfactor, hd + 1)
                    dve.tensor_tensor(tmp[:, hd, :], o_sb[:, hd, :], tmp[:, hd, :], ALU.mult).then_inc(gout, 1)
                for hd in range(GLA_H):
                    dve.wait_ge(y_h, Y_FOX + hd + 1)
                    dve.tensor_tensor(xl[:, 4 + hd, :], tmp[:, hd, :], xh[:, 4 + hd, :].bitcast(F32),
                                      ALU.subtract).then_inc(y_l, 1)

            def mixer():
                pre(1, lambda c: residual(0, c))
                pre_inv(1)
                dve.wait_ge(small_done, 1)
                dve.tensor_tensor(zg[:, :], bank[SMALL_BANK][0:48, :], rinv[0:48, :], ALU.mult).then_inc(z_ready, 1)
                dve.memset(cum_hl[:, :].bitcast(F32), 0.0).then_inc(cum_step, 1)
                dve.wait_ge(z_ready, 1)
                dve.tensor_scalar(cum[:, :], zg[0:FOX_H, :], b_f[:, 0:1], 0.0, ALU.add, ALU.min).then_inc(z_min, 1)
                in_evacuate(0)
                gates()
                dve.wait_ge(cum_hi, 2)
                for r in (32, 96):
                    dve.tensor_tensor(cum_hl[r:r + FOX_H, :], cum[:, :], cum_hl[0:FOX_H, :].bitcast(F32),
                                      ALU.subtract).then_inc(cum_lo, 1)
                in_evacuate(1)
                in_evacuate(2, (0, 1))
                attention(FOX)
                gla()

            def memory():
                def pre(c):
                    pre_lo(2, c)
                    pre_add(2, c)

                for c in range(DC):
                    residual(1, c)
                for g in range(2):
                    for m in range(4):
                        dve.wait_ge(kv_h, 4 * g + m + 1)
                        dve.tensor_tensor(km_lo[:, 4 * g + m, :], bank[KV_BANK["k", g] + m][:, 0:NMEM],
                                          km_hi[:, 4 * g + m, :].bitcast(F32), ALU.subtract).then_inc(kv_l, 1)
                    pre(2 * g)
                    pre(2 * g + 1)
                for k in range(KB):
                    pre(4 + k)
                for g in range(2):
                    for m in range(MC):
                        cols = slice(g * HW, (g + 1) * HW)
                        dve.wait_ge(kv_h, 8 + MC * g + m + 1)
                        dve.tensor_tensor(vm_lo[:, m, cols], bank[KV_BANK["v", g] + m][:, :],
                                          vm_hi[:, m, cols].bitcast(F32), ALU.subtract).then_inc(kv_l, 1)
                pre_inv(2)
                mq_scaled(0)
                mq_lo(0)
                attention(MEM_A)
                attention(MEM_B)

            dve.wait_ge(gains_turned, 1)
            dve.tensor_copy(gains[:, :], bank[7][:, 0:G_ROWS]).then_inc(gains_ready, 1)
            dve.wait_ge(gains_ready, 1)
            for s in range(SUBLAYERS):
                dve.tensor_scalar(post[:, s, :], gains[:, G_POST[s]:G_POST[s] + DC], POST_SCALE[s], None,
                                  ALU.mult).then_inc(gains_ready if s else up_scaled, 1)

            def input_chunk(c):
                dve.wait_ge(turned, c + 1)
                dve.tensor_copy(h[:, c, :], bank[c][:, :]).then_inc(h_ready, 1)
                dve.wait_ge(h_ready, c + 1)

            pre(0, input_chunk)
            swiglu(0, B_UP1)
            post_norm(0)
            mixer()
            post_norm(1)
            memory()
            post_norm(2)
            pre(3, lambda c: residual(2, c))
            swiglu(3, B_UP2)
            post_norm(3)
            for c in (0, 1, 7, 4, 5, 6):
                if c == 1:
                    dve.wait_ge(saved_v, 1)
                    dve.tensor_tensor(f_fin[:, c, :], f_saved[:, 0, :], rinv[:, :], ALU.mult).then_inc(normed_v, 1)
                else:
                    src = f0 if c == 0 else out_bank(3, c)[:, :]
                    dve.scalar_tensor_tensor(out=f_fin[:, c, :], in0=src, scalar=post[:, 3, c:c + 1],
                                             in1=rinv[:, :], op0=ALU.mult, op1=ALU.mult).then_inc(normed_v, 1)
            for c in (4, 5, 6):
                dve.wait_ge(normed_v, c)
                dve.tensor_tensor(h[:, c, :], h[:, c, :], f_fin[:, c, :], ALU.add).then_inc(summed_v, 1)
            for t in range(1, TC, 2):
                dve.wait_ge(oturned, TC + t + 1)
                dve.tensor_copy(out_tok[:, t, HW:D], bank[t][:, :]).then_inc(ocopied_v, 1)

        @block.tensor
        def _(pe):
            def three(dst, w, x, start, stop, loose=False):
                pe.matmul(dst, w[0], x[0], start=start, stop=False, skip_group_check=loose)
                pe.matmul(dst, w[0], x[1], start=False, stop=False, skip_group_check=loose)
                return pe.matmul(dst, w[1], x[0], start=False, stop=stop, skip_group_check=loose)

            def warm_up(dst, products):
                for _ in range(products):
                    pe.matmul(dst[:, :], ones[:, :], ones[:, 0:1].to_broadcast([P, SEQ]), start=True, stop=True)

            def token_sums(dst, parts):
                for n, (square, waits) in enumerate(parts):
                    for semaphore, count in waits:
                        pe.wait_ge(semaphore, count)
                    for t in range(TC):
                        last = pe.matmul(dst[:, t:t + 1], square[:, t * P:(t + 1) * P], ones[:, 0:1],
                                         start=n == t == 0, stop=n == len(parts) - 1, skip_group_check=True)
                return last

            def spread(dst, src):
                for t in range(TC):
                    last = pe.matmul(dst[:, t * P:(t + 1) * P], src[:, t:t + 1].to_broadcast([P, P]), ident[:, :],
                                     start=True, stop=True)
                return last

            def first_block(s, n, b0):
                free = {m: (f_scaled, DC * (s - 1) + m + 1) if s else (h_ready, m + 1) for m in range(4)}
                if s:
                    free[0] = (frinv, s)
                group_block(n, 0, b0, (xh, xl), s=s, quarters=LAST_ORDER, free=free)

            def closing_block(s, n, b0, also=None):
                group_block(n, KB - 1, b0, (xh, xl), s=s, quarters=(0, 1, 2))
                token_sums(bank[STAT_BANK[s]], [
                    (acc, [(hacc_ready, H_ADDS * (s + 1))]),
                    (sq[:, (DC - 1) % 2, :], [(hsq_ready, DC * (s + 1))])]).then_inc(hstat, 1)
                group_block(n, KB - 1, b0, (xh, xl), quarters=(3,))
                if also:
                    also()
                pe.wait_ge(hinv, s + 1)
                spread(bank[STAT_BANK[s]], rinv_tok).then_inc(hspread, 1)

            def turn_h(t):
                for j in range(4):
                    pe.matmul(bank[4 + t][:, j * P:(j + 1) * P], h[:, j, t * P:(t + 1) * P], ident[:, :],
                              start=j == 0, stop=False, skip_group_check=True)

            def turn_f(c):
                for t in range(TC):
                    last = pe.matmul(bank[4 + t][:, c * P:(c + 1) * P], f_fin[:, c, t * P:(t + 1) * P],
                                     ident[:, :], start=False, stop=c == 3, skip_group_check=True)
                    if c == 3:
                        last.then_inc(oturned, 1)

            def out_stat(s):
                if s == SUBLAYERS - 1:
                    pe.wait_ge(saved_v, 1)
                    turn_h(1)
                    pe.wait_ge(saved_a, 1)
                    turn_h(2)
                token_sums(out_bank(s, 0), [
                    (fsq(DC - 2), [(f0_saved, s + 1), (fsq_ready, DC * s + DC - 1)]),
                    (acc, [(facc_ready, F_ADDS * (s + 1))]),
                    (fsq(DC - 1), [(fsq_ready, DC * (s + 1))])]).then_inc(fstat, 1)
                if s == SUBLAYERS - 1:
                    pe.wait_ge(saved_a, 2)
                    turn_h(3)
                pe.wait_ge(finv, s + 1)
                spread(out_bank(s, 0), rinv_tok).then_inc(fspread, 1)

            def weights(n, i=None, step=0):
                if i is not None or n not in HALVED:
                    pe.wait_ge(lo_ready, at_turn(i, step, n + 1))
                return w_hi[:, n % SPLIT, :], w_lo[:, n % SPLIT, :]

            def weight_half(n, c):
                if n in HALVED:
                    pe.wait_ge(*((lo_ready, n + 1) if c % 2 else (lo_half, HALVED.index(n) + 1)))

            def group_block(n, k, b0, x, width=SEQ, s=None, i=None, step=0, quarters=range(4),
                            free={}, pair=False, last_chunk=DC - 1):
                w = weights(n, i, step)
                for q in quarters:
                    c = 2 * k + q // 2
                    if i is None:
                        weight_half(n, c)
                    if s is not None:
                        pe.wait_ge(xl_ready, DC * s + c + 1)
                    for m in (q % 2 * 2, q % 2 * 2 + 1):
                        if m in free:
                            pe.wait_ge(*free[m])
                        cols = slice((c % 2 * 4 + m) * P, (c % 2 * 4 + m + 1) * P)
                        last = three(bank[b0 + m][:, 0:width], (w[0][:, cols], w[1][:, cols]),
                                     (x[0][:, c, :], x[1][:, c, :]), c == 0, c == last_chunk, last_chunk == DC)
                    if q == 2 and pair:
                        last.then_inc(pair_done, 1)
                if 3 in quarters:
                    last.then_inc(w_used, 1)

            def token_block(n, k, b0, x, tokens, quarters=range(4), free={}, pair=False):
                w = weights(n)
                for q in quarters:
                    c = 2 * k + q // 2
                    weight_half(n, c)
                    cols = slice(c % 2 * HW, (c % 2 + 1) * HW)
                    for t in range(q % 2 * tokens // 2, (q % 2 + 1) * tokens // 2):
                        if t in free:
                            pe.wait_ge(*free[t])
                        tok = slice(t * P, (t + 1) * P)
                        last = three(bank[b0 + t][:, :], (x[0][:, c, tok], x[1][:, c, tok]),
                                     (w[0][:, cols], w[1][:, cols]), c == 0, c == DC - 1)
                    if q == 2 and pair:
                        last.then_inc(pair_done, 1)
                if 3 in quarters:
                    last.then_inc(w_used, 1)

            def out_block(s, n, x, first, end, i=None, step=0, free={}, ms=range(DC)):
                w = weights(n, i, step)
                for m in ms:
                    if m in free:
                        pe.wait_ge(*free[m])
                    cols = slice(m * P, (m + 1) * P)
                    last = three(out_bank(s, m)[:, :], (w[0][:, cols], w[1][:, cols]), x, first, end, True)
                    if end and m < DC - 1:
                        last.then_inc(out_done, 1)
                if DC - 1 in ms:
                    last.then_inc(w_used, 1)

            def swiglu(s, up, down):
                first = 2 * FG * (s // 3)
                first_block(s, up, 0)
                for k in range(1, KB - 1):
                    group_block(up + k, k, 0, (xh, xl), s=s)
                closing_block(s, up + KB - 1, 0)
                with pe.Fori(0, FG // 2) as i:
                    for g in range(2):
                        pe.wait_ge(up_scaled, at_turn(i, 4, first + 2 * g + 1))
                        for k in range(KB):
                            parts = range(4)
                            if g == k == 0:
                                group_block(up + KB, 0, 4, (xh, xl), i=i, step=2 * KB, quarters=(0,))
                                pe.wait_ge(hrinv, s + 1)
                                parts = (1, 2, 3)
                            group_block(up + KB * (1 + g) + k, k, 4 * ((1 + g) % 2), (xh, xl),
                                        i=i, step=2 * KB, quarters=parts)
                def hidden(c):
                    return [t[:, bass.ds(c, 1), :].rearrange("p o n -> p (o n)") for t in (mid_hi, mid_lo)]

                pe.wait_ge(up_scaled, first + 2 * FG - 1)
                pe.wait_ge(midl_done, first + 1)
                out_block(s, down, hidden(0), True, False, free={4: (up_scaled, first + 2 * FG + 1)})
                with pe.Fori(0, (FC - 2) // 4) as i:
                    for k in range(4):
                        pe.wait_ge(midl_done, at_turn(i, 4, first + 2 + k))
                        out_block(s, down + 1 + k, hidden(at_turn(i, 4, 1 + k)), False, False, i, 4)
                pe.wait_ge(midl_done, first + FC)
                out_block(s, down + FC - 1, hidden(FC - 1), False, True)
                out_stat(s)

            def fill(turn):
                for q in range(sum(FILL[:turn]), sum(FILL[:turn + 1])):
                    g, q = FILL_GROUPS[q // GROUP_Q], q % GROUP_Q
                    end = q // 4 == KB - 1
                    part = LAST_ORDER[q % 4] if end else q % 4
                    free = {}
                    if q < 2:
                        semaphore, count = {3: (in_lo, 10), 4: (in_tmp, 10), 5: (in_hi, 14)}[g]
                        free = {2 * q: (semaphore, count + 2 * q)}
                    (token_block if g == 4 else group_block)(
                        B_IN + KB * g + q // 4, q // 4, IN_BANK[g], (xh, xl), *([TC] if g == 4 else []),
                        quarters=(part,), free=free, pair=end)

            def attention(phase):
                units, u0, late, mem = UNITS[phase], FIRST_UNIT[phase], LATE[phase], phase != FOX
                y0 = Y_GLA if mem else 0
                depth = 3 if phase == MEM_B else 2
                s_free = ({}, {0: (mq_t, 1), 1: (mq_t, 2)}, {0: (expd, u0), 1: (expd, u0), 2: (pt_l, u0)})[phase]
                p_free = ({}, {0: (mq_t, 3)}, {0: (y_l, y0 + 3), 1: (mq_t, 5)})[phase]
                o_free = ({(hd, 0): (y_l, hd) for hd in range(1, FOX_H)},
                          {(0, 0): (mq_t, 4), (0, 1): (y_l, y0 + 1), (1, 0): (y_l, y0 + 2), (1, 1): (mq_t, 6)},
                          {(2, 0): (mq_t, 7), (2, 1): (mq_t, 8), (3, 0): (y_l, y0 + 4), (3, 1): (y_l, y0 + 5)})[phase]

                def scores(k):
                    hd, i = units[k]
                    w = key_width(mem, i)
                    if k in s_free:
                        pe.wait_ge(*s_free[k])
                    elif k >= depth:
                        pe.wait_ge(expd, u0 + k - depth + 1)
                    dst, tok = s_bank(phase, k)[:, 0:w], slice(i * P, (i + 1) * P)
                    if mem:
                        if i == 0:
                            pe.wait_ge(mq_l, 2 * hd + 2)
                        for e in range(2):
                            c = 2 * hd + e
                            last = three(dst, (qm_hi[:, c, tok], qm_lo[:, c, tok]),
                                         (km_hi[:, c, :], km_lo[:, c, :]), e == 0, e == 1)
                    else:
                        r, c = slice(FOX_D * (hd % 2), FOX_D * (hd % 2 + 1)), hd // 2
                        three(dst, (q_hi[r, c, tok], q_lo[r, c, tok]), (k_hi[r, c, 0:w], k_lo[r, c, 0:w]),
                              True, False)
                        pe.matmul(dst[:, w - P:w], ident_r[:, :], causal[:, :], start=False, stop=False,
                                  skip_group_check=True)
                        last = pe.matmul(dst, sel[r, hd, :], cum_hl[r, 0:w], start=False, stop=True)
                    last.then_inc(scored, 1)

                def turn(k):
                    u, nk = u0 + k, key_width(mem, units[k][1]) // P
                    pe.wait_ge(normed, u + 1)
                    if k in p_free:
                        pe.wait_ge(*p_free[k])
                    elif k >= late:
                        pe.wait_ge(pt_l, u - late + 1)
                    for j in range(nk):
                        last = pe.matmul(p_bank(phase, k)[:, j * P:(j + 1) * P], prob[:, u % 2, j * P:(j + 1) * P],
                                         norm_diag[:, u % 2, :], start=True, stop=True)
                    last.then_inc(pturned, 1)

                def output(done, e):
                    if not 0 <= done < len(units) or units[done][1] < TC - 1:
                        return
                    hd = units[done][0]
                    pe.wait_ge(pt_l, u0 + done + 1)
                    if (hd, e) in o_free:
                        pe.wait_ge(*o_free[hd, e])
                    for j in range(MC if mem else TC):
                        v, c = ((vm_hi, vm_lo), 2 * hd + e) if mem else ((v_hi, v_lo), hd // 2)
                        q0 = 0 if mem else j * P
                        last = three(o_bank(phase, hd, e)[:, q0:SEQ],
                                     (v[0][:, j, c * P:(c + 1) * P], v[1][:, j, c * P:(c + 1) * P]),
                                     (pt_hi[:, j, q0:SEQ], pt_lo[:, j, q0:SEQ]),
                                     j == 0, j == (MC if mem else TC) - 1, True)
                    last.then_inc(pv_done, 1)

                for k in range(len(units) + late + 1):
                    before, after = (MEM_FILL[k] if k < len(MEM_FILL) else (0, 0)) if phase == MEM_A else (0, 0)
                    filled = MEM_FILLED[k] if k < len(MEM_FILL) else 0
                    mem_fill(filled, before)
                    if k < len(units):
                        scores(k)
                    if phase == FOX:
                        fill(k)
                    if phase == MEM_B and k >= len(units):
                        first_output(k - len(units))
                    output(k - late - 1, 0)
                    mem_fill(filled + before, after)
                    if mem:
                        output(k - late - 1, 1)
                    if 0 <= k - late < len(units):
                        turn(k - late)

            def first_output(n):
                free = {2: (expd, N_UNITS - 2), 0: (expd, N_UNITS - 1), 1: (expd, N_UNITS)}
                pe.wait_ge(y_l, Y_GLA + 1)
                out_block(2, B_MO, (xh[:, 0, :], xl[:, 0, :]), True, False, free=free, ms=((2, 0, 1)[n],))

            def mem_fill(q0, n):
                free = {0: {0: (hrinv, 3), 1: (kv_l, 10)}, 1: {2: (kv_l, 11), 3: (kv_l, 12)}}
                for q in range(q0, q0 + n):
                    end = q // 4 == KB - 1
                    group_block(mem_block("q", 1, q // 4), q // 4, MQ_BANK[1], (xh, xl),
                                quarters=(LAST_ORDER[q % 4] if end else q % 4,), free=free.get(q, {}), pair=end)

            def gla():
                def head(hd):
                    e = hd % 2
                    return hd // 2, slice(GLA_K * e, GLA_K * (e + 1)), slice(GLA_V * hd, GLA_V * (hd + 1))

                def scores(m):
                    if m:
                        pe.wait_ge(at_masked, 2 * m)
                    else:
                        pe.wait_ge(ke_saved, 2)
                    tok = slice(m * P, (m + 1) * P)
                    for hd in range(GLA_H):
                        c, r, cols = head(hd)
                        last = pe.matmul(bank[hd % 2][:, c * P:(c + 1) * P], gk[r, c, tok], gq[r, c, tok],
                                         start=True, stop=True)
                    last.then_inc(at_done, 1)

                def chunk_state(n):
                    if n >= 2:
                        pe.wait_ge(st_ready, 2 * n - 3)
                    m, r = n // 2, slice(CHUNK * (n % 2), CHUNK * (n % 2 + 1))
                    for c in range(2):
                        cols = slice(2 * GLA_V * c, 2 * GLA_V * (c + 1))
                        last = pe.matmul(bank[2 + n % 2][:, cols], ke_tok[r, m, c, :], gv[r, m, cols],
                                         start=True, stop=True)
                    last.then_inc(sc_done, 1)

                def outputs(m):
                    pe.wait_ge(at_masked, 2 * m + 2)
                    pe.wait_ge(st_ready, 4 * m + 1)
                    if m == 0:
                        pe.wait_ge(in_tmp, 16)
                    for hd in range(GLA_H):
                        c, r, cols = head(hd)
                        last = pe.matmul(bank[4 + hd][:, m * P:(m + 1) * P], gv[:, m, cols],
                                         at_sb[:, m % 2, cols], start=True, stop=False, skip_group_check=True)
                        for n in (2 * m, 2 * m + 1):
                            if n:
                                tok = slice(n * CHUNK, (n + 1) * CHUNK)
                                last = pe.matmul(bank[4 + hd][:, tok], state[r, n - 1, cols], gq[r, c, tok],
                                                 start=False, stop=n % 2 == 1, skip_group_check=True)
                    last.then_inc(o_done, 1)

                pe.wait_ge(gdec, 3)
                pe.wait_ge(expd, N_FOX)
                for t in range(2):
                    for j in range(4):
                        m, c = 2 * t + j // 2, j % 2
                        last = pe.transpose(bank[t][:, j * P:(j + 1) * P], gke[:, c, m * P:(m + 1) * P],
                                            ident[:, :])
                    last.then_inc(ke_turned, 1)
                pe.wait_ge(y_l, Y_FOX)
                warm_up(bank[2], 1)
                scores(0)
                chunk_state(0)
                for m in range(TC):
                    if m + 1 < TC:
                        scores(m + 1)
                        chunk_state(2 * m + 1)
                        chunk_state(2 * m + 2)
                    outputs(m)

                def mem_turn(half):
                    if half == 0:
                        pe.wait_ge(st_ready, 2 * (NCH - 1) - 1)
                        pe.wait_ge(mem_normed, MC)
                    else:
                        pe.wait_ge(mem_l, 4)
                    for j in range(8):
                        c, t = 4 * half + j // 2, j % 2
                        col = c % 2 * NMEM + t * P
                        last = pe.transpose(bank[2 + c // 2 % 2][:, col:col + P], mem_n[:, t, c * P:(c + 1) * P],
                                            ident[:, :])
                        if j % 4 == 3:
                            last.then_inc(mem_turned, 1)

                def fox_out(q):
                    free = {0: {0: (gcopy, 1), 1: (gcopy, 2)}, 1: {2: (gcopy, 3), 3: (gcopy, 4)}}
                    group_block(B_OUT + q // 4, q // 4, 4, (fox_hi, fox_lo), quarters=(q % 4,), free=free.get(q, {}),
                                last_chunk=DC)

                def sums():
                    for hd in range(GLA_H):
                        pe.wait_ge(gsq, hd + 1)
                        rows = slice(SUM_ROWS * hd, SUM_ROWS * (hd + 1))
                        last = pe.matmul(bank[0][rows, :], ones[:, 0:SUM_ROWS], tmp[:, hd, :],
                                         start=True, stop=True)
                    return last

                def spread_head(hd):
                    if hd >= 2:
                        pe.wait_ge(gfactor, hd - 1)
                    row = SUM_ROWS * hd
                    pe.matmul(bank[1 - hd % 2][:, :], ident[:, row:row + 1].to_broadcast([P, P]), tmp[:, 3, :],
                              start=True, stop=True).then_inc(gspread, 1)

                pe.wait_ge(y_l, Y_FOX)
                fox_out(0)
                fox_out(1)
                fox_out(2)
                sums().then_inc(gstat, 1)
                mem_turn(0)
                fox_out(3)
                fox_out(4)
                pe.wait_ge(ginv, 1)
                spread_head(0)
                spread_head(1)
                fox_out(5)
                mem_turn(1)
                fox_out(6)
                spread_head(2)
                spread_head(3)
                fox_out(7)

            def mixer():
                def small_columns():
                    pe.wait_ge(small_scaled, DC)
                    for c in range(DC):
                        last = pe.matmul(bank[SMALL_BANK][0:48, :], w_small_g[:, c, :], h[:, c, :],
                                         start=c == 0, stop=c == DC - 1)
                    last.then_inc(small_done, 1)

                first_block(1, B_IN, IN_BANK[0])
                for k in range(1, KB - 1):
                    group_block(B_IN + k, k, IN_BANK[0], (xh, xl), s=1)
                closing_block(1, B_IN + KB - 1, IN_BANK[0], small_columns)
                for k in range(KB):
                    end = k == KB - 1
                    free = {2: (hrinv, 2), 3: (z_ready, 1)} if k == 0 else {}
                    group_block(B_IN + KB + k, k, IN_BANK[1], (xh, xl), quarters=LAST_ORDER, free=free, pair=end)
                    if k == 1:
                        pe.wait_ge(in_tmp, 4)
                        for j in range(2):
                            pe.matmul(bank[6 + j][:, :], w_a2[32:48, j * P:(j + 1) * P], zg[32:48, :],
                                      start=True, stop=True).then_inc(ga_done, 1)
                for k in range(KB):
                    free = {2: (z_ready, 3)} if k == 0 else {}
                    token_block(B_IN + 2 * KB + k, k, IN_BANK[2], (xh, xl), TC, quarters=LAST_ORDER, free=free,
                                pair=k == KB - 1)
                pe.wait_ge(in_lo, 8)
                pe.wait_ge(cum_lo, 2)
                pe.wait_ge(sel_ready, 3)
                attention(FOX)
                gla()
                for k in range(2):
                    free = {0: (gfactor, GLA_H), 2: (mem_l, DC)} if k == 0 else {}
                    group_block(B_OUT + 2 + k, k, 0, (fox_hi, fox_lo), free=free, last_chunk=DC)
                for c in range(4, DC):
                    pe.wait_ge(y_l, Y_FOX + c - 3)
                    out_block(1, B_OUT + c, (xh[:, c, :], xl[:, c, :]), False, c == DC - 1)
                out_stat(1)

            def memory():
                for g in range(2):
                    for k in range(KB):
                        free = {m: (f_scaled, DC + 4 * g + m + 1) for m in range(4)} if k == 0 else {}
                        if g == k == 0:
                            free[0] = (frinv, 2)
                        group_block(mem_block("k", g, k), k, KV_BANK["k", g], (mem_hi, mem_lo), NMEM, free=free)
                for kind, g, k in MEM_BLOCKS[2 * KB:-KB]:
                    if kind == "v":
                        free = {m: (kv_l, 2 * g + m + 1) for m in range(MC)} if k == 0 else {}
                        token_block(mem_block("v", g, k), k, KV_BANK["v", g], (mem_hi, mem_lo), MC, free=free)
                    elif k == KB - 1:
                        pe.wait_ge(kv_l, 9)
                        closing_block(2, mem_block("q", 0, k), MQ_BANK[0])
                    else:
                        free = {m: (kv_l, 4 + m + 1) for m in range(4)} if k == 0 else {}
                        group_block(mem_block("q", 0, k), k, MQ_BANK[0], (xh, xl), s=2, free=free)
                attention(MEM_A)
                attention(MEM_B)
                free = {3: (pt_l, N_UNITS), 5: (y_l, Y_GLA + 7), 6: (y_l, Y_GLA + DC)}
                for c in range(DC):
                    pe.wait_ge(y_l, Y_GLA + c + 1)
                    out_block(2, B_MO + c, (xh[:, c, :], xl[:, c, :]), c == 0, c == DC - 1,
                              free={} if c else free, ms=range(DC) if c else range(3, DC))
                out_stat(2)

            pe.wait_ge(consts, 5)
            warm_up(bank[0], WARM_UP)
            pe.wait_ge(gains_landed, 16 * GAIN_LOADS)
            pe.transpose(bank[7][:, 0:G_ROWS], gain_rows[:, :], ident[0:G_ROWS, 0:G_ROWS]).then_inc(gains_turned, 1)
            pe.wait_ge(gains_ready, 1)
            for t in range(TC):
                pe.wait_ge(x_landed[t], 16)
                for c in range(DC):
                    last = pe.transpose(bank[c][:, t * P:(t + 1) * P], x_tok[:, t, c * P:(c + 1) * P], ident[:, :])
                    if t == TC - 1:
                        last.then_inc(turned, 1)
            swiglu(0, B_UP1, B_DOWN1)
            mixer()
            memory()
            swiglu(3, B_UP2, B_DOWN2)
            pe.wait_ge(frinv, SUBLAYERS)
            turn_h(0)
            for c, ready in enumerate(((normed_v, 1), (normed_v, 2), (normed_p, 1), (normed_p, 2))):
                pe.wait_ge(*ready)
                turn_f(c)
            for c, ready in ((4, (summed_v, 1)), (5, (summed_v, 2)), (6, (summed_v, 3)), (7, (summed_p, 1))):
                pe.wait_ge(*ready)
                for t in range(TC):
                    last = pe.transpose(bank[t][:, (c - 4) * P:(c - 3) * P], h[:, c, t * P:(t + 1) * P], ident[:, :])
                    if c == DC - 1:
                        last.then_inc(oturned, 1)


_INS = ("x", "mem", "ffn1_g_pre", "ffn1_w_gu", "ffn1_w_down", "ffn1_g_post", "mix_g_pre", "mix_w_in",
        "mix_w_a2", "mix_b_a", "mix_b_f", "mix_g_gla", "mix_w_out", "mix_g_post", "mem_g_pre",
        "mem_g_kv", "mem_w_q", "mem_w_kv", "mem_w_o", "mem_g_post", "ffn2_g_pre", "ffn2_w_gu",
        "ffn2_w_down", "ffn2_g_post")


def kernel(**inputs):
    import numpy as _np
    import concourse.bacc as _bacc
    from concourse import mybir as _mybir
    from concourse.bass_utils import run_bass_kernel_spmd as _run

    nc = _bacc.Bacc("TRN2", target_bir_lowering=False, num_devices=1)
    arrays, args = {}, {}
    for name in _INS:
        array = _np.ascontiguousarray(inputs[name])
        arrays[f"in_{name}"] = array
        args[name] = nc.dram_tensor(f"in_{name}", array.shape, _mybir.dt.from_np(array.dtype),
                                    kind="ExternalInput").ap()
    out = nc.dram_tensor("out", (1, SEQ, D), _mybir.dt.float32, kind="ExternalOutput").ap()
    build(nc, args, out)
    r = _run(nc, [arrays], core_ids=[0])
    return r.results[0]["out"]
```
